# Optimizing a Trainium2 kernel written in Bass

```python
import math
import jax, jax.numpy as jnp
from jax import lax
import numpy as np

D_MODEL = 1024
BATCH = 1
SEQ = 256
DEPTH = 2
DEC_BATCH = 8
DEC_SEQ = 1
PAST_LEN = 2048
PAGE_SIZE = 128

N_AB_LAYERS = (DEPTH + 1) // 2
N_C_LAYERS = DEPTH // 2
CHUNK = 64
GLA_HEADS = 4
GLA_DK = D_MODEL // 2 // GLA_HEADS
GLA_DV = D_MODEL // GLA_HEADS
GLA_KEY = GLA_HEADS * GLA_DK
GLA_VAL = GLA_HEADS * GLA_DV
GLA_RANK = 16
GLA_NORMALIZER = 16.0
SSD_INNER = D_MODEL
SSD_HEADDIM = 64
SSD_HEADS = SSD_INNER // SSD_HEADDIM
SSD_STATE = 128
SSD_GROUPS = 2
SSD_CONV = 4
SSD_CONV_DIM = SSD_INNER + 2 * SSD_GROUPS * SSD_STATE
HG_EXPAND = 128
HG_HEADS = D_MODEL // HG_EXPAND
HG_F = HG_HEADS * HG_EXPAND
HG_I = D_MODEL
HG_DI = HG_I // HG_HEADS
N_EXPERTS = 16
N_GROUPS = 4
EXPERTS_PER_GROUP = N_EXPERTS // N_GROUPS
TOP_K = 2
D_FF_EXPERT = 512
ALPHA = (2 * DEPTH) ** 0.25
BETA = (8 * DEPTH) ** -0.25
EPS = 1e-5
AB_SPLITS = (GLA_KEY, GLA_KEY, GLA_VAL, GLA_VAL, GLA_RANK, SSD_INNER, SSD_CONV_DIM, SSD_HEADS)
AB_IN = sum(AB_SPLITS)
C_SPLITS = (HG_F, HG_F, HG_I, HG_I)
C_IN = sum(C_SPLITS)

kernel_name = 'hybrid_gla_ssd_hgrn2_moe_step'

F32 = jnp.float32

def split_cols(a, sizes):
    offs = np.cumsum(sizes)[:-1].tolist()
    return jnp.split(a, offs, axis=-1)

def heads(a, h):
    return a.reshape(a.shape[:-1] + (h, -1))

def layer_norm(x, w, b):
    xf = x.astype(F32)
    mu = xf.mean(-1, keepdims=True)
    var = jnp.square(xf - mu).mean(-1, keepdims=True)
    return ((xf - mu) * lax.rsqrt(var + EPS) * w + b).astype(x.dtype)

def rms_norm(x, w):
    xf = x.astype(F32)
    return (xf * lax.rsqrt(jnp.mean(xf * xf, -1, keepdims=True) + EPS) * w).astype(x.dtype)

def chunked_gated_linear(q, k, v, g, s0, scalar_decay, out_dtype):
    bsz, L = q.shape[0], q.shape[1]
    C = min(CHUNK, L)
    n = -(-L // C)
    pad = n * C - L

    def prep(a):
        a = jnp.pad(a.astype(F32), [(0, 0), (0, pad)] + [(0, 0)] * (a.ndim - 2))
        a = a.reshape((bsz, n, C) + a.shape[2:])
        return jnp.moveaxis(a, 1, 0)

    qc, kc, vc, gc = prep(q), prep(k), prep(v), prep(g)
    causal = jnp.tril(jnp.ones((C, C), bool))

    def step(S, inp):
        qb, kb, vb, gb = inp
        G = jnp.cumsum(gb, axis=1)
        G_last = G[:, -1]
        if scalar_decay:
            diff = G[:, :, None, :] - G[:, None, :, :]
            decay = jnp.exp(jnp.where(causal[None, :, :, None], diff, -jnp.inf))
            scores = jnp.einsum('bthk,bshk->btsh', qb, kb) * decay
            q_dec = qb * jnp.exp(G)[..., None]
            k_dec = kb * jnp.exp(G_last[:, None] - G)[..., None]
            s_dec = jnp.exp(G_last)[..., None, None]
        else:
            diff = G[:, :, None] - G[:, None, :]
            decay = jnp.exp(jnp.where(causal[None, :, :, None, None], diff, -jnp.inf))
            scores = jnp.einsum('bthk,bshk,btshk->btsh', qb, kb, decay)
            q_dec = qb * jnp.exp(G)
            k_dec = kb * jnp.exp(G_last[:, None] - G)
            s_dec = jnp.exp(G_last)[..., None]
        o = jnp.einsum('btsh,bshv->bthv', scores, vb) + jnp.einsum('bthk,bhkv->bthv', q_dec, S)
        S = S * s_dec + jnp.einsum('bshk,bshv->bhkv', k_dec, vb)
        return S, o

    S, o = lax.scan(step, s0.astype(F32), (qc, kc, vc, gc))
    o = jnp.moveaxis(o, 0, 1).reshape((bsz, n * C) + o.shape[3:])[:, :L]
    return o.astype(out_dtype), S.astype(s0.dtype)

def causal_conv(xbc, buf, w, b):
    L = xbc.shape[1]
    xp = jnp.concatenate([buf.astype(xbc.dtype), xbc], axis=1)
    out = b
    for j in range(SSD_CONV):
        out = out + xp[:, j:j + L] * w[j]
    return jax.nn.silu(out), xp[:, L:]

def ab_mixer(x, s_gla, s_ssd, s_conv, w_in, w_gk2, b_gk2, gla_norm_w, conv_w, conv_b,
             dt_bias, a_log, d_skip, ssd_norm_w, w_out):
    bsz, L, _ = x.shape
    q, k, v, g_out, lr, z, xbc, dt = split_cols(x @ w_in, AB_SPLITS)
    gk = jax.nn.log_sigmoid((lr @ w_gk2 + b_gk2).astype(F32)) / GLA_NORMALIZER
    o_gla, s_gla = chunked_gated_linear(heads(q, GLA_HEADS) * GLA_DK ** -0.5, heads(k, GLA_HEADS),
                                        heads(v, GLA_HEADS), heads(gk, GLA_HEADS), s_gla, False, x.dtype)
    o_gla = (rms_norm(o_gla, gla_norm_w) * jax.nn.silu(heads(g_out, GLA_HEADS))).reshape(bsz, L, GLA_VAL)
    xbc, s_conv = causal_conv(xbc, s_conv, conv_w, conv_b)
    xs, Bm, Cm = split_cols(xbc, (SSD_INNER, SSD_GROUPS * SSD_STATE, SSD_GROUPS * SSD_STATE))
    xs = heads(xs, SSD_HEADS)
    rep = SSD_HEADS // SSD_GROUPS
    Bm = jnp.repeat(heads(Bm, SSD_GROUPS), rep, axis=2)
    Cm = jnp.repeat(heads(Cm, SSD_GROUPS), rep, axis=2)
    dt = jax.nn.softplus(dt.astype(F32) + dt_bias.astype(F32))
    A = -jnp.exp(a_log.astype(F32))
    y, s_ssd = chunked_gated_linear(Cm, Bm * dt[..., None], xs, dt * A, s_ssd, True, x.dtype)
    y = y + d_skip[:, None].astype(y.dtype) * xs
    yz = y.reshape(bsz, L, SSD_INNER) * jax.nn.silu(z)
    yz = rms_norm(heads(yz, SSD_GROUPS), ssd_norm_w.reshape(SSD_GROUPS, -1)).reshape(bsz, L, SSD_INNER)
    out = jnp.concatenate([o_gla, yz], axis=-1) @ w_out
    return out, s_gla, s_ssd, s_conv

def hgrn_mixer(x, s_hg, w_in, lb, norm_w, w_out):
    bsz, L, _ = x.shape
    q, f, i, g = split_cols(x @ w_in, C_SPLITS)
    q = jax.nn.silu(q)
    lb = lb.astype(F32)
    forget = lb + (1.0 - lb) * jax.nn.sigmoid(f.astype(F32))
    o, s_hg = chunked_gated_linear(heads(q, HG_HEADS), heads(1.0 - forget, HG_HEADS), heads(i, HG_HEADS),
                                   heads(jnp.log(forget), HG_HEADS), s_hg, False, x.dtype)
    o = (rms_norm(o, norm_w) * jax.nn.silu(heads(g, HG_HEADS))).reshape(bsz, L, HG_I)
    return o @ w_out, s_hg

def moe(h, router_w, router_bias, w_gate, w_up, w_down):
    bsz, L, D = h.shape
    t = h.reshape(-1, D)
    scores = jax.nn.sigmoid((t @ router_w).astype(F32))
    sel = scores + router_bias.astype(F32)
    grp = lax.top_k(sel.reshape(-1, N_GROUPS, EXPERTS_PER_GROUP), TOP_K)[0].sum(-1)
    best = jnp.argmax(grp, axis=-1)
    in_group = (jnp.arange(N_EXPERTS) // EXPERTS_PER_GROUP)[None, :] == best[:, None]
    _, idx = lax.top_k(jnp.where(in_group, sel, -jnp.inf), TOP_K)
    w = jnp.take_along_axis(scores, idx, axis=-1)
    w = w / w.sum(-1, keepdims=True)
    gates = (jax.nn.one_hot(idx, N_EXPERTS, dtype=F32) * w[..., None]).sum(1)
    y = jnp.zeros(t.shape, F32)
    for e in range(N_EXPERTS):
        he = jax.nn.silu(t @ w_gate[e]) * (t @ w_up[e])
        y = y + gates[:, e:e + 1] * (he @ w_down[e])
    return y.astype(h.dtype).reshape(bsz, L, D)

def trunk(x, st_gla, st_ssd, st_conv, st_hg, p, lbs):
    new_gla, new_ssd, new_conv, new_hg = [], [], [], []
    for layer in range(DEPTH):
        j = layer // 2
        if layer % 2 == 0:
            mix, sg, ss, sc = ab_mixer(x, st_gla[j], st_ssd[j], st_conv[j], p['w_in_ab'][j], p['w_gk2'][j],
                                       p['b_gk2'][j], p['gla_norm_w'][j], p['conv_w'][j], p['conv_b'][j],
                                       p['dt_bias'][j], p['a_log'][j], p['d_skip'][j], p['ssd_norm_w'][j],
                                       p['w_out_ab'][j])
            new_gla.append(sg)
            new_ssd.append(ss)
            new_conv.append(sc)
        else:
            mix, sh = hgrn_mixer(x, st_hg[j], p['w_in_c'][j], lbs[layer], p['hg_norm_w'][j], p['w_out_c'][j])
            new_hg.append(sh)
        x = layer_norm(ALPHA * x + mix, p['ln1_w'][layer], p['ln1_b'][layer])
        ff = moe(x, p['router_w'], p['router_bias'], p['w_gate'][layer], p['w_up'][layer], p['w_down'][layer])
        x = layer_norm(ALPHA * x + ff, p['ln2_w'][layer], p['ln2_b'][layer])
    return x, jnp.stack(new_gla), jnp.stack(new_ssd), jnp.stack(new_conv), jnp.stack(new_hg)

def setup_inputs(seed: int = 0) -> dict:
    key = jax.random.key(seed)
    ks = iter(jax.random.split(key, 40))

    def nrm(shape, scale):
        return jax.random.normal(next(ks), shape, F32) * scale

    ab_off = np.cumsum((0,) + AB_SPLITS)
    ab_scale = np.ones(AB_IN, np.float32)
    ab_scale[ab_off[2]:ab_off[3]] = BETA
    ab_scale[ab_off[6]:ab_off[6] + SSD_INNER] = BETA
    c_off = np.cumsum((0,) + C_SPLITS)
    c_scale = np.ones(C_IN, np.float32)
    c_scale[c_off[2]:c_off[3]] = BETA
    dt0 = jnp.exp(jax.random.uniform(next(ks), (N_AB_LAYERS, SSD_HEADS), F32, math.log(1e-3), math.log(1e-1)))
    dt_bias = dt0 + jnp.log(-jnp.expm1(-dt0))
    a_log = jnp.log(jax.random.uniform(next(ks), (N_AB_LAYERS, SSD_HEADS), F32, 1.0, 16.0))
    return {
        'x_prompt': nrm((BATCH, SEQ, D_MODEL), 1.0),
        'x_sample': nrm((DEC_BATCH, DEC_SEQ, D_MODEL), 1.0),
        'state_gla': nrm((N_AB_LAYERS, DEC_BATCH, GLA_HEADS, GLA_DK, GLA_DV), 1.0),
        'state_ssd': nrm((N_AB_LAYERS, DEC_BATCH, SSD_HEADS, SSD_STATE, SSD_HEADDIM), 0.5),
        'state_conv': nrm((N_AB_LAYERS, DEC_BATCH, SSD_CONV - 1, SSD_CONV_DIM), 1.0),
        'state_hgrn': nrm((N_C_LAYERS, DEC_BATCH, HG_HEADS, HG_EXPAND, HG_DI), 1.0),
        'w_in_ab': nrm((N_AB_LAYERS, D_MODEL, AB_IN), D_MODEL ** -0.5) * jnp.asarray(ab_scale),
        'w_gk2': nrm((N_AB_LAYERS, GLA_RANK, GLA_KEY), GLA_RANK ** -0.5),
        'b_gk2': nrm((N_AB_LAYERS, GLA_KEY), 0.1),
        'gla_norm_w': 1.0 + nrm((N_AB_LAYERS, GLA_DV), 0.02),
        'conv_w': nrm((N_AB_LAYERS, SSD_CONV, SSD_CONV_DIM), SSD_CONV ** -0.5),
        'conv_b': nrm((N_AB_LAYERS, SSD_CONV_DIM), 0.02),
        'dt_bias': dt_bias,
        'a_log': a_log,
        'd_skip': 1.0 + nrm((N_AB_LAYERS, SSD_HEADS), 0.02),
        'ssd_norm_w': 1.0 + nrm((N_AB_LAYERS, SSD_INNER), 0.02),
        'w_out_ab': nrm((N_AB_LAYERS, GLA_VAL + SSD_INNER, D_MODEL), (GLA_VAL + SSD_INNER) ** -0.5 * BETA),
        'w_in_c': nrm((N_C_LAYERS, D_MODEL, C_IN), D_MODEL ** -0.5) * jnp.asarray(c_scale),
        'lower_bounds': nrm((DEPTH, HG_F), 0.1),
        'hg_norm_w': 1.0 + nrm((N_C_LAYERS, HG_DI), 0.02),
        'w_out_c': nrm((N_C_LAYERS, HG_I, D_MODEL), HG_I ** -0.5 * BETA),
        'router_w': nrm((D_MODEL, N_EXPERTS), D_MODEL ** -0.5),
        'router_bias': nrm((N_EXPERTS,), 0.01),
        'w_gate': nrm((DEPTH, N_EXPERTS, D_MODEL, D_FF_EXPERT), D_MODEL ** -0.5),
        'w_up': nrm((DEPTH, N_EXPERTS, D_MODEL, D_FF_EXPERT), D_MODEL ** -0.5),
        'w_down': nrm((DEPTH, N_EXPERTS, D_FF_EXPERT, D_MODEL), D_FF_EXPERT ** -0.5 * BETA),
        'ln1_w': 1.0 + nrm((DEPTH, D_MODEL), 0.02),
        'ln1_b': nrm((DEPTH, D_MODEL), 0.02),
        'ln2_w': 1.0 + nrm((DEPTH, D_MODEL), 0.02),
        'ln2_b': nrm((DEPTH, D_MODEL), 0.02),
    }

def reference(x_prompt, x_sample, state_gla, state_ssd, state_conv, state_hgrn,
              w_in_ab, w_gk2, b_gk2, gla_norm_w, conv_w, conv_b, dt_bias, a_log, d_skip, ssd_norm_w, w_out_ab,
              w_in_c, lower_bounds, hg_norm_w, w_out_c,
              router_w, router_bias, w_gate, w_up, w_down,
              ln1_w, ln1_b, ln2_w, ln2_b):
    p = dict(w_in_ab=w_in_ab, w_gk2=w_gk2, b_gk2=b_gk2, gla_norm_w=gla_norm_w, conv_w=conv_w, conv_b=conv_b,
             dt_bias=dt_bias, a_log=a_log, d_skip=d_skip, ssd_norm_w=ssd_norm_w, w_out_ab=w_out_ab,
             w_in_c=w_in_c, hg_norm_w=hg_norm_w, w_out_c=w_out_c, router_w=router_w, router_bias=router_bias,
             w_gate=w_gate, w_up=w_up, w_down=w_down, ln1_w=ln1_w, ln1_b=ln1_b, ln2_w=ln2_w, ln2_b=ln2_b)
    lbs = jax.nn.softmax(lower_bounds.astype(F32), axis=0)
    lbs = jnp.cumsum(lbs, axis=0) - lbs[0]
    bp = x_prompt.shape[0]

    def zeros_like_state(s):
        return jnp.zeros((s.shape[0], bp) + s.shape[2:], x_prompt.dtype)

    y_prompt, gla_p, ssd_p, conv_p, hg_p = trunk(x_prompt, zeros_like_state(state_gla), zeros_like_state(state_ssd),
                                                 zeros_like_state(state_conv), zeros_like_state(state_hgrn), p, lbs)
    y_sample, gla_s, ssd_s, conv_s, hg_s = trunk(x_sample, state_gla, state_ssd, state_conv, state_hgrn, p, lbs)
    return (y_prompt, y_sample, gla_p, ssd_p, conv_p, hg_p, gla_s, ssd_s, conv_s, hg_s)


_drawn_inputs = setup_inputs


def setup_inputs(seed=0):
    import zlib

    import numpy as np

    out = dict(_drawn_inputs(seed))
    spreads = {}
    factors = {'gla_norm_w': 3.294, 'ssd_norm_w': 3.456, 'hg_norm_w': 3.36}
    for name, (base, spread) in spreads.items():
        noise = np.random.default_rng([zlib.crc32(name.encode()), seed]).standard_normal(out[name].shape)
        drawn = base * np.exp(spread * noise) if base else spread * noise
        out[name] = __import__('jax').numpy.asarray(drawn.astype(out[name].dtype))
    for name, factor in factors.items():
        out[name] = (out[name] * factor).astype(out[name].dtype)
    return out
```

```python
from contextlib import ExitStack

import concourse.bass as bass
from concourse import mybir

F32 = mybir.dt.float32
ALU = mybir.AluOpType
ACT = mybir.ActivationFunctionType
AX = mybir.AxisListType.X

P = 128
D = 1024
DC = D // P
NP = 256
NB = 8
T = NP + NB
DEPTH = 2
ALPHA = (2 * DEPTH) ** 0.25
EPS = 1e-5
C = 64
NC = NP // C
CS = 128
NCS = NP // CS
E_N, E_G, E_K, FF = 16, 4, 2, 512
SLOTS = 6
SLOT_W = 4096
HEAD_SCALE = 128 ** -0.5
SSD_HEADS = 16
NORM_GLA, NORM_SSD, NORM_HG = 256, 512, 128
BIG = 1.0e30

V_BGK, V_GLAN, V_SSDN, V_LN1W, V_LN1B, V_LN2W, V_LN2B, V_HGN, V_LB = 0, 4, 6, 14, 30, 46, 62, 78, 79
V_N = 95

Q0, K0, VV0, G0, Z0, XS0, B0, C0 = 0, 4, 8, 16, 24, 32, 40, 42
AB_CHUNKS = 44


def trunk_program(nc, ins, outs):
    (x_prompt, x_sample, state_gla, state_ssd, state_conv, state_hgrn, w_in_ab, w_gk2, b_gk2, gla_norm_w, conv_w,
     conv_b, dt_bias, a_log, d_skip, ssd_norm_w, w_out_ab, w_in_c, lower_bounds, hg_norm_w, w_out_c, router_w,
     router_bias, w_gate, w_up, w_down, ln1_w, ln1_b, ln2_w, ln2_b) = ins
    (y_prompt, y_sample, gla_p, ssd_p, conv_p, hg_p, gla_s, ssd_s, conv_s, hg_s) = outs

    with ExitStack() as ctx:
        def sb(name, shape, dt=F32):
            return ctx.enter_context(nc.sbuf_tensor(name, shape, dt))

        sems = {}

        def sem(name):
            if name not in sems:
                sems[name] = ctx.enter_context(nc.semaphore(name))
            return sems[name]

        bank = [ctx.enter_context(nc.psum_tensor(f"bank{i}", [P, 512], F32)) for i in range(8)]

        ring = sb("ring", [P, SLOTS, SLOT_W])
        xT = sb("xT", [P, DC, T])
        A = sb("A", [P, AB_CHUNKS, T])
        W = sb("W", [P, 10880])
        ident = sb("ident", [P, P])
        ones = sb("ones", [P, P])
        causal = sb("causal", [P, P])
        restart = sb("restart", [P, NP])
        cols = sb("cols", [P, V_N])
        router = sb("router", [P, DC, E_N])
        rbias = sb("rbias", [P, E_N])
        small = sb("small", [16, 4])
        dskip = sb("dskip", [P, 8])
        lbc = sb("lbc", [P, 3, 8])
        score = sb("score", [P, 3, E_N])
        gate = sb("gate", [P, 3, E_N])
        gateT = sb("gateT", [E_N, T])
        rt = sb("rt", [P, 8, 3, E_N])
        idx16 = sb("idx16", [P, E_N])

        def area(base, *shape):
            n = 1
            for s in shape:
                n *= s
            assert base + n <= W.shape[1]
            v = W[:, base:base + n]
            if len(shape) == 2:
                v = v.rearrange("p (a b) -> p a b", a=shape[0])
            if len(shape) == 3:
                v = v.rearrange("p (a b c) -> p a b c", a=shape[0], b=shape[1])
            return v

        Aflat = A[:, :, :].rearrange("p a t -> p (a t)")

        fills = []
        ab_cols = [g * 512 for g in range(6)] + [3088 + g * 512 for g in range(5)]
        for c0 in ab_cols:
            fills.append((w_in_ab[0, :, c0:c0 + 512].rearrange("(c p) n -> p c n", p=P), 8))
        for g in range(4):
            fills.append((w_out_ab[0, :, g * 256:g * 256 + 256].rearrange("(c p) n -> p c n", p=P), 16))
        AB_IN0, AB_OUT0, MOE0 = 0, 11, 15
        MOE_SLOTS = 3 * E_N
        C_IN0 = MOE0 + MOE_SLOTS
        C_OUT0 = C_IN0 + 8
        MOE1 = C_OUT0 + 2
        TOTAL = MOE1 + MOE_SLOTS

        def slot(n, k):
            return ring[:, n % SLOTS, :].rearrange("p (c n) -> p c n", c=k)

        def expert_views(layer, e):
            return [
                (w_gate[layer, e].rearrange("o (c p) n -> p (o c) n", p=P), 8),
                (w_up[layer, e].rearrange("o (c p) n -> p (o c) n", p=P), 8),
                (w_down[layer, e].rearrange("o (c p) n -> p (o c) n", p=P), 4),
            ]

        block = ctx.enter_context(nc.Block())

        class Steps:

            def __init__(self, eng, name):
                self.eng, self.sem, self.n = eng, sem(name), 0

            def add(self, ins):
                ins.then_inc(self.sem, 1)
                self.n += 1

            def settle(self):
                self.eng.wait_ge(self.sem, self.n)

            def run(self, ins):
                self.add(ins)
                self.settle()

        def stage_end(eng, k):
            eng.sem_inc(sem("stage_ended"), 1)
            eng.wait_ge(sem("stage_ended"), 4 * k)

        @block.sync
        def _(sp):
            def last_reader(n):
                if n < AB_OUT0:
                    return "in0_ready", 4 * (n + 1)
                if n < MOE0:
                    return "out0_ready", 2 * (n - AB_OUT0 + 1)
                if n < C_IN0:
                    e, i = divmod(n - MOE0, 3)
                    return ("moe_gu", 4 * (e + 1)) if i < 2 else ("moe_down", 8 * (e + 1))
                if n < C_OUT0:
                    return "in1_ready", 4 * (n - C_IN0 + 1)
                return "out1_ready", 4 * (n - C_OUT0 + 1)

            def fill(n, src, k):
                if n >= SLOTS:
                    name, value = last_reader(n - SLOTS)
                    sp.wait_ge(sem(name), value)
                sp.dma_start(slot(n, k), src).then_inc(sem(f"slot_filled{n % SLOTS}"), 16)

            def fill_experts(n0, layer):
                for e in range(2):
                    for i, (src, k) in enumerate(expert_views(layer, bass.ds(e, 1))):
                        fill(n0 + 3 * e + i, src, k)
                with sp.Fori(1, E_N // 2) as pair:
                    e = 2 * pair
                    for j in range(2):
                        for i, (src, k) in enumerate(expert_views(layer, bass.ds(e + j, 1))):
                            n = n0 + 3 * j + i
                            if i < 2:
                                sp.wait_ge(sem("moe_gu"), 4 * (E_N * layer + e) + 4 * (j - 1))
                            else:
                                sp.wait_ge(sem("moe_down"), 8 * (E_N * layer + e) + 8 * (j - 1))
                            sp.dma_start(slot(n, k), src).then_inc(sem(f"slot_filled{n % SLOTS}"), 16)

            for n, (src, k) in enumerate(fills):
                fill(n, src, k)
            fill_experts(MOE0, 0)
            for g in range(8):
                fill(C_IN0 + g, w_in_c[0, :, g * 512:g * 512 + 512].rearrange("(c p) n -> p c n", p=P), 8)
            for g in range(2):
                fill(C_OUT0 + g, w_out_c[0, :, g * 512:g * 512 + 512].rearrange("(c p) n -> p c n", p=P), 8)
            fill_experts(MOE1, 1)

        xrows = area(0, 3, D)
        vrows = area(3072, P)
        crows = area(3200, 12 * P)
        wsmall = area(4736, 8, 32)
        convout = area(4992, 12 * P)
        cacc = area(6528, 2, T)
        convc = area(7056, 12, 29)
        gka = area(7564, 4, T)
        gkz = area(8620, 4, T)
        wgk = area(9676, 512)[0:16, :]
        lrT = area(10188, T)[0:16, :]
        gkg = sb("gkg", [P, 4, T])
        decx = sb("decx", [P, 8, NB])
        mh = W[:, 0:2 * 4 * T].rearrange("p (j f t) -> p j f t", j=2, f=4)
        mg = area(2112, 2, T)
        mgb = area(2640, T)
        msel = area(2904, 2, P)
        lnsq = A[:, 0:8, :]
        xacc = A[:, 16:24, :]
        lnm = area(3200, T)
        lnr = area(3500, T)

        def head_area(h):
            b = 3072 * (h % 2)
            names = {}
            for i, n in enumerate(["G", "E1", "E2", "EL", "EG", "QD"]):
                names[n] = area(b + 256 * i, NP)
            names["ktm"] = area(b + 1536, NC, P)
            names["vtm"] = area(b + 2048, NC, 256)
            return names
        SC = area(6144, NP)
        ST = area(6400, NC, 256)
        KDEC = area(7424, 128)
        KMASK = area(7552, 4, P)
        VDEC = area(8064, 256)
        DEC = area(8320, 8)
        QS = area(8328, 8)
        DST = area(8600, 4, 256)
        SQ = area(9624, 2, T)
        s_E = W[:, 0:2048].rearrange("p (c h t) -> p c h t", c=NCS, h=8)
        s_xdt = area(2048, NCS, 512)
        s_xw = area(3072, NCS, 512)
        s_btm = area(4096, NCS, P)
        s_g0 = area(4352, NCS, P)
        s_S = area(4608, NCS, 512)
        s_eg = area(5632, 512)
        s_yi = area(6144, 512)
        s_xdec = area(6656, 512)
        s_bdec = area(7168, P)
        s_bmask = area(7296, NB, P)
        s_dst = area(8320, 2, 512)
        s_sq = area(9344, 4, T)
        s_tm = area(10400, 4, 16)
        s_w = area(10464, 2, 16)
        s_el = area(10496, 2, 16)
        s_dd = area(10528, 16)
        s_egd = area(10544, NB, 16)
        dtT = sb("dtT", [16, 3, T])

        @block.gpsimd
        def _(pool):
            st = Steps(pool, "pool_steps")
            st.add(pool.memset(ident[:, :], 0.0))
            st.add(pool.memset(ones[:, :], 1.0))
            st.add(pool.memset(causal[:, :], 1.0))
            st.add(pool.memset(restart[:, :], 1.0))
            st.add(pool.iota(rt[:, 0, 0, :].bitcast(mybir.dt.int32), pattern=[[-1, E_N]], base=E_N, channel_multiplier=0))
            st.settle()
            st.add(pool.affine_select(out=ident[:, :], in_=ident[:, :], compare_op=ALU.not_equal, fill=1.0, base=0,
                                      pattern=[[-1, P]], channel_multiplier=1))
            st.add(pool.affine_select(out=causal[:, :], in_=causal[:, :], compare_op=ALU.is_ge, fill=0.0, base=0,
                                      pattern=[[1, P]], channel_multiplier=-1))
            st.add(pool.memset(restart[:, :].rearrange("p (c t) -> p c t", t=C)[:, :, 0:1], 0.0))
            st.add(pool.tensor_copy(idx16[:, :], rt[:, 0, 0, :].bitcast(mybir.dt.int32)))
            st.settle()
            pool.sem_inc(sem("consts_made"), 1)

            def gated_states(layer, nh, dv, src, dst_p, dst_s):
                tag = "heads"
                H0 = 4 * layer
                for h in range(nh):
                    for q in range(2):
                        n = 2 * h + q
                        if n == 0:
                            pool.wait_ge(sem(tag + "_area_free"), layer + 1)
                        buf = DST[:, :, 0:dv]
                        if n >= 1:
                            pool.wait_ge(sem(tag + "_state_stored"), 16 * (2 * H0 + n))
                        pool.dma_start(buf, src[0, 4 * q:4 * q + 4, h].rearrange("b k v -> k b v")).then_inc(
                            sem(tag + "_state_loaded"), 16)
                        pool.wait_ge(sem(tag + "_state_used"), (2 * H0 + n) + 1)
                        pool.dma_start(dst_s[0, 4 * q:4 * q + 4, h].rearrange("b k v -> k b v"), buf).then_inc(
                            sem(tag + "_state_stored"), 16)
                    pool.wait_ge(sem(tag + "_states_ready"), (H0 + h) + 1)
                    pool.dma_start(dst_p[0, 0, h], ST[:, NC - 1, 0:dv]).then_inc(sem(tag + "_prompt_state_stored"), 16)
                pool.wait_ge(sem(tag + "_state_stored"), 16 * 2 * (H0 + nh))
                pool.wait_ge(sem(tag + "_prompt_state_stored"), 16 * (H0 + nh))

            pool.wait_ge(sem("convout_ready"), 3)
            pool.dma_start(conv_p[0, 0], convout[5:8, :]).then_inc(sem("conv_stored"), 16)
            pool.dma_start(conv_s[0, :, 2], convout[8:16, :]).then_inc(sem("conv_stored"), 16)
            pool.dma_start(conv_s[0, :, 0:2], state_conv[0, :, 1:3]).then_inc(sem("conv_stored"), 16)
            pool.wait_ge(sem("conv_stored"), 48)
            stage_end(pool, 1)
            gated_states(0, 4, 256, state_gla, gla_p, gla_s)
            stage_end(pool, 2)
            for g in range(2):
                for b in range(NB):
                    n = NB * g + b
                    buf = s_dst[:, n % 2, :].rearrange("p (h v) -> p h v", h=8)
                    if n >= 2:
                        pool.wait_ge(sem(f"ssd_stored{n % 2}"), 16 * (n // 2))
                    pool.dma_start(buf, state_ssd[0, b, 8 * g:8 * g + 8].rearrange("h n v -> n h v")).then_inc(
                        sem(f"ssd_loaded{n % 2}"), 16)
                    if n >= 1:
                        m = n - 1
                        pool.wait_ge(sem("ssd_state_used"), m + 1)
                        pool.dma_start(ssd_s[0, m % NB, 8 * (m // NB):8 * (m // NB) + 8].rearrange("h n v -> n h v"),
                                       s_dst[:, m % 2, :].rearrange("p (h v) -> p h v", h=8)).then_inc(
                            sem(f"ssd_stored{m % 2}"), 16)
                if g == 0:
                    pool.wait_ge(sem("ssd_prompt_state"), 1)
                    pool.dma_start(ssd_p[0, 0, 0:8].rearrange("h n v -> n h v"),
                                   s_S[:, 1, :].rearrange("p (h v) -> p h v", h=8)).then_inc(sem("ssd_p_stored"), 16)
            m = 2 * NB - 1
            pool.wait_ge(sem("ssd_state_used"), m + 1)
            pool.dma_start(ssd_s[0, NB - 1, 8:16].rearrange("h n v -> n h v"),
                           s_dst[:, m % 2, :].rearrange("p (h v) -> p h v", h=8)).then_inc(sem(f"ssd_stored{m % 2}"), 16)
            pool.wait_ge(sem("ssd_prompt_state"), 2)
            pool.dma_start(ssd_p[0, 0, 8:16].rearrange("h n v -> n h v"),
                           s_S[:, 1, :].rearrange("p (h v) -> p h v", h=8)).then_inc(sem("ssd_p_stored"), 16)
            for i in range(2):
                pool.wait_ge(sem(f"ssd_stored{i}"), 16 * NB)
            pool.wait_ge(sem("ssd_p_stored"), 32)
            for k in range(3, 6):
                stage_end(pool, k)
            gated_states(1, 8, 128, state_hgrn, hg_p, hg_s)
            for k in range(6, 9):
                stage_end(pool, k)

        @block.tensor
        def _(pe):
            def slot_ready(n, base=None):
                pe.wait_ge(sem(f"slot_filled{n % SLOTS}"), 16 * (n // SLOTS + 1))

            pe.wait_ge(sem("consts_made"), 1)
            pe.wait_ge(sem("x_loaded"), 32)
            for c in range(DC):
                for b, n in enumerate((P, P, NB)):
                    tr = pe.transpose(bank[c][:, b * P:b * P + n], xrows[0:n, b, c * P:(c + 1) * P], ident[0:n, 0:n])
                tr.then_inc(sem("xT_turned"), 1)
            pe.wait_ge(sem("vectors_loaded"), 16 * 21)
            pe.wait_ge(sem("xT_copied"), 8)
            pe.transpose(bank[0][:, 0:V_N], vrows[0:V_N, :], ident[0:V_N, 0:V_N]).then_inc(sem("vectors_turned"), 1)
            for m in range(12):
                tr = pe.transpose(bank[1][:, m * 29:(m + 1) * 29], crows[0:29, m * P:(m + 1) * P], ident[0:29, 0:29])
            tr.then_inc(sem("vectors_turned"), 1)
            pe.wait_ge(sem("xT_copied"), 8)
            pe.wait_ge(sem("vectors_copied"), 2)
            m = 0
            for g in range(11):
                slot_ready(AB_IN0 + g)
                w = slot(AB_IN0 + g, 8)
                for i in range(4):
                    if m >= 4:
                        pe.wait_ge(sem(f"in0_copied{m % 2}"), (m - 4) // 2 + 1)
                    for c in range(DC):
                        mm = pe.matmul(bank[m % 4][:, 0:T], w[:, c, i * P:(i + 1) * P], xT[:, c, :],
                                       start=(c == 0), stop=(c == DC - 1))
                    mm.then_inc(sem("in0_ready"), 1)
                    m += 1
            for i in range(2):
                for c in range(DC):
                    mm = pe.matmul(bank[4 + i][0:16, 0:T], wsmall[:, c, 16 * i:16 * i + 16], xT[:, c, :],
                                   start=(c == 0), stop=(c == DC - 1))
                mm.then_inc(sem("small_ready"), 1)
            pe.wait_ge(sem("in0_copied0"), 22)
            pe.wait_ge(sem("in0_copied1"), 22)
            pe.wait_ge(sem("small_copied"), 2)
            for m in range(12):
                tr = pe.transpose(bank[5 + m // 4][0:16, (m % 4) * P:(m % 4 + 1) * P], A[:, XS0 + m, NP - 8:T],
                                  ident[:, :])
                if m % 4 == 3:
                    tr.then_inc(sem("conv_turned"), 1)
            for h in range(4):
                mm = pe.matmul(bank[h][:, 0:T], wgk[:, h * P:(h + 1) * P], lrT[:, :], start=True, stop=True)
                mm.then_inc(sem("gk_ready"), 1)
            stage_end(pe, 1)

            def gated_heads(layer, nh, dv, qa, ka, va):
                tag = "heads_"
                H0 = 4 * layer
                J = dv // P
                for h in range(nh):
                    hb = head_area(h)
                    if h >= 1:
                        pe.wait_ge(sem(tag + "normed"), (H0 + h))
                    per = 512 // dv
                    for c in range(NC):
                        for j in range(J):
                            tr = pe.transpose(bank[c // per][0:C, (c % per) * dv + j * P:(c % per) * dv + (j + 1) * P],
                                              va(h, j)[:, c * C:(c + 1) * C], ident[:, :])
                    pe.transpose(bank[2][0:NB, 0:P], ka(h)[:, NP:T], ident[:, :])
                    for j in range(J):
                        tr = pe.transpose(bank[2][0:NB, (j + 1) * P:(j + 2) * P], va(h, j)[:, NP:T], ident[:, :])
                    tr.then_inc(sem(tag + "v_turned"), 1)
                    pe.wait_ge(sem(tag + "prepared"), (H0 + h) + 1)
                    for c in range(NC):
                        s = slice(c * C, (c + 1) * C)
                        mm = pe.matmul(bank[4][0:C, s], hb["E2"][:, s], hb["E1"][:, s], start=True, stop=True)
                    mm.then_inc(sem(tag + "scores_ready"), 1)
                    for c in range(NC):
                        s = slice(c * C, (c + 1) * C)
                        tr = pe.transpose(bank[3][0:C, c * P:(c + 1) * P], hb["EL"][:, s], ident[:, :])
                    tr.then_inc(sem(tag + "k_turned"), 1)
                    pe.wait_ge(sem(tag + "kv_copied"), 3 * (H0 + h) + 3)
                    for c in range(NC):
                        mm = pe.matmul(bank[c // per][:, (c % per) * dv:(c % per + 1) * dv], hb["ktm"][0:C, c, :],
                                       hb["vtm"][0:C, c, 0:dv], start=True, stop=True)
                    mm.then_inc(sem(tag + "updates_ready"), 1)
                    for b in range(NB):
                        if b % 4 == 0:
                            pe.wait_ge(sem(tag + "kmask_ready"), 2 * (H0 + h) + b // 4 + 1)
                        if b >= 2:
                            pe.wait_ge(sem(tag + "dec_updated"), NB * (H0 + h) + b - 1)
                        pe.matmul(bank[6 + b % 2][:, 0:dv], KMASK[0:NB, b % 4, :], VDEC[0:NB, 0:dv], start=True,
                                  stop=True).then_inc(sem(tag + "dec_update_ready"), 1)
                        if b % 4 == 3:
                            pe.wait_ge(sem(tag + "dec_updated"), NB * (H0 + h) + b + 1)
                            pe.wait_ge(sem(tag + "scores_masked"), (H0 + h) + 1)
                            for bb in range(b - 3, b + 1):
                                for j in range(J):
                                    mm = pe.matmul(bank[4][:, 256 + j * NB + bb:257 + j * NB + bb],
                                                   DST[:, bb % 4, j * P:(j + 1) * P], QS[:, bb:bb + 1],
                                                   start=True, stop=True)
                            mm.then_inc(sem(tag + "state_used"), 1)
                    pe.wait_ge(sem(tag + "states_ready"), (H0 + h) + 1)
                    for j in range(J):
                        for c in range(NC):
                            s = slice(c * C, (c + 1) * C)
                            mm = pe.matmul(bank[5][:, j * NP + c * C:j * NP + (c + 1) * C],
                                           hb["vtm"][0:C, c, j * P:(j + 1) * P], SC[0:C, s], start=True, stop=(c == 0))
                            if c > 0:
                                mm = pe.matmul(bank[5][:, j * NP + c * C:j * NP + (c + 1) * C],
                                               ST[:, c - 1, j * P:(j + 1) * P], hb["QD"][:, s], start=False, stop=True)
                    mm.then_inc(sem(tag + "out_ready"), 1)
                    pe.wait_ge(sem(tag + "squared"), (H0 + h) + 1)
                    for j in range(J):
                        mm = pe.matmul(bank[3][:, 0:T], ones[:, :], SQ[:, j, :], start=(j == 0), stop=(j == J - 1))
                    mm.then_inc(sem(tag + "square_sums"), 1)

            gated_heads(0, 4, 256, lambda h: A[:, Q0 + h, :], lambda h: A[:, K0 + h, :],
                        lambda h, j: A[:, VV0 + 2 * h + j, :])
            stage_end(pe, 2)

            pe.wait_ge(sem("dt_ready"), 1)
            for c in range(NCS):
                s = slice(c * CS, (c + 1) * CS)
                pe.transpose(bank[0][:, 16 * c:16 * c + 16], dtT[:, 1, s], ident[0:16, 0:16])
                pe.transpose(bank[0][:, 32 + 16 * c:48 + 16 * c], dtT[:, 0, s], ident[0:16, 0:16])
            pe.transpose(bank[0][0:NB, 64:80], dtT[:, 0, NP:T], ident[0:16, 0:16])
            for c in range(NCS):
                pe.matmul(bank[0][:, 80 + 16 * c:96 + 16 * c],
                          dtT[:, 1, (c + 1) * CS - 1:(c + 1) * CS].to_broadcast([16, P]), ident[0:16, 0:16],
                          start=True, stop=True)
            for b in range(NB):
                mm = pe.matmul(bank[0][:, 112 + 16 * b:128 + 16 * b],
                               dtT[:, 2, NP + b:NP + b + 1].to_broadcast([16, P]), ident[0:16, 0:16],
                               start=True, stop=True)
            mm.then_inc(sem("tm_ready"), 1)
            pe.wait_ge(sem("tm_copied"), 1)
            for g in range(2):
                BT, CT = A[:, B0 + g, :], A[:, C0 + g, :]
                if g == 1:
                    pe.wait_ge(sem("ssd_normed"), 1)
                for c in range(NCS):
                    s = slice(c * CS, (c + 1) * CS)
                    pe.transpose(bank[0][:, c * P:(c + 1) * P], BT[:, s], ident[:, :])
                pe.transpose(bank[0][0:NB, 256:384], BT[:, NP:T], ident[:, :])
                for c in range(NCS):
                    s = slice(c * CS, (c + 1) * CS)
                    for j in range(4):
                        pe.transpose(bank[1 + c][:, j * P:(j + 1) * P], A[:, XS0 + 4 * g + j, s], ident[:, :])
                for j in range(4):
                    pe.transpose(bank[3][0:NB, j * P:(j + 1) * P], A[:, XS0 + 4 * g + j, NP:T], ident[:, :])
                for c in range(NCS):
                    s = slice(c * CS, (c + 1) * CS)
                    mm = pe.matmul(bank[4][:, c * P:(c + 1) * P], BT[:, s], CT[:, s], start=True, stop=True)
                mm.then_inc(sem("ssd_turned"), 1)
                for pr in range(4):
                    if pr >= 2:
                        pe.wait_ge(sem("ssd_diffs"), 4 * g + pr - 1)
                    for i in range(2):
                        h = 8 * g + 2 * pr + i
                        mm = pe.matmul(bank[5 + pr % 2][:, i * NP:(i + 1) * NP],
                                       ident[0:16, h:h + 1].to_broadcast([16, P]), dtT[:, 1, 0:NP],
                                       start=True, stop=True)
                    mm.then_inc(sem("gbc_ready"), 1)
                pe.wait_ge(sem("ssd_tm_copied"), g + 1)
                for c in range(NCS):
                    if c == 1:
                        pe.wait_ge(sem("ssd_state0"), g + 1)
                    pe.matmul(bank[7][:, :], s_btm[:, c, :], s_xw[:, c, :], start=True, stop=True).then_inc(
                        sem("ssd_update_ready"), 1)
                pe.wait_ge(sem("ssd_btm_copied"), g + 1)
                for j in range(4):
                    h = 8 * g + 2 * j
                    for i in range(2):
                        mm = pe.matmul(bank[0][64 * i:64 * i + 64, j * P:(j + 1) * P],
                                       ident[0:16, h + i:h + i + 1].to_broadcast([16, 64]), dtT[:, 2, CS:NP],
                                       start=True, stop=True)
                mm.then_inc(sem("eg_ready"), 1)
                pe.wait_ge(sem("ssd_scores"), 2 * g + 2)
                for j in range(4):
                    for c in range(NCS):
                        for i in range(2):
                            hh = 2 * j + i
                            mm = pe.matmul(bank[1 + j // 2][64 * i:64 * i + 64,
                                                            (j % 2) * NP + c * CS:(j % 2) * NP + (c + 1) * CS],
                                           s_xdt[:, c, hh * 64:(hh + 1) * 64], s_E[:, c, hh, :], start=True, stop=True)
                mm.then_inc(sem("ssd_intra"), 1)
                for j in range(4):
                    mm = pe.matmul(bank[3][:, j * P:(j + 1) * P], s_S[:, 0, j * P:(j + 1) * P], CT[:, CS:NP],
                                   start=True, stop=True)
                mm.then_inc(sem("ssd_inter"), 1)
                for b in range(NB):
                    n = NB * g + b
                    if b == 0:
                        pe.wait_ge(sem("ssd_diffs"), 4 * g + 4)
                    if b >= 2:
                        pe.wait_ge(sem("ssd_dec_updated"), n - 1)
                    else:
                        pe.wait_ge(sem("bmask_ready"), g + 1)
                    pe.matmul(bank[5 + b % 2][:, :], s_bmask[0:NB, b, :], s_xdec[0:NB, :], start=True, stop=True
                              ).then_inc(sem("ssd_dec_ready"), 1)
                    pe.wait_ge(sem("ssd_dec_updated"), n + 1)
                    for j in range(4):
                        mm = pe.matmul(bank[4][:, 256 + j * NB + b:257 + j * NB + b], s_dst[:, n % 2, j * P:(j + 1) * P],
                                       CT[:, NP + b:NP + b + 1], start=True, stop=True)
                    mm.then_inc(sem("ssd_state_used"), 1)
                pe.wait_ge(sem("ssd_squared"), g + 1)
                for j in range(4):
                    mm = pe.matmul(bank[7][:, 0:T], ones[:, :], s_sq[:, j, :], start=(j == 0), stop=(j == 3))
                mm.then_inc(sem("ssd_square_sums"), 1)
            stage_end(pe, 3)

            def out_project(n0, groups, kc, srcs, tag):
                m = 0
                per = DC // groups
                for g in range(groups):
                    slot_ready(n0 + g)
                    w = slot(n0 + g, kc)
                    for i in range(per):
                        for c in range(kc):
                            mm = pe.matmul(bank[m][:, 0:T], w[:, c, i * P:(i + 1) * P], srcs(c),
                                           start=(c == 0), stop=(c == kc - 1))
                        mm.then_inc(sem(tag + "_ready"), 1)
                        m += 1

            def norm_sums(k):
                pe.wait_ge(sem("norm_residual"), k + 1)
                for c in range(DC):
                    mm = pe.matmul(bank[0][:, 0:T], ones[:, :], xT[:, c, :], start=(c == 0), stop=(c == DC - 1))
                mm.then_inc(sem("norm_sum"), 1)
                pe.wait_ge(sem("norm_squares"), k + 1)
                for c in range(DC):
                    mm = pe.matmul(bank[1][:, 0:T], ones[:, :], lnsq[:, c, :], start=(c == 0), stop=(c == DC - 1))
                mm.then_inc(sem("norm_sum"), 1)

            def experts(n0, layer):
                tag = "moe"
                for b, n in enumerate((P, P, NB)):
                    for c in range(DC):
                        mm = pe.matmul(bank[2][0:n, 16 * b:16 * b + 16], xT[:, c, b * P:b * P + n], router[:, c, :],
                                       start=(c == 0), stop=(c == DC - 1))
                mm.then_inc(sem(tag + "_logits"), 1)
                pe.wait_ge(sem(tag + "_gates"), layer + 1)
                for b, n in enumerate((P, P, NB)):
                    tr = pe.transpose(bank[3][0:16, b * P:b * P + n], gate[0:n, b, :], ident[0:n, 0:n])
                tr.then_inc(sem(tag + "_gates_turned"), 1)
                pe.wait_ge(sem(tag + "_gates_copied"), layer + 1)
                with pe.Fori(0, E_N // 2) as pair:
                    e = 2 * pair
                    for j in range(2):
                        pe.wait_ge(sem(tag + "_sel"), (E_N * layer + e) + j + 1)
                        pe.wait_ge(sem(tag + "_gbc_copied"), (E_N * layer + e) + j + 1)
                        pe.matmul(bank[6][:, 0:T], msel[0:16, j, :], gateT[:, :], start=True, stop=True).then_inc(
                            sem(tag + "_gbc"), 1)
                        n = n0 + 3 * j
                        for i in range(2):
                            pe.wait_ge(sem(f"slot_filled{(n + i) % SLOTS}"), 8 * e + 16 * ((n + i) // SLOTS + 1))
                        wg, wu = slot(n, 8), slot(n + 1, 8)
                        for f in range(4):
                            k = 4 * j + f
                            pe.wait_ge(sem(tag + "_hidden"), 4 * (E_N * layer + e) + k + 1)
                            for c in range(DC):
                                pe.matmul(bank[f % 2][:, 0:T], wg[:, c, f * P:(f + 1) * P], xT[:, c, :],
                                          start=(c == 0), stop=(c == DC - 1))
                            for c in range(DC):
                                mm = pe.matmul(bank[2 + f % 2][:, 0:T], wu[:, c, f * P:(f + 1) * P], xT[:, c, :],
                                               start=(c == 0), stop=(c == DC - 1))
                            mm.then_inc(sem(tag + "_gu"), 1)
                        pe.wait_ge(sem(f"slot_filled{(n + 2) % SLOTS}"), 8 * e + 16 * ((n + 2) // SLOTS + 1))
                        pe.wait_ge(sem(tag + "_hidden"), 4 * (E_N * layer + e) + 4 * j + 6)
                        wd = slot(n + 2, 4)
                        for d in range(DC):
                            pe.wait_ge(sem(tag + "_down_added"), 8 * (E_N * layer + e) + 8 * j + d + 1)
                            for f in range(4):
                                mm = pe.matmul(bank[4 + d % 2][:, 0:T], wd[:, f, d * P:(d + 1) * P], mh[:, j, f, :],
                                               start=(f == 0), stop=(f == 3))
                            mm.then_inc(sem(tag + "_down"), 1)

            def out_chunks(c):
                return A[:, (VV0 + c) if c < 8 else (XS0 + c - 8), :]

            out_project(AB_OUT0, 4, 16, out_chunks, "out0")
            norm_sums(0)
            stage_end(pe, 4)
            experts(MOE0, 0)
            norm_sums(1)
            stage_end(pe, 5)
            m = 0
            for g in range(8):
                slot_ready(C_IN0 + g)
                w = slot(C_IN0 + g, 8)
                for i in range(4):
                    if m >= 4:
                        pe.wait_ge(sem(f"in1_copied{m % 2}"), (m - 4) // 2 + 1)
                    for c in range(DC):
                        mm = pe.matmul(bank[m % 4][:, 0:T], w[:, c, i * P:(i + 1) * P], xT[:, c, :],
                                       start=(c == 0), stop=(c == DC - 1))
                    mm.then_inc(sem("in1_ready"), 1)
                    m += 1
            pe.wait_ge(sem("hg_prepared"), 1)
            pe.wait_ge(sem("in1_copied0"), 16)
            pe.wait_ge(sem("in1_copied1"), 16)
            gated_heads(1, 8, 128, lambda h: A[:, h, :], lambda h: A[:, 32 + h, :], lambda h, j: A[:, 16 + h, :])
            stage_end(pe, 6)
            out_project(C_OUT0, 2, 8, lambda c: A[:, 16 + c, :], "out1")
            norm_sums(2)
            stage_end(pe, 7)
            experts(MOE1, 1)
            norm_sums(3)
            stage_end(pe, 8)
            for b, n in enumerate((P, P, NB)):
                for c in range(DC):
                    tr = pe.transpose(bank[2 * b + c // 4][0:n, (c % 4) * P:(c % 4 + 1) * P], xT[:, c, b * P:b * P + n],
                                      ident[:, :])
                    if c % 4 == 3:
                        tr.then_inc(sem("y_turned"), 1)

        @block.scalar
        def _(act):
            def load(dst, src, name):
                act.dma_start(dst, src, allow_slow_non_contiguous=True).then_inc(sem(name), 16)

            load(xrows[:, 0:2, :], x_prompt[0].rearrange("(b p) d -> p b d", p=P), "x_loaded")
            load(xrows[0:NB, 2, :], x_sample.rearrange("b o d -> (b o) d"), "x_loaded")

            def rows(r, n, v):
                load(vrows[r:r + n, :], v, "vectors_loaded")

            rows(V_BGK, 4, b_gk2.rearrange("o (r p) -> (o r) p", p=P))
            rows(V_GLAN, 2, gla_norm_w.rearrange("o (r p) -> (o r) p", p=P))
            rows(V_SSDN, 8, ssd_norm_w.rearrange("o (r p) -> (o r) p", p=P))
            for r, v in ((V_LN1W, ln1_w), (V_LN1B, ln1_b), (V_LN2W, ln2_w), (V_LN2B, ln2_b)):
                rows(r, 16, v.rearrange("o (r p) -> (o r) p", p=P))
            rows(V_HGN, 1, hg_norm_w)
            rows(V_LB, 16, lower_bounds.rearrange("o (r p) -> (o r) p", p=P))
            load(crows[0:24, :], state_conv[0].rearrange("b j n -> (b j) n"), "vectors_loaded")
            load(crows[24:28, :], conv_w[0], "vectors_loaded")
            load(crows[28:29, :], conv_b, "vectors_loaded")
            load(wgk[:, :], w_gk2[0], "vectors_loaded")
            load(router[:, :, :], router_w.rearrange("(c p) e -> p c e", p=P), "vectors_loaded")
            load(wsmall[:, :, 0:16], w_in_ab[0, :, 3072:3088].rearrange("(c p) n -> p c n", p=P), "vectors_loaded")
            load(wsmall[:, :, 16:32], w_in_ab[0, :, 5648:5664].rearrange("(c p) n -> p c n", p=P), "vectors_loaded")
            load(small[:, 0:1], dt_bias.rearrange("o h -> h o"), "vectors_loaded")
            load(small[:, 1:2], a_log.rearrange("o h -> h o"), "vectors_loaded")
            load(rbias[:, :], router_bias.rearrange("(o e) -> o e", o=1).to_broadcast([P, E_N]), "vectors_loaded")
            for i in range(2):
                load(dskip[64 * i:64 * i + 64, :],
                     d_skip.rearrange("o (j i) -> o i j", i=2)[:, i, :].to_broadcast([64, 8]), "vectors_loaded")

            st = Steps(act, "act_steps")
            for c in range(0, DC, 2):
                act.wait_ge(sem("xT_turned"), c + 1)
                st.run(act.copy(xT[:, c, :], bank[c][:, 0:T]))
                act.sem_inc(sem("xT_copied"), 1)
            act.wait_ge(sem("vectors_turned"), 1)
            st.run(act.copy(cols[:, :], bank[0][:, 0:V_N]))
            act.sem_inc(sem("vectors_copied"), 1)
            st.run(act.activation(small[:, 2:3], small[:, 1:2], ACT.Exp))
            act.wait_ge(sem("lb_diff"), 1)
            st.run(act.activation(lbc[:, 0, :], lbc[:, 2, :], ACT.Tanh, scale=0.5))
            act.sem_inc(sem("lb_tanh"), 1)

            for m in range(0, AB_CHUNKS, 2):
                act.wait_ge(sem("in0_ready"), m + 1)
                act.copy(A[:, m, :], bank[m % 4][:, 0:T]).then_inc(sem("in0_copied0"), 1)
            act.wait_ge(sem("in0_copied0"), 22)
            act.wait_ge(sem("in0_copied1"), 22)
            act.wait_ge(sem("conv_turned"), 3)
            for a0 in (G0, Z0):
                st.run(act.activation(A[:, a0:a0 + 8, :], A[:, a0:a0 + 8, :], ACT.Silu))
            for m in range(12):
                act.wait_ge(sem("conv_done"), m + 1)
                act.activation(A[:, XS0 + m, :], cacc[:, m % 2, :], ACT.Silu).then_inc(sem("conv_silu"), 1)
            act.wait_ge(sem("conv_silu"), 12)
            for h in range(4):
                act.wait_ge(sem("gk_ready"), h + 1)
                st.run(act.activation(gkz[:, h, :], bank[h][:, 0:T], ACT.Identity, bias=cols[:, V_BGK + h:V_BGK + h + 1]))
            st.run(act.activation(gka[:, :, :], gkz[:, :, :], ACT.Abs))
            st.run(act.activation(gka[:, :, :], gka[:, :, :], ACT.Exp, scale=-1.0))
            st.run(act.activation(gka[:, :, :], gka[:, :, :], ACT.Ln, bias=1.0))
            act.wait_ge(sem("small_copied"), 2)
            st.run(act.activation(dtT[:, 0, :], dtT[:, 0, :], ACT.Identity, bias=small[:, 0:1]))
            st.run(act.activation(dtT[:, 1, :], dtT[:, 0, :], ACT.Abs))
            st.run(act.activation(dtT[:, 1, :], dtT[:, 1, :], ACT.Exp, scale=-1.0))
            st.run(act.activation(dtT[:, 1, :], dtT[:, 1, :], ACT.Ln, bias=1.0))
            act.sem_inc(sem("gates_ln"), 1)
            stage_end(act, 1)

            def gated_heads(layer, nh, dv, va, gates):
                tag = "heads_"
                H0 = 4 * layer
                J = dv // P

                def exps(h):
                    hb = head_area(h)
                    act.wait_ge(sem(tag + "g_scanned"), (H0 + h) + 1)
                    st.add(act.activation(hb["E2"], hb["E1"], ACT.Exp, scale=-1.0))
                    st.add(act.activation(hb["EG"], hb["G"], ACT.Exp))
                    st.add(act.activation(hb["EL"], hb["EL"], ACT.Exp))
                    st.settle()
                    act.activation(hb["E1"], hb["E1"], ACT.Exp).then_inc(sem(tag + "exps"), 1)
                    act.wait_ge(sem(tag + "exps"), (H0 + h) + 1)

                st.run(act.activation(decx[:, 0:nh, :], (gkg[:, 0:4, NP:T] if layer == 0 else A[:, 8:16, NP:T]), ACT.Exp))
                act.sem_inc(sem("dec_exps"), 1)
                exps(0)
                for h in range(nh):
                    hb = head_area(h)
                    per = 512 // dv
                    act.wait_ge(sem(tag + "v_turned"), (H0 + h) + 1)
                    act.activation(hb["vtm"][0:C, 0:per, 0:dv], bank[0][0:C, :].rearrange("p (c v) -> p c v", v=dv),
                                   ACT.Copy).then_inc(sem(tag + "kv_copied"), 1)
                    if per < NC:
                        act.activation(hb["vtm"][0:C, per:NC, 0:dv], bank[1][0:C, :].rearrange("p (c v) -> p c v", v=dv),
                                       ACT.Copy).then_inc(sem(tag + "kv_copied"), 1)
                    else:
                        act.sem_inc(sem(tag + "kv_copied"), 1)
                    act.wait_ge(sem(tag + "k_turned"), (H0 + h) + 1)
                    act.activation(hb["ktm"][0:C, :, :], bank[3][0:C, :].rearrange("p (c k) -> p c k", k=P),
                                   ACT.Copy).then_inc(sem(tag + "kv_copied"), 1)
                    if h + 1 < nh:
                        exps(h + 1)
                    act.wait_ge(sem(tag + "out_copied"), (H0 + h) + 1)
                    for j in range(J):
                        sq = act.activation(SQ[:, j, :], va(h, j), ACT.Square, scale=dv ** -0.5)
                        st.add(sq)
                    st.settle()
                    act.sem_inc(sem(tag + "squared"), 1)
                gall = gkg[:, :, :] if layer == 0 else A[:, 8:16, :]
                act.wait_ge(sem(tag + "normed"), H0 + nh)
                st.run(act.activation(gall, gall, ACT.Sqrt))
                act.sem_inc(sem(tag + "roots"), 1)

            gated_heads(0, 4, 256, lambda h, j: A[:, VV0 + 2 * h + j, :], None)
            act.wait_ge(sem("dt_scanned"), 1)
            st.run(act.activation(dtT[:, 2, :], dtT[:, 1, :], ACT.Exp))
            act.sem_inc(sem("dt_ready"), 1)
            stage_end(act, 2)
            act.wait_ge(sem("tm_ready"), 1)
            st.add(act.copy(s_tm[:, :, :], bank[0][:, 0:64].rearrange("p (a h) -> p a h", h=16)))
            st.add(act.copy(s_dd[0:NB, :], bank[0][0:NB, 64:80]))
            st.add(act.activation(s_el[:, :, :], bank[0][:, 80:112].rearrange("p (a h) -> p a h", h=16), ACT.Copy))
            st.add(act.copy(s_egd[:, :, :], bank[0][:, 112:240].rearrange("p (a h) -> p a h", h=16)))
            st.settle()
            act.sem_inc(sem("tm_copied"), 1)
            act.wait_ge(sem("w_diff"), 1)
            st.add(act.activation(s_w[:, :, :], s_w[:, :, :], ACT.Exp))
            st.add(act.activation(s_el[:, :, :], s_el[:, :, :], ACT.Exp))
            st.settle()
            act.sem_inc(sem("w_exp"), 1)
            for g in range(2):
                act.wait_ge(sem("ssd_turned"), g + 1)
                if g == 1:
                    act.wait_ge(sem("ssd_normed"), 1)
                st.add(act.copy(s_btm[:, :, :], bank[0][:, 0:256].rearrange("p (c k) -> p c k", k=P)))
                st.add(act.copy(s_bdec[0:NB, :], bank[0][0:NB, 256:384]))
                st.settle()
                act.sem_inc(sem("ssd_btm_copied"), 1)
                for pr in range(4):
                    act.wait_ge(sem("ssd_diffs"), 4 * g + pr + 1)
                    for c in range(NCS):
                        e = s_E[:, c, 2 * pr:2 * pr + 2, :]
                        st.add(act.activation(e, e, ACT.Exp))
                st.settle()
                act.sem_inc(sem("ssd_exps"), 1)
                act.wait_ge(sem("ssd_update_ready"), 2 * g + 1)
                st.run(act.copy(s_S[:, 0, :], bank[7][:, :]))
                act.sem_inc(sem("ssd_state0"), 1)
                act.wait_ge(sem("eg_ready"), g + 1)
                st.run(act.copy(s_eg[:, :], bank[0][:, :]))
                act.sem_inc(sem("eg_copied"), 1)
                act.wait_ge(sem("ssd_gated"), g + 1)
                st.run(act.activation(s_sq[:, :, :], A[:, XS0 + 4 * g:XS0 + 4 * g + 4, :], ACT.Square,
                                      scale=NORM_SSD ** -0.5))
                act.sem_inc(sem("ssd_squared"), 1)
            act.wait_ge(sem("ssd_normed"), 2)
            st.run(act.activation(gkg[:, 0:2, :], gkg[:, 0:2, :], ACT.Sqrt))
            act.sem_inc(sem("ssd_roots"), 1)
            stage_end(act, 3)

            def squares(k):
                act.wait_ge(sem("norm_centered"), k + 1)
                st.run(act.activation(lnsq[:, :, :], xT[:, :, :], ACT.Square, scale=D ** -0.5))
                act.sem_inc(sem("norm_squares"), 1)
                act.wait_ge(sem("norm_variance"), k + 1)
                st.run(act.activation(lnr[:, :], lnr[:, :], ACT.Sqrt))
                act.sem_inc(sem("norm_roots"), 1)

            def experts(layer):
                tag = "moe"
                act.wait_ge(sem(tag + "_logits"), layer + 1)
                act.wait_ge(sem(tag + "_score_cleared"), layer + 1)
                for b, n in enumerate((P, P, NB)):
                    st.add(act.activation(score[0:n, b, :], bank[2][0:n, 16 * b:16 * b + 16], ACT.Sigmoid))
                st.settle()
                act.sem_inc(sem(tag + "_scores"), 1)
                if layer == 0:
                    act.sem_inc(sem(tag + "_gbc_copied"), 1)
                with act.Fori(0, E_N // 2) as pair:
                    e = 2 * pair
                    for j in range(2):
                        act.wait_ge(sem(tag + "_gbc"), (E_N * layer + e) + j + 1)
                        act.wait_ge(sem(tag + "_hidden"), 4 * (E_N * layer + e) + 4 * j + 2)
                        act.copy(mgb[:, :], bank[6][:, 0:T]).then_inc(sem(tag + "_gbc_copied"), 1)
                        for f in range(4):
                            act.wait_ge(sem(tag + "_gu"), 4 * (E_N * layer + e) + 4 * j + f + 1)
                            act.wait_ge(sem(tag + "_hidden"), 4 * (E_N * layer + e) + 4 * j + f + 1)
                            act.activation(mg[:, f % 2, :], bank[f % 2][:, 0:T], ACT.Silu).then_inc(sem(tag + "_silu"), 1)

            squares(0)
            stage_end(act, 4)
            experts(0)
            squares(1)
            stage_end(act, 5)
            for m in range(0, 32, 2):
                act.wait_ge(sem("in1_ready"), m + 1)
                act.copy(A[:, m, :], bank[m % 4][:, 0:T]).then_inc(sem("in1_copied0"), 1)
            act.wait_ge(sem("in1_copied0"), 16)
            act.wait_ge(sem("in1_copied1"), 16)
            st.add(act.activation(A[:, 8:16, :], A[:, 8:16, :], ACT.Tanh, scale=0.5))
            st.settle()
            act.sem_inc(sem("hg_tanh"), 1)
            st.add(act.activation(A[:, 0:8, :], A[:, 0:8, :], ACT.Silu))
            st.add(act.activation(A[:, 24:32, :], A[:, 24:32, :], ACT.Silu))
            st.settle()
            act.wait_ge(sem("hg_forget"), 1)
            st.run(act.activation(A[:, 8:16, :], A[:, 8:16, :], ACT.Ln))
            act.sem_inc(sem("hg_log"), 1)
            gated_heads(1, 8, 128, lambda h, j: A[:, 16 + h, :], None)
            stage_end(act, 6)
            squares(2)
            stage_end(act, 7)
            experts(1)
            squares(3)
            stage_end(act, 8)
            yrows = area(0, 3, D)
            for b, n in enumerate((P, P, NB)):
                for i in range(2):
                    act.wait_ge(sem("y_turned"), 2 * b + i + 1)
                    st.run(act.copy(yrows[0:n, b, i * 512:(i + 1) * 512], bank[2 * b + i][0:n, :]))
                if b < 2:
                    act.dma_start(y_prompt[0, b * P:(b + 1) * P, :], yrows[:, b, :]).then_inc(sem("y_stored"), 16)
                else:
                    act.dma_start(y_sample.rearrange("b o d -> (b o) d"), yrows[0:NB, 2, :]).then_inc(sem("y_stored"), 16)
            act.wait_ge(sem("y_stored"), 48)

        @block.vector
        def _(dve):
            st = Steps(dve, "dve_steps")

            def tt(out, a, b, op):
                st.run(dve.tensor_tensor(out, a, b, op))

            for c in range(1, DC, 2):
                dve.wait_ge(sem("xT_turned"), c + 1)
                st.run(dve.tensor_copy(xT[:, c, :], bank[c][:, 0:T]))
                dve.sem_inc(sem("xT_copied"), 1)
            dve.wait_ge(sem("vectors_turned"), 2)
            st.run(dve.tensor_copy(convc[:, :, :], bank[1][:, 0:348].rearrange("p (m r) -> p m r", r=29)))
            dve.sem_inc(sem("vectors_copied"), 1)
            dve.wait_ge(sem("vectors_copied"), 2)
            dve.wait_ge(sem("consts_made"), 1)
            st.run(dve.tensor_tensor(lbc[:, 2, :], cols[:, V_LB + 8:V_LB + 16], cols[:, V_LB:V_LB + 8], ALU.subtract))
            dve.sem_inc(sem("lb_diff"), 1)
            dve.wait_ge(sem("lb_tanh"), 1)
            st.run(dve.tensor_scalar(lbc[:, 1, :], lbc[:, 0, :], -0.25, 0.25, ALU.mult, ALU.add))
            st.run(dve.tensor_scalar(small[:, 2:3], small[:, 2:3], -1.0, None, ALU.mult))

            for m in range(1, AB_CHUNKS, 2):
                dve.wait_ge(sem("in0_ready"), m + 1)
                dve.tensor_copy(A[:, m, :], bank[m % 4][:, 0:T]).then_inc(sem("in0_copied1"), 1)
            dve.wait_ge(sem("small_ready"), 2)
            dve.tensor_copy(lrT[:, :], bank[4][0:16, 0:T]).then_inc(sem("small_copied"), 1)
            dve.tensor_copy(dtT[:, 0, :], bank[5][0:16, 0:T]).then_inc(sem("small_copied"), 1)
            dve.wait_ge(sem("in0_copied0"), 22)
            dve.wait_ge(sem("in0_copied1"), 22)
            for i in range(3):
                dve.wait_ge(sem("conv_turned"), i + 1)
                dve.tensor_copy(convout[0:16, i * 512:(i + 1) * 512], bank[5 + i][0:16, :]).then_inc(sem("convout_ready"), 1)
            for m in range(12):
                x, acc, cc = A[:, XS0 + m, :], cacc[:, m % 2, :], convc[:, m, :]
                if m >= 2:
                    dve.wait_ge(sem("conv_silu"), m - 1)
                st.run(dve.tensor_scalar(acc, x, cc[:, 27:28], cc[:, 28:29], ALU.mult, ALU.add))
                for j in range(3):
                    sh = 3 - j
                    st.add(dve.scalar_tensor_tensor(acc[:, sh:NP], x[:, 0:NP - sh], cc[:, 24 + j:25 + j],
                                                    acc[:, sh:NP], ALU.mult, ALU.add))
                    old = cc[:, 0:24].rearrange("p (b j) -> p b j", j=3)[:, :, j]
                    if j < 2:
                        st.run(dve.scalar_tensor_tensor(acc[:, NP:T], old, cc[:, 24 + j:25 + j], acc[:, NP:T],
                                                        ALU.mult, ALU.add))
                    else:
                        st.settle()
                        dve.scalar_tensor_tensor(acc[:, NP:T], old, cc[:, 24 + j:25 + j], acc[:, NP:T],
                                                 ALU.mult, ALU.add).then_inc(sem("conv_done"), 1)
            dve.wait_ge(sem("gates_ln"), 1)
            st.run(dve.tensor_scalar(gkz[:, :, :], gkz[:, :, :], 0.0, 1.0 / 16.0, ALU.min, ALU.mult))
            st.run(dve.scalar_tensor_tensor(gkg[:, :, :], gka[:, :, :], -1.0 / 16.0, gkz[:, :, :], ALU.mult, ALU.add))
            st.run(dve.scalar_tensor_tensor(dtT[:, 0, :], dtT[:, 0, :], 0.0, dtT[:, 1, :], ALU.max, ALU.add))
            st.run(dve.tensor_scalar(dtT[:, 2, :], dtT[:, 0, :], small[:, 2:3], None, ALU.mult))
            for c in range(NCS):
                s = slice(c * CS, (c + 1) * CS)
                st.add(dve.tensor_tensor_scan(dtT[:, 1, s], ones[0:16, 0:CS], dtT[:, 2, s], 0.0, ALU.mult, ALU.add))
            st.add(dve.tensor_copy(dtT[:, 1, NP:T], dtT[:, 2, NP:T]))
            st.settle()
            dve.sem_inc(sem("dt_scanned"), 1)
            stage_end(dve, 1)
            dve.sem_inc(sem("heads_area_free"), 1)

            def gated_heads(layer, nh, dv, qa, ka, va, ga, oa, scale, wcol):
                tag = "heads_"
                H0 = 4 * layer
                J = dv // P

                def prep(h):
                    hb = head_area(h)
                    g = ga(h)
                    v4 = lambda t: t.rearrange("p (c t) -> p c t", t=C)
                    st.run(dve.tensor_tensor_scan(hb["G"], restart[:, :], g[:, 0:NP], 0.0, ALU.mult, ALU.add))
                    G4 = v4(hb["G"])
                    st.add(dve.tensor_tensor(v4(hb["E1"]), G4, G4[:, :, C // 2 - 1:C // 2].to_broadcast([P, NC, C]),
                                             ALU.subtract))
                    st.add(dve.tensor_tensor(v4(hb["EL"]), G4[:, :, C - 1:C].to_broadcast([P, NC, C]), G4, ALU.subtract))
                    st.settle()
                    dve.sem_inc(sem(tag + "g_scanned"), 1)

                def prods(h):
                    hb = head_area(h)
                    dve.wait_ge(sem(tag + "exps"), (H0 + h) + 1)
                    q, k = qa(h), ka(h)
                    st.add(dve.scalar_tensor_tensor(hb["E1"], q[:, 0:NP], scale, hb["E1"], ALU.mult, ALU.mult))
                    st.add(dve.tensor_tensor(hb["E2"], k[:, 0:NP], hb["E2"], ALU.mult))
                    st.add(dve.scalar_tensor_tensor(hb["QD"], q[:, 0:NP], scale, hb["EG"], ALU.mult, ALU.mult))
                    st.add(dve.tensor_tensor(hb["EL"], k[:, 0:NP], hb["EL"], ALU.mult))
                    st.settle()
                    dve.sem_inc(sem(tag + "prepared"), 1)

                prep(0)
                prods(0)
                for h in range(nh):
                    hb = head_area(h)
                    if h + 1 < nh:
                        prep(h + 1)
                    st.add(dve.tensor_scalar(QS[:, :], qa(h)[:, NP:T], scale, None, ALU.mult))
                    dve.wait_ge(sem(tag + "v_turned"), (H0 + h) + 1)
                    st.add(dve.tensor_copy(KDEC[0:NB, :], bank[2][0:NB, 0:P]))
                    st.add(dve.tensor_copy(VDEC[0:NB, 0:dv], bank[2][0:NB, P:P + dv]))
                    st.settle()
                    km = lambda q: st.run(dve.tensor_tensor(
                        KMASK[0:NB, :, :], KDEC[0:NB, :].rearrange("p (o k) -> p o k", o=1).to_broadcast([NB, 4, P]),
                        ident[0:NB, 4 * q:4 * q + 4].rearrange("p (b o) -> p b o", o=1).to_broadcast([NB, 4, P]), ALU.mult))
                    km(0)
                    dve.sem_inc(sem(tag + "kmask_ready"), 1)
                    dve.wait_ge(sem(tag + "scores_ready"), (H0 + h) + 1)
                    if h >= 1:
                        dve.wait_ge(sem(tag + "out_ready"), (H0 + h))
                    st.run(dve.tensor_tensor(SC[0:C, :].rearrange("p (c t) -> p c t", t=C),
                                             bank[4][0:C, 0:NP].rearrange("p (c t) -> p c t", t=C),
                                             causal[0:C, 0:C].rearrange("p (o t) -> p o t", o=1).to_broadcast([C, NC, C]),
                                             ALU.mult))
                    dve.sem_inc(sem(tag + "scores_masked"), 1)
                    dve.wait_ge(sem(tag + "updates_ready"), (H0 + h) + 1)
                    if h >= 1:
                        dve.wait_ge(sem(tag + "prompt_state_stored"), 16 * (H0 + h))
                    per = 512 // dv
                    for c in range(NC):
                        u = bank[c // per][:, (c % per) * dv:(c % per + 1) * dv]
                        if c == 0:
                            st.run(dve.tensor_copy(ST[:, 0, 0:dv], u))
                        else:
                            st.run(dve.scalar_tensor_tensor(ST[:, c, 0:dv], ST[:, c - 1, 0:dv],
                                                            hb["EG"][:, (c + 1) * C - 1:(c + 1) * C], u, ALU.mult, ALU.add))
                    dve.sem_inc(sem(tag + "states_ready"), 1)
                    for b in range(NB):
                        if b % 4 == 0:
                            dve.wait_ge(sem(tag + "state_loaded"), 16 * (2 * (H0 + h) + b // 4 + 1))
                        if b == 4:
                            dve.wait_ge(sem(tag + "state_used"), 2 * (H0 + h) + 1)
                            km(1)
                            dve.sem_inc(sem(tag + "kmask_ready"), 1)
                        dve.wait_ge(sem(tag + "dec_update_ready"), NB * (H0 + h) + b + 1)
                        s = DST[:, b % 4, 0:dv]
                        dve.scalar_tensor_tensor(s, s, decg(h)[:, b:b + 1], bank[6 + b % 2][:, 0:dv],
                                                 ALU.mult, ALU.add).then_inc(sem(tag + "dec_updated"), 1)
                    if h + 1 < nh:
                        prods(h + 1)
                    dve.wait_ge(sem(tag + "out_ready"), (H0 + h) + 1)
                    dve.wait_ge(sem(tag + "state_used"), 2 * (H0 + h) + 2)
                    for j in range(J):
                        st.add(dve.tensor_copy(oa(h, j)[:, 0:NP], bank[5][:, j * NP:(j + 1) * NP]))
                        st.add(dve.tensor_copy(oa(h, j)[:, NP:T], bank[4][:, 256 + j * NB:256 + (j + 1) * NB]))
                    st.settle()
                    dve.sem_inc(sem(tag + "out_copied"), 1)
                    dve.wait_ge(sem(tag + "square_sums"), (H0 + h) + 1)
                    st.run(dve.tensor_scalar(ga(h), bank[3][:, 0:T], EPS, None, ALU.add))
                    dve.sem_inc(sem(tag + "normed"), 1)
                dve.wait_ge(sem(tag + "roots"), layer + 1)
                gall = gkg[:, :, :] if layer == 0 else A[:, 8:16, :]
                st.run(dve.reciprocal(gall, gall))
                for h in range(nh):
                    for j in range(J):
                        st.add(dve.tensor_tensor(oa(h, j), oa(h, j), ga(h), ALU.mult))
                st.settle()
                for h in range(nh):
                    for j in range(J):
                        st.add(dve.scalar_tensor_tensor(oa(h, j), oa(h, j), cols[:, wcol + j:wcol + j + 1],
                                                        gate_of(layer, h, j), ALU.mult, ALU.mult))
                st.settle()

            def decg(h):
                return decx[:, h, :]

            def gate_of(layer, h, j):
                return A[:, G0 + 2 * h + j, :] if layer == 0 else A[:, 24 + h, :]

            dve.wait_ge(sem("dec_exps"), 1)
            gated_heads(0, 4, 256, lambda h: A[:, Q0 + h, :], lambda h: A[:, K0 + h, :],
                        lambda h, j: A[:, VV0 + 2 * h + j, :], lambda h: gkg[:, h, :],
                        lambda h, j: A[:, VV0 + 2 * h + j, :], HEAD_SCALE, V_GLAN)
            stage_end(dve, 2)

            dve.wait_ge(sem("tm_copied"), 1)
            st.run(dve.tensor_tensor(s_w[:, :, :], s_el[:, :, :], s_tm[:, 0:2, :], ALU.subtract))
            dve.sem_inc(sem("w_diff"), 1)
            dve.wait_ge(sem("w_exp"), 1)
            st.run(dve.tensor_tensor(s_w[:, :, :], s_w[:, :, :], s_tm[:, 2:4, :], ALU.mult))
            for g in range(2):
                hs = slice(8 * g, 8 * g + 8)

                def per_head(a, n, w=64):
                    return a.rearrange("p (h o) -> p h o", o=1).to_broadcast([n, 8, w])
                h8 = lambda t: t.rearrange("p (h v) -> p h v", h=8)
                dve.wait_ge(sem("ssd_turned"), g + 1)
                for c in range(NCS):
                    xp = h8(bank[1 + c][:, :])
                    st.add(dve.tensor_tensor(h8(s_xdt[:, c, :]), xp, per_head(s_tm[:, 2 + c, hs], P), ALU.mult))
                    st.add(dve.tensor_tensor(h8(s_xw[:, c, :]), xp, per_head(s_w[:, c, hs], P), ALU.mult))
                st.add(dve.tensor_tensor(h8(s_xdec[0:NB, :]), h8(bank[3][0:NB, :]), per_head(s_dd[0:NB, hs], NB), ALU.mult))
                st.add(dve.tensor_tensor(s_g0[:, :, :], bank[4][:, 0:256].rearrange("p (c t) -> p c t", t=P),
                                         causal[:, :].rearrange("p (o t) -> p o t", o=1).to_broadcast([P, NCS, P]), ALU.mult))
                dve.wait_ge(sem("ssd_btm_copied"), g + 1)
                st.add(dve.tensor_tensor(
                    s_bmask[0:NB, :, :], s_bdec[0:NB, :].rearrange("p (o k) -> p o k", o=1).to_broadcast([NB, NB, P]),
                    ident[0:NB, 0:NB].rearrange("p (b o) -> p b o", o=1).to_broadcast([NB, NB, P]), ALU.mult))
                st.settle()
                dve.sem_inc(sem("ssd_tm_copied"), 1)
                dve.sem_inc(sem("bmask_ready"), 1)
                for pr in range(4):
                    dve.wait_ge(sem("gbc_ready"), 4 * g + pr + 1)
                    for i in range(2):
                        for c in range(NCS):
                            hh = 2 * pr + i
                            st.add(dve.tensor_scalar(s_E[:, c, hh, :], bank[5 + pr % 2][:, i * NP + c * CS:i * NP + (c + 1) * CS],
                                                     s_tm[:, c, 8 * g + hh:8 * g + hh + 1], 0.0, ALU.subtract, ALU.min))
                    st.settle()
                    dve.sem_inc(sem("ssd_diffs"), 1)
                dve.wait_ge(sem("ssd_exps"), g + 1)
                for c in range(NCS):
                    st.run(dve.tensor_tensor(s_E[:, c, :, :], s_E[:, c, :, :],
                                             s_g0[:, c, :].rearrange("p (o t) -> p o t", o=1).to_broadcast([P, 8, P]), ALU.mult))
                    dve.sem_inc(sem("ssd_scores"), 1)
                dve.wait_ge(sem("ssd_state0"), g + 1)
                if g == 1:
                    dve.wait_ge(sem("ssd_p_stored"), 16)
                st.run(dve.tensor_tensor(h8(s_S[:, 1, :]), h8(s_S[:, 0, :]), per_head(s_el[:, 1, hs], P), ALU.mult))
                dve.wait_ge(sem("ssd_update_ready"), 2 * g + 2)
                st.run(dve.tensor_tensor(s_S[:, 1, :], s_S[:, 1, :], bank[7][:, :], ALU.add))
                dve.sem_inc(sem("ssd_prompt_state"), 1)
                for b in range(NB):
                    n = NB * g + b
                    dve.wait_ge(sem(f"ssd_loaded{n % 2}"), 16 * (n // 2 + 1))
                    s = s_dst[:, n % 2, :]
                    st.run(dve.tensor_tensor(h8(s), h8(s), per_head(s_egd[:, b, hs], P), ALU.mult))
                    dve.wait_ge(sem("ssd_dec_ready"), n + 1)
                    dve.tensor_tensor(s, s, bank[5 + b % 2][:, :], ALU.add).then_inc(sem("ssd_dec_updated"), 1)
                dve.wait_ge(sem("eg_copied"), g + 1)
                dve.wait_ge(sem("ssd_inter"), g + 1)
                st.run(dve.tensor_tensor(s_yi[:, :], s_eg[:, :], bank[3][:, :], ALU.mult))
                dve.wait_ge(sem("ssd_state_used"), NB * g + NB)
                for j in range(4):
                    y = A[:, XS0 + 4 * g + j, :]
                    dk = dskip[:, 4 * g + j:4 * g + j + 1]
                    st.add(dve.scalar_tensor_tensor(y[:, 0:NP], y[:, 0:NP], dk, bank[1 + j // 2][:, (j % 2) * NP:(j % 2 + 1) * NP],
                                                    ALU.mult, ALU.add))
                    st.add(dve.scalar_tensor_tensor(y[:, NP:T], y[:, NP:T], dk, bank[4][:, 256 + j * NB:256 + (j + 1) * NB],
                                                    ALU.mult, ALU.add))
                st.settle()
                ys = A[:, XS0 + 4 * g:XS0 + 4 * g + 4, :]
                st.run(dve.tensor_tensor(ys[:, :, CS:NP], ys[:, :, CS:NP], s_yi[:, :].rearrange("p (j t) -> p j t", t=P), ALU.add))
                st.run(dve.tensor_tensor(ys, ys, A[:, Z0 + 4 * g:Z0 + 4 * g + 4, :], ALU.mult))
                dve.sem_inc(sem("ssd_gated"), 1)
                dve.wait_ge(sem("ssd_square_sums"), g + 1)
                st.run(dve.tensor_scalar(gkg[:, g, :], bank[7][:, 0:T], EPS, None, ALU.add))
                dve.sem_inc(sem("ssd_normed"), 1)
            dve.wait_ge(sem("ssd_roots"), 1)
            st.run(dve.reciprocal(gkg[:, 0:2, :], gkg[:, 0:2, :]))
            for j in range(8):
                w = cols[:, V_SSDN + j:V_SSDN + j + 1]
                st.add(dve.scalar_tensor_tensor(A[:, XS0 + j, :], A[:, XS0 + j, :], w, gkg[:, j // 4, :], ALU.mult, ALU.mult))
            st.settle()
            stage_end(dve, 3)

            def add_out(tag):
                for m in range(DC):
                    dve.wait_ge(sem(tag + "_ready"), m + 1)
                    st.add(dve.scalar_tensor_tensor(xT[:, m, :], xT[:, m, :], ALPHA, bank[m][:, 0:T], ALU.mult, ALU.add))
                st.settle()

            def layer_norm(k, wcol, bcol):
                dve.sem_inc(sem("norm_residual"), 1)
                dve.wait_ge(sem("norm_sum"), 2 * k + 1)
                st.run(dve.tensor_scalar(lnm[:, :], bank[0][:, 0:T], 1.0 / D, None, ALU.mult))
                bc = lambda t: t.rearrange("p (o t) -> p o t", o=1).to_broadcast([P, DC, T])
                st.run(dve.tensor_tensor(xT[:, :, :], xT[:, :, :], bc(lnm[:, :]), ALU.subtract))
                dve.sem_inc(sem("norm_centered"), 1)
                dve.wait_ge(sem("norm_sum"), 2 * k + 2)
                st.run(dve.tensor_scalar(lnr[:, :], bank[1][:, 0:T], EPS, None, ALU.add))
                dve.sem_inc(sem("norm_variance"), 1)
                dve.wait_ge(sem("norm_roots"), k + 1)
                st.run(dve.reciprocal(lnr[:, :], lnr[:, :]))
                st.run(dve.tensor_tensor(xT[:, :, :], xT[:, :, :], bc(lnr[:, :]), ALU.mult))
                for c in range(DC):
                    st.add(dve.tensor_scalar(xT[:, c, :], xT[:, c, :], cols[:, wcol + c:wcol + c + 1],
                                             cols[:, bcol + c:bcol + c + 1], ALU.mult, ALU.add))
                st.settle()

            def pick_first(out, val, mx, sel, width):
                b3 = lambda t: t.to_broadcast([P, 3, width])
                ix = idx16[:, 0:width].rearrange("p (o e) -> p o e", o=1).to_broadcast([P, 3, width])
                st.run(dve.tensor_reduce(mx, val, AX, ALU.max))
                st.run(dve.tensor_tensor(sel, val, b3(mx), ALU.is_equal))
                st.run(dve.tensor_tensor(sel, sel, ix, ALU.mult))
                st.run(dve.tensor_reduce(mx, sel, AX, ALU.max))
                st.run(dve.tensor_tensor(out, sel, b3(mx), ALU.is_equal))

            def route(layer):
                tag = "moe"
                st.run(dve.memset(score[:, :, :], 0.5))
                dve.sem_inc(sem(tag + "_score_cleared"), 1)
                dve.wait_ge(sem(tag + "_scores"), layer + 1)
                sel, t1, t2, oh = (rt[:, i, :, :] for i in range(4))
                mx = rt[:, 4, :, 0:1]
                grp = rt[:, 5, :, 0:4]
                tt(sel, score[:, :, :], rbias[:, :].rearrange("p (o e) -> p o e", o=1).to_broadcast([P, 3, E_N]), ALU.add)
                s4 = sel.rearrange("p b (g i) -> p b g i", i=4)
                v = [s4[:, :, :, i] for i in range(4)]
                a1 = t1.rearrange("p b (g i) -> p b g i", i=4)
                w = [a1[:, :, :, i] for i in range(4)]
                tt(w[0], v[0], v[1], ALU.max)
                tt(w[1], v[0], v[1], ALU.min)
                tt(w[2], v[2], v[3], ALU.max)
                tt(w[3], v[2], v[3], ALU.min)
                a2 = t2.rearrange("p b (g i) -> p b g i", i=4)
                u = [a2[:, :, :, i] for i in range(4)]
                tt(u[0], w[0], w[2], ALU.max)
                tt(u[1], w[0], w[2], ALU.min)
                tt(u[2], w[1], w[3], ALU.max)
                tt(u[3], u[1], u[2], ALU.max)
                tt(grp, u[0], u[3], ALU.add)
                pick_first(rt[:, 6, :, 0:4], grp, mx, rt[:, 7, :, 0:4], 4)
                gsel = rt[:, 6, :, 0:4]
                for i in range(4):
                    tt(w[i], v[i], gsel, ALU.mult)
                st.run(dve.tensor_scalar(rt[:, 7, :, 0:4], gsel, -1.0, BIG, ALU.add, ALU.mult))
                for i in range(4):
                    tt(w[i], w[i], rt[:, 7, :, 0:4], ALU.add)
                pick_first(oh, t1, mx, t2, E_N)
                st.run(dve.scalar_tensor_tensor(t1, oh, -2.0 * BIG, t1, ALU.mult, ALU.add))
                pick_first(rt[:, 7, :, :], t1, mx, t2, E_N)
                tt(oh, oh, rt[:, 7, :, :], ALU.add)
                tt(gate[:, :, :], score[:, :, :], oh, ALU.mult)
                st.run(dve.tensor_reduce(mx, gate[:, :, :], AX, ALU.add))
                st.run(dve.reciprocal(mx, mx))
                tt(gate[:, :, :], gate[:, :, :], mx.to_broadcast([P, 3, E_N]), ALU.mult)
                dve.sem_inc(sem(tag + "_gates"), 1)
                dve.wait_ge(sem(tag + "_gates_turned"), layer + 1)
                st.run(dve.tensor_copy(gateT[:, :], bank[3][0:16, 0:T]))
                dve.sem_inc(sem(tag + "_gates_copied"), 1)

            def experts(layer):
                tag = "moe"
                st.run(dve.tensor_scalar(xacc[:, :, :], xT[:, :, :], ALPHA, None, ALU.mult))
                if layer == 0:
                    dve.sem_inc(sem(tag + "_hidden"), 2)
                    dve.sem_inc(sem(tag + "_down_added"), 2)
                with dve.Fori(0, E_N // 2) as pair:
                    e = 2 * pair
                    for j in range(2):
                        sel = dve.tensor_copy(msel[0:16, j, :], ident[0:16, bass.ds(e + j, 1)].to_broadcast([16, P]))
                        sel.then_inc(sem(tag + "_sel"), 1)
                        dve.wait_ge(sem(tag + "_gbc_copied"), (E_N * layer + e) + j + 2)
                        for f in range(4):
                            k = 4 * j + f
                            dve.wait_ge(sem(tag + "_silu"), 4 * (E_N * layer + e) + k + 1)
                            h = mh[:, j, f, :]
                            dve.tensor_tensor(mg[:, f % 2, :], mg[:, f % 2, :], mgb[:, :], ALU.mult).then_inc(
                                sem(tag + "_weighted"), 1)
                            dve.wait_ge(sem(tag + "_weighted"), 4 * (E_N * layer + e) + k + 1)
                            dve.tensor_tensor(h, mg[:, f % 2, :], bank[2 + f % 2][:, 0:T], ALU.mult).then_inc(
                                sem(tag + "_hidden"), 1)
                        dve.wait_ge(sem(tag + "_down_added"), 8 * (E_N * layer + e) + 8 * j + 2)
                        for d in range(DC):
                            dve.wait_ge(sem(tag + "_down"), 8 * (E_N * layer + e) + 8 * j + d + 1)
                            dve.tensor_tensor(xacc[:, d, :], xacc[:, d, :], bank[4 + d % 2][:, 0:T], ALU.add).then_inc(
                                sem(tag + "_down_added"), 1)
                dve.wait_ge(sem(tag + "_down_added"), 2 + E_N * DC * (layer + 1))
                st.run(dve.tensor_copy(xT[:, :, :], xacc[:, :, :]))

            add_out("out0")
            layer_norm(0, V_LN1W, V_LN1B)
            stage_end(dve, 4)
            route(0)
            experts(0)
            layer_norm(1, V_LN2W, V_LN2B)
            stage_end(dve, 5)
            for m in range(1, 32, 2):
                dve.wait_ge(sem("in1_ready"), m + 1)
                dve.tensor_copy(A[:, m, :], bank[m % 4][:, 0:T]).then_inc(sem("in1_copied1"), 1)
            dve.wait_ge(sem("hg_tanh"), 1)
            for h in range(8):
                k = A[:, 32 + h, :]
                st.run(dve.tensor_scalar(k, A[:, 8 + h, :], -1.0, 1.0, ALU.mult, ALU.add))
                st.run(dve.tensor_scalar(k, k, lbc[:, 1, h:h + 1], None, ALU.mult))
            st.run(dve.tensor_scalar(A[:, 8:16, :], A[:, 32:40, :], -1.0, 1.0, ALU.mult, ALU.add))
            dve.sem_inc(sem("hg_forget"), 1)
            dve.wait_ge(sem("hg_log"), 1)
            dve.sem_inc(sem("hg_prepared"), 1)
            dve.sem_inc(sem("heads_area_free"), 1)
            dve.wait_ge(sem("dec_exps"), 2)
            gated_heads(1, 8, 128, lambda h: A[:, h, :], lambda h: A[:, 32 + h, :], None, lambda h: A[:, 8 + h, :],
                        lambda h, j: A[:, 16 + h, :], 1.0, V_HGN)
            stage_end(dve, 6)
            add_out("out1")
            layer_norm(2, V_LN1W + 8, V_LN1B + 8)
            stage_end(dve, 7)
            route(1)
            experts(1)
            layer_norm(3, V_LN2W + 8, V_LN2B + 8)
            stage_end(dve, 8)


_INS = ['x_prompt', 'x_sample', 'state_gla', 'state_ssd', 'state_conv', 'state_hgrn', 'w_in_ab', 'w_gk2', 'b_gk2',
        'gla_norm_w', 'conv_w', 'conv_b', 'dt_bias', 'a_log', 'd_skip', 'ssd_norm_w', 'w_out_ab', 'w_in_c',
        'lower_bounds', 'hg_norm_w', 'w_out_c', 'router_w', 'router_bias', 'w_gate', 'w_up', 'w_down', 'ln1_w',
        'ln1_b', 'ln2_w', 'ln2_b']
_OUTS = [(1, 256, 1024), (8, 1, 1024), (1, 1, 4, 128, 256), (1, 1, 16, 128, 64), (1, 1, 3, 1536), (1, 1, 8, 128, 128),
         (1, 8, 4, 128, 256), (1, 8, 16, 128, 64), (1, 8, 3, 1536), (1, 8, 8, 128, 128)]


def kernel(**inputs):
    import numpy as np
    import concourse.bacc as bacc
    from concourse.bass_utils import run_bass_kernel_spmd

    nc = bacc.Bacc("TRN2", target_bir_lowering=False, num_devices=1)
    arrays, ins, outs = {}, [], []
    for name in _INS:
        a = np.ascontiguousarray(inputs[name])
        arrays[f"in_{name}"] = a
        ins.append(nc.dram_tensor(f"in_{name}", a.shape, mybir.dt.from_np(a.dtype), kind="ExternalInput").ap())
    for i, shape in enumerate(_OUTS):
        outs.append(nc.dram_tensor(f"out_{i}", shape, F32, kind="ExternalOutput").ap())
    trunk_program(nc, ins, outs)
    r = run_bass_kernel_spmd(nc, [arrays], core_ids=[0])
    return tuple(r.results[0][f"out_{i}"] for i in range(len(_OUTS)))
```

```python
from contextlib import ExitStack

import concourse.bass as bass
from concourse import mybir

F32 = mybir.dt.float32
ALU = mybir.AluOpType
ACT = mybir.ActivationFunctionType
AX = mybir.AxisListType.X

P = 128
D = 1024
DC = D // P
NP = 256
NB = 8
T = NP + NB
DEPTH = 2
ALPHA = (2 * DEPTH) ** 0.25
EPS = 1e-5
C = 64
NC = NP // C
CS = 128
NCS = NP // CS
E_N, E_G, E_K, FF = 16, 4, 2, 512
SLOTS = 6
SLOT_W = 4096
HEAD_SCALE = 128 ** -0.5
SSD_HEADS = 16
CAP = 64
PCAP = CAP - NB
PLIM = PCAP
NORM_GLA, NORM_SSD, NORM_HG = 256, 512, 128
BIG = 1.0e30

V_BGK, V_GLAN, V_SSDN, V_LN1W, V_LN1B, V_LN2W, V_LN2B, V_HGN, V_LB = 0, 4, 6, 14, 30, 46, 62, 78, 79
V_N = 95

Q0, K0, VV0, G0, Z0, XS0, B0, C0 = 0, 4, 8, 16, 24, 32, 40, 42
AB_CHUNKS = 44


def trunk_program(nc, ins, outs):
    (x_prompt, x_sample, state_gla, state_ssd, state_conv, state_hgrn, w_in_ab, w_gk2, b_gk2, gla_norm_w, conv_w,
     conv_b, dt_bias, a_log, d_skip, ssd_norm_w, w_out_ab, w_in_c, lower_bounds, hg_norm_w, w_out_c, router_w,
     router_bias, w_gate, w_up, w_down, ln1_w, ln1_b, ln2_w, ln2_b) = ins
    (y_prompt, y_sample, gla_p, ssd_p, conv_p, hg_p, gla_s, ssd_s, conv_s, hg_s) = outs

    with ExitStack() as ctx:
        def sb(name, shape, dt=F32):
            return ctx.enter_context(nc.sbuf_tensor(name, shape, dt))

        sems = {}

        def sem(name):
            if name not in sems:
                sems[name] = ctx.enter_context(nc.semaphore(name))
            return sems[name]

        bank = [ctx.enter_context(nc.psum_tensor(f"bank{i}", [P, 512], F32)) for i in range(8)]

        ring = sb("ring", [P, SLOTS, SLOT_W])
        xT = sb("xT", [P, DC, T])
        A = sb("A", [P, AB_CHUNKS, T])
        W = sb("W", [P, 10880])
        ident = sb("ident", [P, P])
        ones = sb("ones", [P, P])
        causal = sb("causal", [P, P])
        restart = sb("restart", [P, NP])
        cols = sb("cols", [P, V_N])
        router = sb("router", [P, DC, E_N])
        rbias = sb("rbias", [P, E_N])
        small = sb("small", [16, 4])
        dskip = sb("dskip", [P, 8])
        lbc = sb("lbc", [P, 3, 8])
        score = sb("score", [P, 3, E_N])
        gate = sb("gate", [P, 3, E_N])
        rt = sb("rt", [P, 8, 3, E_N])
        idx16 = sb("idx16", [P, E_N])
        strict = sb("strict", [P, P])
        iota = sb("iota", [P, 64])
        over = sb("over", [P, 1], mybir.dt.int32)

        def area(base, *shape):
            n = 1
            for s in shape:
                n *= s
            assert base + n <= W.shape[1]
            v = W[:, base:base + n]
            if len(shape) == 2:
                v = v.rearrange("p (a b) -> p a b", a=shape[0])
            if len(shape) == 3:
                v = v.rearrange("p (a b c) -> p a b c", a=shape[0], b=shape[1])
            return v

        Aflat = A[:, :, :].rearrange("p a t -> p (a t)")

        fills = []
        ab_cols = [g * 512 for g in range(6)] + [3088 + g * 512 for g in range(5)]
        for c0 in ab_cols:
            fills.append((w_in_ab[0, :, c0:c0 + 512].rearrange("(c p) n -> p c n", p=P), 8))
        for g in range(4):
            fills.append((w_out_ab[0, :, g * 256:g * 256 + 256].rearrange("(c p) n -> p c n", p=P), 16))
        AB_IN0, AB_OUT0, MOE0 = 0, 11, 15
        MOE_SLOTS = 3 * E_N
        C_IN0 = MOE0 + MOE_SLOTS
        C_OUT0 = C_IN0 + 8
        MOE1 = C_OUT0 + 2
        TOTAL = MOE1 + MOE_SLOTS

        def slot(n, k):
            return ring[:, n % SLOTS, :].rearrange("p (c n) -> p c n", c=k)

        def expert_views(layer, e):
            return [
                (w_gate[layer, e].rearrange("o (c p) n -> p (o c) n", p=P), 8),
                (w_up[layer, e].rearrange("o (c p) n -> p (o c) n", p=P), 8),
                (w_down[layer, e].rearrange("o (c p) n -> p (o c) n", p=P), 4),
            ]

        block = ctx.enter_context(nc.Block())

        class Steps:

            def __init__(self, eng, name):
                self.eng, self.sem, self.n = eng, sem(name), 0

            def add(self, ins):
                ins.then_inc(self.sem, 1)
                self.n += 1

            def settle(self):
                self.eng.wait_ge(self.sem, self.n)

            def run(self, ins):
                self.add(ins)
                self.settle()

        def stage_end(eng, k):
            eng.sem_inc(sem("stage_ended"), 1)
            eng.wait_ge(sem("stage_ended"), 4 * k)

        @block.sync
        def _(sp):
            def last_reader(n):
                if n < AB_OUT0:
                    return "in0_ready", 4 * (n + 1)
                if n < MOE0:
                    return "out0_ready", 2 * (n - AB_OUT0 + 1)
                if n < C_IN0:
                    e, i = divmod(n - MOE0, 3)
                    return ("moe_gu" if i < 2 else "moe_down"), e + 1
                if n < C_OUT0:
                    return "in1_ready", 4 * (n - C_IN0 + 1)
                return "out1_ready", 4 * (n - C_OUT0 + 1)

            def fill(n, src, k):
                if n >= SLOTS:
                    name, value = last_reader(n - SLOTS)
                    sp.wait_ge(sem(name), value)
                sp.dma_start(slot(n, k), src).then_inc(sem(f"slot_filled{n % SLOTS}"), 16)

            def fill_experts(n0, layer):
                for e in range(2):
                    for i, (src, k) in enumerate(expert_views(layer, bass.ds(e, 1))):
                        fill(n0 + 3 * e + i, src, k)
                with sp.Fori(1, E_N // 2) as pair:
                    e = 2 * pair
                    for j in range(2):
                        for i, (src, k) in enumerate(expert_views(layer, bass.ds(e + j, 1))):
                            n = n0 + 3 * j + i
                            if i < 2:
                                sp.wait_ge(sem("moe_gu"), E_N * layer + e + j - 1)
                            else:
                                sp.wait_ge(sem("moe_down"), E_N * layer + e + j - 1)
                            sp.dma_start(slot(n, k), src).then_inc(sem(f"slot_filled{n % SLOTS}"), 16)

            def fill_over(layer):
                sp.wait_ge(sem("over_known"), layer + 1)
                flag = sp.value_load(over[0:1, 0:1], min_val=0, max_val=1)
                with sp.If(flag > 0):
                    sp.wait_ge(sem("moe_gu"), E_N * (layer + 1))
                    sp.wait_ge(sem("moe_down"), E_N * (layer + 1))
                    with sp.Fori(0, E_N) as e:
                        sp.wait_ge(sem("over_read"), E_N * layer + e + 1)
                        for i, (src, k) in enumerate(expert_views(layer, bass.ds(e, 1))):
                            sp.dma_start(slot(i, k), src).then_inc(sem(f"over_filled{i}"), 16)
                    sp.wait_ge(sem("over_read"), E_N * (layer + 1) + 1)
                if layer == 0:
                    with sp.If(flag < 1):
                        for i in range(3):
                            sp.sem_inc(sem(f"over_filled{i}"), 16 * E_N)

            for n, (src, k) in enumerate(fills):
                fill(n, src, k)
            fill_experts(MOE0, 0)
            fill_over(0)
            for g in range(8):
                fill(C_IN0 + g, w_in_c[0, :, g * 512:g * 512 + 512].rearrange("(c p) n -> p c n", p=P), 8)
            for g in range(2):
                fill(C_OUT0 + g, w_out_c[0, :, g * 512:g * 512 + 512].rearrange("(c p) n -> p c n", p=P), 8)
            fill_experts(MOE1, 1)
            fill_over(1)

        xrows = area(0, 3, D)
        vrows = area(3072, P)
        crows = area(3200, 12 * P)
        wsmall = area(4736, 8, 32)
        convout = area(4992, 12 * P)
        cacc = area(6528, 2, T)
        convc = area(7056, 12, 29)
        gka = area(7564, 4, T)
        gkz = area(8620, 4, T)
        wgk = area(9676, 512)[0:16, :]
        lrT = area(10188, T)[0:16, :]
        gkg = sb("gkg", [P, 4, T])
        decx = sb("decx", [P, 8, NB])
        XG = Aflat[:, 0:10240].rearrange("p (e c s) -> p e c s", e=20, c=DC)
        SLOT1 = Aflat[:, 8192:10240].rearrange("p (b e s) -> p b e s", b=2, e=E_N)
        xg = Aflat[:, 10240:11264].rearrange("p (j c s) -> p j c s", j=2, c=DC)
        xtm = area(0, 2, D)
        Y = area(0, D)
        WS = area(2048, 2, E_N, CAP)
        WS2 = area(4096, E_N, CAP)
        PT = area(5120, 8, T)
        xacc = area(7232, DC, T)
        hT = area(9344, 2, 4 * CAP)
        sg = area(9856, 2, 4 * CAP)
        oh_ = Aflat[:, 0:4 * NP].rearrange("p (f t) -> p f t", f=4)
        og = Aflat[:, 1024:1024 + 2 * NP].rearrange("p (f t) -> p f t", f=2)
        ogb = Aflat[:, 1536:1536 + NP]
        osel = Aflat[0:16, 1792:1792 + P]
        ogT = Aflat[0:16, 2048:2048 + NP]
        lnsq = A[:, 0:8, :]
        lnm = area(0, T)
        lnr = area(512, T)

        def head_area(h):
            b = 3072 * (h % 2)
            names = {}
            for i, n in enumerate(["G", "E1", "E2", "EL", "EG", "QD"]):
                names[n] = area(b + 256 * i, NP)
            names["ktm"] = area(b + 1536, NC, P)
            names["vtm"] = area(b + 2048, NC, 256)
            return names
        SC = area(6144, NP)
        ST = area(6400, NC, 256)
        KDEC = area(7424, 128)
        KMASK = area(7552, 4, P)
        VDEC = area(8064, 256)
        DEC = area(8320, 8)
        QS = area(8328, 8)
        DST = area(8600, 4, 256)
        SQ = area(9624, 2, T)
        s_E = W[:, 0:2048].rearrange("p (c h t) -> p c h t", c=NCS, h=8)
        s_xdt = area(2048, NCS, 512)
        s_xw = area(3072, NCS, 512)
        s_btm = area(4096, NCS, P)
        s_g0 = area(4352, NCS, P)
        s_S = area(4608, NCS, 512)
        s_eg = area(5632, 512)
        s_yi = area(6144, 512)
        s_xdec = area(6656, 512)
        s_bdec = area(7168, P)
        s_bmask = area(7296, NB, P)
        s_dst = area(8320, 2, 512)
        s_sq = area(9344, 4, T)
        s_tm = area(10400, 4, 16)
        s_w = area(10464, 2, 16)
        s_el = area(10496, 2, 16)
        s_dd = area(10528, 16)
        s_egd = area(10544, NB, 16)
        dtT = sb("dtT", [16, 3, T])

        @block.gpsimd
        def _(pool):
            st = Steps(pool, "pool_steps")
            st.add(pool.memset(ident[:, :], 0.0))
            st.add(pool.memset(ones[:, :], 1.0))
            st.add(pool.memset(causal[:, :], 1.0))
            st.add(pool.memset(strict[:, :], 1.0))
            st.add(pool.memset(restart[:, :], 1.0))
            st.add(pool.iota(rt[:, 0, 0, :].bitcast(mybir.dt.int32), pattern=[[-1, E_N]], base=E_N, channel_multiplier=0))
            st.add(pool.iota(convout[:, 0:64].bitcast(mybir.dt.int32), pattern=[[1, 64]], base=0, channel_multiplier=0))
            st.settle()
            st.add(pool.tensor_copy(iota[:, :], convout[:, 0:64].bitcast(mybir.dt.int32)))
            st.add(pool.affine_select(out=ident[:, :], in_=ident[:, :], compare_op=ALU.not_equal, fill=1.0, base=0,
                                      pattern=[[-1, P]], channel_multiplier=1))
            st.add(pool.affine_select(out=causal[:, :], in_=causal[:, :], compare_op=ALU.is_ge, fill=0.0, base=0,
                                      pattern=[[1, P]], channel_multiplier=-1))
            st.add(pool.affine_select(out=strict[:, :], in_=strict[:, :], compare_op=ALU.is_ge, fill=0.0, base=-1,
                                      pattern=[[1, P]], channel_multiplier=-1))
            st.add(pool.memset(restart[:, :].rearrange("p (c t) -> p c t", t=C)[:, :, 0:1], 0.0))
            st.add(pool.tensor_copy(idx16[:, :], rt[:, 0, 0, :].bitcast(mybir.dt.int32)))
            st.settle()
            pool.sem_inc(sem("consts_made"), 1)

            def gated_states(layer, nh, dv, src, dst_p, dst_s):
                tag = "heads"
                H0 = 4 * layer
                for h in range(nh):
                    for q in range(2):
                        n = 2 * h + q
                        if n == 0:
                            pool.wait_ge(sem(tag + "_area_free"), layer + 1)
                        buf = DST[:, :, 0:dv]
                        if n >= 1:
                            pool.wait_ge(sem(tag + "_state_stored"), 16 * (2 * H0 + n))
                        pool.dma_start(buf, src[0, 4 * q:4 * q + 4, h].rearrange("b k v -> k b v")).then_inc(
                            sem(tag + "_state_loaded"), 16)
                        pool.wait_ge(sem(tag + "_state_used"), (2 * H0 + n) + 1)
                        pool.dma_start(dst_s[0, 4 * q:4 * q + 4, h].rearrange("b k v -> k b v"), buf).then_inc(
                            sem(tag + "_state_stored"), 16)
                    pool.wait_ge(sem(tag + "_states_ready"), (H0 + h) + 1)
                    pool.dma_start(dst_p[0, 0, h], ST[:, NC - 1, 0:dv]).then_inc(sem(tag + "_prompt_state_stored"), 16)
                pool.wait_ge(sem(tag + "_state_stored"), 16 * 2 * (H0 + nh))
                pool.wait_ge(sem(tag + "_prompt_state_stored"), 16 * (H0 + nh))

            pool.wait_ge(sem("convout_ready"), 3)
            pool.dma_start(conv_p[0, 0], convout[5:8, :]).then_inc(sem("conv_stored"), 16)
            pool.dma_start(conv_s[0, :, 2], convout[8:16, :]).then_inc(sem("conv_stored"), 16)
            pool.dma_start(conv_s[0, :, 0:2], state_conv[0, :, 1:3]).then_inc(sem("conv_stored"), 16)
            pool.wait_ge(sem("conv_stored"), 48)
            stage_end(pool, 1)
            gated_states(0, 4, 256, state_gla, gla_p, gla_s)
            stage_end(pool, 2)
            for g in range(2):
                for b in range(NB):
                    n = NB * g + b
                    buf = s_dst[:, n % 2, :].rearrange("p (h v) -> p h v", h=8)
                    if n >= 2:
                        pool.wait_ge(sem(f"ssd_stored{n % 2}"), 16 * (n // 2))
                    pool.dma_start(buf, state_ssd[0, b, 8 * g:8 * g + 8].rearrange("h n v -> n h v")).then_inc(
                        sem(f"ssd_loaded{n % 2}"), 16)
                    if n >= 1:
                        m = n - 1
                        pool.wait_ge(sem("ssd_state_used"), m + 1)
                        pool.dma_start(ssd_s[0, m % NB, 8 * (m // NB):8 * (m // NB) + 8].rearrange("h n v -> n h v"),
                                       s_dst[:, m % 2, :].rearrange("p (h v) -> p h v", h=8)).then_inc(
                            sem(f"ssd_stored{m % 2}"), 16)
                if g == 0:
                    pool.wait_ge(sem("ssd_prompt_state"), 1)
                    pool.dma_start(ssd_p[0, 0, 0:8].rearrange("h n v -> n h v"),
                                   s_S[:, 1, :].rearrange("p (h v) -> p h v", h=8)).then_inc(sem("ssd_p_stored"), 16)
            m = 2 * NB - 1
            pool.wait_ge(sem("ssd_state_used"), m + 1)
            pool.dma_start(ssd_s[0, NB - 1, 8:16].rearrange("h n v -> n h v"),
                           s_dst[:, m % 2, :].rearrange("p (h v) -> p h v", h=8)).then_inc(sem(f"ssd_stored{m % 2}"), 16)
            pool.wait_ge(sem("ssd_prompt_state"), 2)
            pool.dma_start(ssd_p[0, 0, 8:16].rearrange("h n v -> n h v"),
                           s_S[:, 1, :].rearrange("p (h v) -> p h v", h=8)).then_inc(sem("ssd_p_stored"), 16)
            for i in range(2):
                pool.wait_ge(sem(f"ssd_stored{i}"), 16 * NB)
            pool.wait_ge(sem("ssd_p_stored"), 32)
            for k in range(3, 6):
                stage_end(pool, k)
            gated_states(1, 8, 128, state_hgrn, hg_p, hg_s)
            for k in range(6, 9):
                stage_end(pool, k)

        @block.tensor
        def _(pe):
            def slot_ready(n, base=None):
                pe.wait_ge(sem(f"slot_filled{n % SLOTS}"), 16 * (n // SLOTS + 1))

            pe.sem_inc(sem("over_read"), 1)
            pe.wait_ge(sem("consts_made"), 1)
            pe.wait_ge(sem("x_loaded"), 32)
            for c in range(DC):
                for b, n in enumerate((P, P, NB)):
                    tr = pe.transpose(bank[c][:, b * P:b * P + n], xrows[0:n, b, c * P:(c + 1) * P], ident[0:n, 0:n])
                tr.then_inc(sem("xT_turned"), 1)
            pe.wait_ge(sem("vectors_loaded"), 16 * 21)
            pe.wait_ge(sem("xT_copied"), 8)
            pe.transpose(bank[0][:, 0:V_N], vrows[0:V_N, :], ident[0:V_N, 0:V_N]).then_inc(sem("vectors_turned"), 1)
            for m in range(12):
                tr = pe.transpose(bank[1][:, m * 29:(m + 1) * 29], crows[0:29, m * P:(m + 1) * P], ident[0:29, 0:29])
            tr.then_inc(sem("vectors_turned"), 1)
            pe.wait_ge(sem("xT_copied"), 8)
            pe.wait_ge(sem("vectors_copied"), 2)
            m = 0
            for g in range(11):
                slot_ready(AB_IN0 + g)
                w = slot(AB_IN0 + g, 8)
                for i in range(4):
                    if m >= 4:
                        pe.wait_ge(sem(f"in0_copied{m % 2}"), (m - 4) // 2 + 1)
                    for c in range(DC):
                        mm = pe.matmul(bank[m % 4][:, 0:T], w[:, c, i * P:(i + 1) * P], xT[:, c, :],
                                       start=(c == 0), stop=(c == DC - 1))
                    mm.then_inc(sem("in0_ready"), 1)
                    m += 1
            for i in range(2):
                for c in range(DC):
                    mm = pe.matmul(bank[4 + i][0:16, 0:T], wsmall[:, c, 16 * i:16 * i + 16], xT[:, c, :],
                                   start=(c == 0), stop=(c == DC - 1))
                mm.then_inc(sem("small_ready"), 1)
            pe.wait_ge(sem("in0_copied0"), 22)
            pe.wait_ge(sem("in0_copied1"), 22)
            pe.wait_ge(sem("small_copied"), 2)
            for m in range(12):
                tr = pe.transpose(bank[5 + m // 4][0:16, (m % 4) * P:(m % 4 + 1) * P], A[:, XS0 + m, NP - 8:T],
                                  ident[:, :])
                if m % 4 == 3:
                    tr.then_inc(sem("conv_turned"), 1)
            for h in range(4):
                mm = pe.matmul(bank[h][:, 0:T], wgk[:, h * P:(h + 1) * P], lrT[:, :], start=True, stop=True)
                mm.then_inc(sem("gk_ready"), 1)
            stage_end(pe, 1)

            def gated_heads(layer, nh, dv, qa, ka, va):
                tag = "heads_"
                H0 = 4 * layer
                J = dv // P
                for h in range(nh):
                    hb = head_area(h)
                    if h >= 1:
                        pe.wait_ge(sem(tag + "normed"), (H0 + h))
                    per = 512 // dv
                    for c in range(NC):
                        for j in range(J):
                            tr = pe.transpose(bank[c // per][0:C, (c % per) * dv + j * P:(c % per) * dv + (j + 1) * P],
                                              va(h, j)[:, c * C:(c + 1) * C], ident[:, :])
                    pe.transpose(bank[2][0:NB, 0:P], ka(h)[:, NP:T], ident[:, :])
                    for j in range(J):
                        tr = pe.transpose(bank[2][0:NB, (j + 1) * P:(j + 2) * P], va(h, j)[:, NP:T], ident[:, :])
                    tr.then_inc(sem(tag + "v_turned"), 1)
                    pe.wait_ge(sem(tag + "prepared"), (H0 + h) + 1)
                    for c in range(NC):
                        s = slice(c * C, (c + 1) * C)
                        mm = pe.matmul(bank[4][0:C, s], hb["E2"][:, s], hb["E1"][:, s], start=True, stop=True)
                    mm.then_inc(sem(tag + "scores_ready"), 1)
                    for c in range(NC):
                        s = slice(c * C, (c + 1) * C)
                        tr = pe.transpose(bank[3][0:C, c * P:(c + 1) * P], hb["EL"][:, s], ident[:, :])
                    tr.then_inc(sem(tag + "k_turned"), 1)
                    pe.wait_ge(sem(tag + "kv_copied"), 3 * (H0 + h) + 3)
                    for c in range(NC):
                        mm = pe.matmul(bank[c // per][:, (c % per) * dv:(c % per + 1) * dv], hb["ktm"][0:C, c, :],
                                       hb["vtm"][0:C, c, 0:dv], start=True, stop=True)
                    mm.then_inc(sem(tag + "updates_ready"), 1)
                    for b in range(NB):
                        if b % 4 == 0:
                            pe.wait_ge(sem(tag + "kmask_ready"), 2 * (H0 + h) + b // 4 + 1)
                        if b >= 2:
                            pe.wait_ge(sem(tag + "dec_updated"), NB * (H0 + h) + b - 1)
                        pe.matmul(bank[6 + b % 2][:, 0:dv], KMASK[0:NB, b % 4, :], VDEC[0:NB, 0:dv], start=True,
                                  stop=True).then_inc(sem(tag + "dec_update_ready"), 1)
                        if b % 4 == 3:
                            pe.wait_ge(sem(tag + "dec_updated"), NB * (H0 + h) + b + 1)
                            pe.wait_ge(sem(tag + "scores_masked"), (H0 + h) + 1)
                            for bb in range(b - 3, b + 1):
                                for j in range(J):
                                    mm = pe.matmul(bank[4][:, 256 + j * NB + bb:257 + j * NB + bb],
                                                   DST[:, bb % 4, j * P:(j + 1) * P], QS[:, bb:bb + 1],
                                                   start=True, stop=True)
                            mm.then_inc(sem(tag + "state_used"), 1)
                    pe.wait_ge(sem(tag + "states_ready"), (H0 + h) + 1)
                    for j in range(J):
                        for c in range(NC):
                            s = slice(c * C, (c + 1) * C)
                            mm = pe.matmul(bank[5][:, j * NP + c * C:j * NP + (c + 1) * C],
                                           hb["vtm"][0:C, c, j * P:(j + 1) * P], SC[0:C, s], start=True, stop=(c == 0))
                            if c > 0:
                                mm = pe.matmul(bank[5][:, j * NP + c * C:j * NP + (c + 1) * C],
                                               ST[:, c - 1, j * P:(j + 1) * P], hb["QD"][:, s], start=False, stop=True)
                    mm.then_inc(sem(tag + "out_ready"), 1)
                    pe.wait_ge(sem(tag + "squared"), (H0 + h) + 1)
                    for j in range(J):
                        mm = pe.matmul(bank[3][:, 0:T], ones[:, :], SQ[:, j, :], start=(j == 0), stop=(j == J - 1))
                    mm.then_inc(sem(tag + "square_sums"), 1)

            gated_heads(0, 4, 256, lambda h: A[:, Q0 + h, :], lambda h: A[:, K0 + h, :],
                        lambda h, j: A[:, VV0 + 2 * h + j, :])
            stage_end(pe, 2)

            pe.wait_ge(sem("dt_ready"), 1)
            for c in range(NCS):
                s = slice(c * CS, (c + 1) * CS)
                pe.transpose(bank[0][:, 16 * c:16 * c + 16], dtT[:, 1, s], ident[0:16, 0:16])
                pe.transpose(bank[0][:, 32 + 16 * c:48 + 16 * c], dtT[:, 0, s], ident[0:16, 0:16])
            pe.transpose(bank[0][0:NB, 64:80], dtT[:, 0, NP:T], ident[0:16, 0:16])
            for c in range(NCS):
                pe.matmul(bank[0][:, 80 + 16 * c:96 + 16 * c],
                          dtT[:, 1, (c + 1) * CS - 1:(c + 1) * CS].to_broadcast([16, P]), ident[0:16, 0:16],
                          start=True, stop=True)
            for b in range(NB):
                mm = pe.matmul(bank[0][:, 112 + 16 * b:128 + 16 * b],
                               dtT[:, 2, NP + b:NP + b + 1].to_broadcast([16, P]), ident[0:16, 0:16],
                               start=True, stop=True)
            mm.then_inc(sem("tm_ready"), 1)
            pe.wait_ge(sem("tm_copied"), 1)
            for g in range(2):
                BT, CT = A[:, B0 + g, :], A[:, C0 + g, :]
                if g == 1:
                    pe.wait_ge(sem("ssd_normed"), 1)
                for c in range(NCS):
                    s = slice(c * CS, (c + 1) * CS)
                    pe.transpose(bank[0][:, c * P:(c + 1) * P], BT[:, s], ident[:, :])
                pe.transpose(bank[0][0:NB, 256:384], BT[:, NP:T], ident[:, :])
                for c in range(NCS):
                    s = slice(c * CS, (c + 1) * CS)
                    for j in range(4):
                        pe.transpose(bank[1 + c][:, j * P:(j + 1) * P], A[:, XS0 + 4 * g + j, s], ident[:, :])
                for j in range(4):
                    pe.transpose(bank[3][0:NB, j * P:(j + 1) * P], A[:, XS0 + 4 * g + j, NP:T], ident[:, :])
                for c in range(NCS):
                    s = slice(c * CS, (c + 1) * CS)
                    mm = pe.matmul(bank[4][:, c * P:(c + 1) * P], BT[:, s], CT[:, s], start=True, stop=True)
                mm.then_inc(sem("ssd_turned"), 1)
                for pr in range(4):
                    if pr >= 2:
                        pe.wait_ge(sem("ssd_diffs"), 4 * g + pr - 1)
                    for i in range(2):
                        h = 8 * g + 2 * pr + i
                        mm = pe.matmul(bank[5 + pr % 2][:, i * NP:(i + 1) * NP],
                                       ident[0:16, h:h + 1].to_broadcast([16, P]), dtT[:, 1, 0:NP],
                                       start=True, stop=True)
                    mm.then_inc(sem("gbc_ready"), 1)
                pe.wait_ge(sem("ssd_tm_copied"), g + 1)
                for c in range(NCS):
                    if c == 1:
                        pe.wait_ge(sem("ssd_state0"), g + 1)
                    pe.matmul(bank[7][:, :], s_btm[:, c, :], s_xw[:, c, :], start=True, stop=True).then_inc(
                        sem("ssd_update_ready"), 1)
                pe.wait_ge(sem("ssd_btm_copied"), g + 1)
                for j in range(4):
                    h = 8 * g + 2 * j
                    for i in range(2):
                        mm = pe.matmul(bank[0][64 * i:64 * i + 64, j * P:(j + 1) * P],
                                       ident[0:16, h + i:h + i + 1].to_broadcast([16, 64]), dtT[:, 2, CS:NP],
                                       start=True, stop=True)
                mm.then_inc(sem("eg_ready"), 1)
                pe.wait_ge(sem("ssd_scores"), 2 * g + 2)
                for j in range(4):
                    for c in range(NCS):
                        for i in range(2):
                            hh = 2 * j + i
                            mm = pe.matmul(bank[1 + j // 2][64 * i:64 * i + 64,
                                                            (j % 2) * NP + c * CS:(j % 2) * NP + (c + 1) * CS],
                                           s_xdt[:, c, hh * 64:(hh + 1) * 64], s_E[:, c, hh, :], start=True, stop=True)
                mm.then_inc(sem("ssd_intra"), 1)
                for j in range(4):
                    mm = pe.matmul(bank[3][:, j * P:(j + 1) * P], s_S[:, 0, j * P:(j + 1) * P], CT[:, CS:NP],
                                   start=True, stop=True)
                mm.then_inc(sem("ssd_inter"), 1)
                for b in range(NB):
                    n = NB * g + b
                    if b == 0:
                        pe.wait_ge(sem("ssd_diffs"), 4 * g + 4)
                    if b >= 2:
                        pe.wait_ge(sem("ssd_dec_updated"), n - 1)
                    else:
                        pe.wait_ge(sem("bmask_ready"), g + 1)
                    pe.matmul(bank[5 + b % 2][:, :], s_bmask[0:NB, b, :], s_xdec[0:NB, :], start=True, stop=True
                              ).then_inc(sem("ssd_dec_ready"), 1)
                    pe.wait_ge(sem("ssd_dec_updated"), n + 1)
                    for j in range(4):
                        mm = pe.matmul(bank[4][:, 256 + j * NB + b:257 + j * NB + b], s_dst[:, n % 2, j * P:(j + 1) * P],
                                       CT[:, NP + b:NP + b + 1], start=True, stop=True)
                    mm.then_inc(sem("ssd_state_used"), 1)
                pe.wait_ge(sem("ssd_squared"), g + 1)
                for j in range(4):
                    mm = pe.matmul(bank[7][:, 0:T], ones[:, :], s_sq[:, j, :], start=(j == 0), stop=(j == 3))
                mm.then_inc(sem("ssd_square_sums"), 1)
            stage_end(pe, 3)

            def out_project(n0, groups, kc, srcs, tag):
                m = 0
                per = DC // groups
                for g in range(groups):
                    slot_ready(n0 + g)
                    w = slot(n0 + g, kc)
                    for i in range(per):
                        for c in range(kc):
                            mm = pe.matmul(bank[m][:, 0:T], w[:, c, i * P:(i + 1) * P], srcs(c),
                                           start=(c == 0), stop=(c == kc - 1))
                        mm.then_inc(sem(tag + "_ready"), 1)
                        m += 1

            def norm_sums(k, src):
                pe.wait_ge(sem("norm_residual"), k + 1)
                for c in range(DC):
                    mm = pe.matmul(bank[0][:, 0:T], ones[:, :], src[:, c, :], start=(c == 0), stop=(c == DC - 1))
                mm.then_inc(sem("norm_sum"), 1)
                pe.wait_ge(sem("norm_squares"), k + 1)
                for c in range(DC):
                    mm = pe.matmul(bank[1][:, 0:T], ones[:, :], lnsq[:, c, :], start=(c == 0), stop=(c == DC - 1))
                mm.then_inc(sem("norm_sum"), 1)

            def experts(n0, layer):
                E0 = E_N * layer
                for b, n in enumerate((P, P, NB)):
                    for c in range(DC):
                        mm = pe.matmul(bank[2][0:n, 16 * b:16 * b + 16], xT[:, c, b * P:b * P + n], router[:, c, :],
                                       start=(c == 0), stop=(c == DC - 1))
                mm.then_inc(sem("moe_logits"), 1)
                for b in range(2):
                    for c in range(DC):
                        tr = pe.transpose(bank[4 + 2 * b + c // 4][:, (c % 4) * P:(c % 4 + 1) * P],
                                          xT[:, c, b * P:(b + 1) * P], ident[:, :])
                        if c % 4 == 3:
                            tr.then_inc(sem("xtm_turned"), 1)
                pe.wait_ge(sem("moe_chosen"), layer + 1)
                chosen = rt[:, 3, :, :]
                pe.matmul(bank[3][:, 0:16], strict[:, :], chosen[:, 0, :], start=True, stop=True)
                for i, last in enumerate((strict[:, :], ones[:, :])):
                    pe.matmul(bank[3][:, 16 + 16 * i:32 + 16 * i], ones[:, :], chosen[:, 0, :], start=True, stop=False)
                    mm = pe.matmul(bank[3][:, 16 + 16 * i:32 + 16 * i], last, chosen[:, 1, :], start=False, stop=True)
                mm.then_inc(sem("moe_places"), 1)
                pe.wait_ge(sem("moe_slots"), layer + 1)
                pe.wait_ge(sem("xtm_copied"), 4 * (layer + 1))
                for i in range(2 * DC):
                    half, c = divmod(i, DC)
                    if i >= 4:
                        pe.wait_ge(sem(f"gathered{i % 2}"), DC * layer + (i - 4) // 2 + 1)
                    for b in range(2):
                        mm = pe.matmul(bank[i % 4][:, 0:8 * PCAP], xtm[:, b, c * P:(c + 1) * P],
                                       SLOT1[:, b, 8 * half:8 * half + 8, 0:PCAP], start=(b == 0), stop=(b == 1))
                    mm.then_inc(sem("gather_ready"), 1)
                pe.wait_ge(sem("moe_weighted"), layer + 1)
                for q in range(8):
                    if q >= 4:
                        pe.wait_ge(sem("pt_copied"), 8 * layer + q - 3)
                    for b in range(2):
                        pe.transpose(bank[4 + q % 4][:, b * P:(b + 1) * P],
                                     WS[:, b, 2 * q:2 * q + 2, :].rearrange("p e s -> p (e s)"), ident[:, :])
                    pe.transpose(bank[4 + q % 4][:, NP:T], WS2[0:NB, 2 * q:2 * q + 2, :].rearrange("p e s -> p (e s)"),
                                 ident[0:NB, 0:NB]).then_inc(sem("pt_turned"), 1)
                pe.wait_ge(sem("pt_copied"), 8 * (layer + 1))
                for i in range(2):
                    pe.wait_ge(sem(f"gathered{i}"), DC * (layer + 1))
                with pe.Fori(0, E_N // 2) as pair:
                    e = 2 * pair + E0
                    for j in range(2):
                        n = n0 + 3 * j
                        pe.wait_ge(sem("xg_copied"), 2 * pair + (18 * layer + j + 1))
                        pe.wait_ge(sem("moe_hidden"), e + j + 1)
                        for i in range(2):
                            pe.wait_ge(sem(f"slot_filled{(n + i) % SLOTS}"), 16 * pair + 16 * ((n + i) // SLOTS + 1))
                            w = slot(n + i, 8)
                            for f in range(4):
                                for c in range(DC):
                                    mm = pe.matmul(bank[2 * i + j][:, f * CAP:(f + 1) * CAP], w[:, c, f * P:(f + 1) * P],
                                                   xg[:, j, c, :], start=(c == 0), stop=(c == DC - 1))
                        mm.then_inc(sem("moe_gu"), 1)
                        if j == 0:
                            for i in range(2):
                                pe.wait_ge(sem(f"y_copied{i}"), pair + 8 * layer + 1)
                        pe.wait_ge(sem(f"slot_filled{(n + 2) % SLOTS}"), 16 * pair + 16 * ((n + 2) // SLOTS + 1))
                        pe.wait_ge(sem("moe_hidden"), e + j + 3)
                        w = slot(n + 2, 4)
                        for i in range(2):
                            for f in range(4):
                                mm = pe.matmul(bank[4 + i][64 * j:64 * j + 64, :], hT[:, j, f * CAP:(f + 1) * CAP],
                                               w[:, f, 512 * i:512 * (i + 1)], start=(f == 0), stop=(f == 3))
                        mm.then_inc(sem("moe_down"), 1)
                    for i in range(2):
                        pe.wait_ge(sem(f"y_copied{i}"), pair + 8 * layer + 2)
                    for c in range(DC):
                        pe.wait_ge(sem("moe_added"), DC * pair + (64 * layer + c + 1))
                        pe.matmul(bank[6 + c % 2][:, 0:T], Y[:, c * P:(c + 1) * P],
                                  PT[:, bass.ds(pair, 1), :].rearrange("p o t -> p (o t)"),
                                  start=True, stop=True).then_inc(sem("moe_back"), 1)
                pe.wait_ge(sem("over_known"), layer + 1)
                flag = pe.value_load(over[0:1, 0:1], min_val=0, max_val=1)
                with pe.If(flag > 0):
                    pe.wait_ge(sem("over_gates"), layer + 1)
                    for b in range(2):
                        tr = pe.transpose(bank[7][0:16, b * P:(b + 1) * P], rt[:, 6, b, :], ident[:, :])
                    tr.then_inc(sem("over_turned"), 1)
                    with pe.Fori(0, E_N) as e:
                        x = E0 + e
                        pe.wait_ge(sem("over_sel"), x + 1)
                        pe.wait_ge(sem("over_gates_copied"), layer + 1)
                        pe.matmul(bank[6][:, 0:NP], osel, ogT, start=True, stop=True).then_inc(sem("over_spread"), 1)
                        for i in range(2):
                            pe.wait_ge(sem(f"over_filled{i}"), 16 * x + 16)
                        for f in range(4):
                            pe.wait_ge(sem("over_hidden"), 4 * x + f + 1)
                            for i in range(2):
                                for c in range(DC):
                                    mm = pe.matmul(bank[2 * i + f % 2][:, 0:NP], slot(i, 8)[:, c, f * P:(f + 1) * P],
                                                   xT[:, c, 0:NP], start=(c == 0), stop=(c == DC - 1))
                            mm.then_inc(sem("over_gu"), 1)
                        pe.wait_ge(sem("over_filled2"), 16 * x + 16)
                        pe.wait_ge(sem("over_hidden"), 4 * x + 6)
                        for d in range(DC):
                            pe.wait_ge(sem("over_added"), DC * x + d + 1)
                            for f in range(4):
                                mm = pe.matmul(bank[4 + d % 2][:, 0:NP], slot(2, 4)[:, f, d * P:(d + 1) * P],
                                               oh_[:, f, :], start=(f == 0), stop=(f == 3))
                            mm.then_inc(sem("over_down"), 1)
                        pe.wait_ge(sem("over_down"), DC * x + DC)
                        pe.sem_inc(sem("over_read"), 1)
                if layer == 0:
                    with pe.If(flag < 1):
                        for name, k in (("turned", 1), ("spread", E_N), ("gu", 4 * E_N), ("down", DC * E_N), ("read", E_N)):
                            pe.sem_inc(sem("over_" + name), k)

            def out_chunks(c):
                return A[:, (VV0 + c) if c < 8 else (XS0 + c - 8), :]

            out_project(AB_OUT0, 4, 16, out_chunks, "out0")
            norm_sums(0, xT)
            stage_end(pe, 4)
            experts(MOE0, 0)
            norm_sums(1, xacc)
            stage_end(pe, 5)
            m = 0
            for g in range(8):
                slot_ready(C_IN0 + g)
                w = slot(C_IN0 + g, 8)
                for i in range(4):
                    if m >= 4:
                        pe.wait_ge(sem(f"in1_copied{m % 2}"), (m - 4) // 2 + 1)
                    for c in range(DC):
                        mm = pe.matmul(bank[m % 4][:, 0:T], w[:, c, i * P:(i + 1) * P], xT[:, c, :],
                                       start=(c == 0), stop=(c == DC - 1))
                    mm.then_inc(sem("in1_ready"), 1)
                    m += 1
            pe.wait_ge(sem("hg_prepared"), 1)
            pe.wait_ge(sem("in1_copied0"), 16)
            pe.wait_ge(sem("in1_copied1"), 16)
            gated_heads(1, 8, 128, lambda h: A[:, h, :], lambda h: A[:, 32 + h, :], lambda h, j: A[:, 16 + h, :])
            stage_end(pe, 6)
            out_project(C_OUT0, 2, 8, lambda c: A[:, 16 + c, :], "out1")
            norm_sums(2, xT)
            stage_end(pe, 7)
            experts(MOE1, 1)
            norm_sums(3, xacc)
            stage_end(pe, 8)
            for b, n in enumerate((P, P, NB)):
                for c in range(DC):
                    tr = pe.transpose(bank[2 * b + c // 4][0:n, (c % 4) * P:(c % 4 + 1) * P], xT[:, c, b * P:b * P + n],
                                      ident[:, :])
                    if c % 4 == 3:
                        tr.then_inc(sem("y_turned"), 1)

        @block.scalar
        def _(act):
            def load(dst, src, name):
                act.dma_start(dst, src, allow_slow_non_contiguous=True).then_inc(sem(name), 16)

            load(xrows[:, 0:2, :], x_prompt[0].rearrange("(b p) d -> p b d", p=P), "x_loaded")
            load(xrows[0:NB, 2, :], x_sample.rearrange("b o d -> (b o) d"), "x_loaded")

            def rows(r, n, v):
                load(vrows[r:r + n, :], v, "vectors_loaded")

            rows(V_BGK, 4, b_gk2.rearrange("o (r p) -> (o r) p", p=P))
            rows(V_GLAN, 2, gla_norm_w.rearrange("o (r p) -> (o r) p", p=P))
            rows(V_SSDN, 8, ssd_norm_w.rearrange("o (r p) -> (o r) p", p=P))
            for r, v in ((V_LN1W, ln1_w), (V_LN1B, ln1_b), (V_LN2W, ln2_w), (V_LN2B, ln2_b)):
                rows(r, 16, v.rearrange("o (r p) -> (o r) p", p=P))
            rows(V_HGN, 1, hg_norm_w)
            rows(V_LB, 16, lower_bounds.rearrange("o (r p) -> (o r) p", p=P))
            load(crows[0:24, :], state_conv[0].rearrange("b j n -> (b j) n"), "vectors_loaded")
            load(crows[24:28, :], conv_w[0], "vectors_loaded")
            load(crows[28:29, :], conv_b, "vectors_loaded")
            load(wgk[:, :], w_gk2[0], "vectors_loaded")
            load(router[:, :, :], router_w.rearrange("(c p) e -> p c e", p=P), "vectors_loaded")
            load(wsmall[:, :, 0:16], w_in_ab[0, :, 3072:3088].rearrange("(c p) n -> p c n", p=P), "vectors_loaded")
            load(wsmall[:, :, 16:32], w_in_ab[0, :, 5648:5664].rearrange("(c p) n -> p c n", p=P), "vectors_loaded")
            load(small[:, 0:1], dt_bias.rearrange("o h -> h o"), "vectors_loaded")
            load(small[:, 1:2], a_log.rearrange("o h -> h o"), "vectors_loaded")
            load(rbias[:, :], router_bias.rearrange("(o e) -> o e", o=1).to_broadcast([P, E_N]), "vectors_loaded")
            for i in range(2):
                load(dskip[64 * i:64 * i + 64, :],
                     d_skip.rearrange("o (j i) -> o i j", i=2)[:, i, :].to_broadcast([64, 8]), "vectors_loaded")

            st = Steps(act, "act_steps")
            for c in range(0, DC, 2):
                act.wait_ge(sem("xT_turned"), c + 1)
                st.run(act.copy(xT[:, c, :], bank[c][:, 0:T]))
                act.sem_inc(sem("xT_copied"), 1)
            act.wait_ge(sem("vectors_turned"), 1)
            st.run(act.copy(cols[:, :], bank[0][:, 0:V_N]))
            act.sem_inc(sem("vectors_copied"), 1)
            st.run(act.activation(small[:, 2:3], small[:, 1:2], ACT.Exp))
            act.wait_ge(sem("lb_diff"), 1)
            st.run(act.activation(lbc[:, 0, :], lbc[:, 2, :], ACT.Tanh, scale=0.5))
            act.sem_inc(sem("lb_tanh"), 1)

            for m in range(0, AB_CHUNKS, 2):
                act.wait_ge(sem("in0_ready"), m + 1)
                act.copy(A[:, m, :], bank[m % 4][:, 0:T]).then_inc(sem("in0_copied0"), 1)
            act.wait_ge(sem("in0_copied0"), 22)
            act.wait_ge(sem("in0_copied1"), 22)
            act.wait_ge(sem("conv_turned"), 3)
            for a0 in (G0, Z0):
                st.run(act.activation(A[:, a0:a0 + 8, :], A[:, a0:a0 + 8, :], ACT.Silu))
            for m in range(12):
                act.wait_ge(sem("conv_done"), m + 1)
                act.activation(A[:, XS0 + m, :], cacc[:, m % 2, :], ACT.Silu).then_inc(sem("conv_silu"), 1)
            act.wait_ge(sem("conv_silu"), 12)
            for h in range(4):
                act.wait_ge(sem("gk_ready"), h + 1)
                st.run(act.activation(gkz[:, h, :], bank[h][:, 0:T], ACT.Identity, bias=cols[:, V_BGK + h:V_BGK + h + 1]))
            st.run(act.activation(gka[:, :, :], gkz[:, :, :], ACT.Abs))
            st.run(act.activation(gka[:, :, :], gka[:, :, :], ACT.Exp, scale=-1.0))
            st.run(act.activation(gka[:, :, :], gka[:, :, :], ACT.Ln, bias=1.0))
            act.wait_ge(sem("small_copied"), 2)
            st.run(act.activation(dtT[:, 0, :], dtT[:, 0, :], ACT.Identity, bias=small[:, 0:1]))
            st.run(act.activation(dtT[:, 1, :], dtT[:, 0, :], ACT.Abs))
            st.run(act.activation(dtT[:, 1, :], dtT[:, 1, :], ACT.Exp, scale=-1.0))
            st.run(act.activation(dtT[:, 1, :], dtT[:, 1, :], ACT.Ln, bias=1.0))
            act.sem_inc(sem("gates_ln"), 1)
            stage_end(act, 1)

            def gated_heads(layer, nh, dv, va, gates):
                tag = "heads_"
                H0 = 4 * layer
                J = dv // P

                def exps(h):
                    hb = head_area(h)
                    act.wait_ge(sem(tag + "g_scanned"), (H0 + h) + 1)
                    st.add(act.activation(hb["E2"], hb["E1"], ACT.Exp, scale=-1.0))
                    st.add(act.activation(hb["EG"], hb["G"], ACT.Exp))
                    st.add(act.activation(hb["EL"], hb["EL"], ACT.Exp))
                    st.settle()
                    act.activation(hb["E1"], hb["E1"], ACT.Exp).then_inc(sem(tag + "exps"), 1)
                    act.wait_ge(sem(tag + "exps"), (H0 + h) + 1)

                st.run(act.activation(decx[:, 0:nh, :], (gkg[:, 0:4, NP:T] if layer == 0 else A[:, 8:16, NP:T]), ACT.Exp))
                act.sem_inc(sem("dec_exps"), 1)
                exps(0)
                for h in range(nh):
                    hb = head_area(h)
                    per = 512 // dv
                    act.wait_ge(sem(tag + "v_turned"), (H0 + h) + 1)
                    act.activation(hb["vtm"][0:C, 0:per, 0:dv], bank[0][0:C, :].rearrange("p (c v) -> p c v", v=dv),
                                   ACT.Copy).then_inc(sem(tag + "kv_copied"), 1)
                    if per < NC:
                        act.activation(hb["vtm"][0:C, per:NC, 0:dv], bank[1][0:C, :].rearrange("p (c v) -> p c v", v=dv),
                                       ACT.Copy).then_inc(sem(tag + "kv_copied"), 1)
                    else:
                        act.sem_inc(sem(tag + "kv_copied"), 1)
                    act.wait_ge(sem(tag + "k_turned"), (H0 + h) + 1)
                    act.activation(hb["ktm"][0:C, :, :], bank[3][0:C, :].rearrange("p (c k) -> p c k", k=P),
                                   ACT.Copy).then_inc(sem(tag + "kv_copied"), 1)
                    if h + 1 < nh:
                        exps(h + 1)
                    act.wait_ge(sem(tag + "out_copied"), (H0 + h) + 1)
                    for j in range(J):
                        sq = act.activation(SQ[:, j, :], va(h, j), ACT.Square, scale=dv ** -0.5)
                        st.add(sq)
                    st.settle()
                    act.sem_inc(sem(tag + "squared"), 1)
                gall = gkg[:, :, :] if layer == 0 else A[:, 8:16, :]
                act.wait_ge(sem(tag + "normed"), H0 + nh)
                st.run(act.activation(gall, gall, ACT.Sqrt))
                act.sem_inc(sem(tag + "roots"), 1)

            gated_heads(0, 4, 256, lambda h, j: A[:, VV0 + 2 * h + j, :], None)
            act.wait_ge(sem("dt_scanned"), 1)
            st.run(act.activation(dtT[:, 2, :], dtT[:, 1, :], ACT.Exp))
            act.sem_inc(sem("dt_ready"), 1)
            stage_end(act, 2)
            act.wait_ge(sem("tm_ready"), 1)
            st.add(act.copy(s_tm[:, :, :], bank[0][:, 0:64].rearrange("p (a h) -> p a h", h=16)))
            st.add(act.copy(s_dd[0:NB, :], bank[0][0:NB, 64:80]))
            st.add(act.activation(s_el[:, :, :], bank[0][:, 80:112].rearrange("p (a h) -> p a h", h=16), ACT.Copy))
            st.add(act.copy(s_egd[:, :, :], bank[0][:, 112:240].rearrange("p (a h) -> p a h", h=16)))
            st.settle()
            act.sem_inc(sem("tm_copied"), 1)
            act.wait_ge(sem("w_diff"), 1)
            st.add(act.activation(s_w[:, :, :], s_w[:, :, :], ACT.Exp))
            st.add(act.activation(s_el[:, :, :], s_el[:, :, :], ACT.Exp))
            st.settle()
            act.sem_inc(sem("w_exp"), 1)
            for g in range(2):
                act.wait_ge(sem("ssd_turned"), g + 1)
                if g == 1:
                    act.wait_ge(sem("ssd_normed"), 1)
                st.add(act.copy(s_btm[:, :, :], bank[0][:, 0:256].rearrange("p (c k) -> p c k", k=P)))
                st.add(act.copy(s_bdec[0:NB, :], bank[0][0:NB, 256:384]))
                st.settle()
                act.sem_inc(sem("ssd_btm_copied"), 1)
                for pr in range(4):
                    act.wait_ge(sem("ssd_diffs"), 4 * g + pr + 1)
                    for c in range(NCS):
                        e = s_E[:, c, 2 * pr:2 * pr + 2, :]
                        st.add(act.activation(e, e, ACT.Exp))
                st.settle()
                act.sem_inc(sem("ssd_exps"), 1)
                act.wait_ge(sem("ssd_update_ready"), 2 * g + 1)
                st.run(act.copy(s_S[:, 0, :], bank[7][:, :]))
                act.sem_inc(sem("ssd_state0"), 1)
                act.wait_ge(sem("eg_ready"), g + 1)
                st.run(act.copy(s_eg[:, :], bank[0][:, :]))
                act.sem_inc(sem("eg_copied"), 1)
                act.wait_ge(sem("ssd_gated"), g + 1)
                st.run(act.activation(s_sq[:, :, :], A[:, XS0 + 4 * g:XS0 + 4 * g + 4, :], ACT.Square,
                                      scale=NORM_SSD ** -0.5))
                act.sem_inc(sem("ssd_squared"), 1)
            act.wait_ge(sem("ssd_normed"), 2)
            st.run(act.activation(gkg[:, 0:2, :], gkg[:, 0:2, :], ACT.Sqrt))
            act.sem_inc(sem("ssd_roots"), 1)
            stage_end(act, 3)

            def squares(k):
                act.wait_ge(sem("norm_centered"), k + 1)
                st.run(act.activation(lnsq[:, :, :], xT[:, :, :], ACT.Square, scale=D ** -0.5))
                act.sem_inc(sem("norm_squares"), 1)
                act.wait_ge(sem("norm_variance"), k + 1)
                st.run(act.activation(lnr[:, :], lnr[:, :], ACT.Sqrt))
                act.sem_inc(sem("norm_roots"), 1)

            def experts(layer):
                E0 = E_N * layer
                act.wait_ge(sem("moe_logits"), layer + 1)
                act.wait_ge(sem("moe_score_cleared"), layer + 1)
                for b, n in enumerate((P, P, NB)):
                    st.add(act.activation(score[0:n, b, :], bank[2][0:n, 16 * b:16 * b + 16], ACT.Sigmoid))
                st.settle()
                act.sem_inc(sem("moe_scores"), 1)
                for i in range(4):
                    act.wait_ge(sem("xtm_turned"), 4 * layer + i + 1)
                    act.copy(xtm[:, i // 2, (i % 2) * 512:(i % 2 + 1) * 512], bank[4 + i][:, :]).then_inc(
                        sem("xtm_copied"), 1)
                for i in range(0, 2 * DC, 2):
                    act.wait_ge(sem("gather_ready"), 2 * DC * layer + i + 1)
                    half, c = divmod(i, DC)
                    act.activation(XG[:, 8 * half:8 * half + 8, c, 0:PCAP],
                                   bank[i % 4][:, 0:8 * PCAP].rearrange("p (e s) -> p e s", e=8), ACT.Copy).then_inc(
                        sem("gathered0"), 1)
                for q in range(8):
                    act.wait_ge(sem("pt_turned"), 8 * layer + q + 1)
                    act.copy(PT[:, q, :], bank[4 + q % 4][:, 0:T]).then_inc(sem("pt_copied"), 1)
                if layer == 0:
                    act.sem_inc(sem("y_copied0"), 1)
                with act.Fori(0, E_N // 2) as pair:
                    e = 2 * pair + E0
                    for j in range(2):
                        act.wait_ge(sem("moe_gu"), e + j + 1)
                        act.wait_ge(sem("moe_hidden"), e + j + 1)
                        act.activation(sg[:, j, :], bank[j][:, 0:4 * CAP], ACT.Silu).then_inc(sem("moe_silu"), 1)
                    act.wait_ge(sem("moe_down"), e + 2)
                    act.copy(Y[:, 0:512], bank[4][:, :]).then_inc(sem("y_copied0"), 1)
                act.wait_ge(sem("over_known"), layer + 1)
                flag = act.value_load(over[0:1, 0:1], min_val=0, max_val=1)
                with act.If(flag > 0):
                    with act.Fori(0, E_N) as e:
                        x = E0 + e
                        act.wait_ge(sem("over_spread"), x + 1)
                        act.wait_ge(sem("over_hidden"), 4 * x + 2)
                        act.copy(ogb, bank[6][:, 0:NP]).then_inc(sem("over_spread_copied"), 1)
                        for f in range(4):
                            act.wait_ge(sem("over_gu"), 4 * x + f + 1)
                            act.wait_ge(sem("over_hidden"), 4 * x + f + 1)
                            act.activation(og[:, f % 2, :], bank[f % 2][:, 0:NP], ACT.Silu).then_inc(sem("over_silu"), 1)
                if layer == 0:
                    with act.If(flag < 1):
                        act.sem_inc(sem("over_spread_copied"), E_N)
                        act.sem_inc(sem("over_silu"), 4 * E_N)

            squares(0)
            stage_end(act, 4)
            experts(0)
            squares(1)
            stage_end(act, 5)
            for m in range(0, 32, 2):
                act.wait_ge(sem("in1_ready"), m + 1)
                act.copy(A[:, m, :], bank[m % 4][:, 0:T]).then_inc(sem("in1_copied0"), 1)
            act.wait_ge(sem("in1_copied0"), 16)
            act.wait_ge(sem("in1_copied1"), 16)
            st.add(act.activation(A[:, 8:16, :], A[:, 8:16, :], ACT.Tanh, scale=0.5))
            st.settle()
            act.sem_inc(sem("hg_tanh"), 1)
            st.add(act.activation(A[:, 0:8, :], A[:, 0:8, :], ACT.Silu))
            st.add(act.activation(A[:, 24:32, :], A[:, 24:32, :], ACT.Silu))
            st.settle()
            act.wait_ge(sem("hg_forget"), 1)
            st.run(act.activation(A[:, 8:16, :], A[:, 8:16, :], ACT.Ln))
            act.sem_inc(sem("hg_log"), 1)
            gated_heads(1, 8, 128, lambda h, j: A[:, 16 + h, :], None)
            stage_end(act, 6)
            squares(2)
            stage_end(act, 7)
            experts(1)
            squares(3)
            stage_end(act, 8)
            yrows = area(0, 3, D)
            for b, n in enumerate((P, P, NB)):
                for i in range(2):
                    act.wait_ge(sem("y_turned"), 2 * b + i + 1)
                    st.run(act.copy(yrows[0:n, b, i * 512:(i + 1) * 512], bank[2 * b + i][0:n, :]))
                if b < 2:
                    act.dma_start(y_prompt[0, b * P:(b + 1) * P, :], yrows[:, b, :]).then_inc(sem("y_stored"), 16)
                else:
                    act.dma_start(y_sample.rearrange("b o d -> (b o) d"), yrows[0:NB, 2, :]).then_inc(sem("y_stored"), 16)
            act.wait_ge(sem("y_stored"), 48)

        @block.vector
        def _(dve):
            st = Steps(dve, "dve_steps")

            def tt(out, a, b, op):
                st.run(dve.tensor_tensor(out, a, b, op))

            for c in range(1, DC, 2):
                dve.wait_ge(sem("xT_turned"), c + 1)
                st.run(dve.tensor_copy(xT[:, c, :], bank[c][:, 0:T]))
                dve.sem_inc(sem("xT_copied"), 1)
            dve.wait_ge(sem("vectors_turned"), 2)
            st.run(dve.tensor_copy(convc[:, :, :], bank[1][:, 0:348].rearrange("p (m r) -> p m r", r=29)))
            dve.sem_inc(sem("vectors_copied"), 1)
            dve.wait_ge(sem("vectors_copied"), 2)
            dve.wait_ge(sem("consts_made"), 1)
            st.run(dve.tensor_tensor(lbc[:, 2, :], cols[:, V_LB + 8:V_LB + 16], cols[:, V_LB:V_LB + 8], ALU.subtract))
            dve.sem_inc(sem("lb_diff"), 1)
            dve.wait_ge(sem("lb_tanh"), 1)
            st.run(dve.tensor_scalar(lbc[:, 1, :], lbc[:, 0, :], -0.25, 0.25, ALU.mult, ALU.add))
            st.run(dve.tensor_scalar(small[:, 2:3], small[:, 2:3], -1.0, None, ALU.mult))

            for m in range(1, AB_CHUNKS, 2):
                dve.wait_ge(sem("in0_ready"), m + 1)
                dve.tensor_copy(A[:, m, :], bank[m % 4][:, 0:T]).then_inc(sem("in0_copied1"), 1)
            dve.wait_ge(sem("small_ready"), 2)
            dve.tensor_copy(lrT[:, :], bank[4][0:16, 0:T]).then_inc(sem("small_copied"), 1)
            dve.tensor_copy(dtT[:, 0, :], bank[5][0:16, 0:T]).then_inc(sem("small_copied"), 1)
            dve.wait_ge(sem("in0_copied0"), 22)
            dve.wait_ge(sem("in0_copied1"), 22)
            for i in range(3):
                dve.wait_ge(sem("conv_turned"), i + 1)
                dve.tensor_copy(convout[0:16, i * 512:(i + 1) * 512], bank[5 + i][0:16, :]).then_inc(sem("convout_ready"), 1)
            for m in range(12):
                x, acc, cc = A[:, XS0 + m, :], cacc[:, m % 2, :], convc[:, m, :]
                if m >= 2:
                    dve.wait_ge(sem("conv_silu"), m - 1)
                st.run(dve.tensor_scalar(acc, x, cc[:, 27:28], cc[:, 28:29], ALU.mult, ALU.add))
                for j in range(3):
                    sh = 3 - j
                    st.add(dve.scalar_tensor_tensor(acc[:, sh:NP], x[:, 0:NP - sh], cc[:, 24 + j:25 + j],
                                                    acc[:, sh:NP], ALU.mult, ALU.add))
                    old = cc[:, 0:24].rearrange("p (b j) -> p b j", j=3)[:, :, j]
                    if j < 2:
                        st.run(dve.scalar_tensor_tensor(acc[:, NP:T], old, cc[:, 24 + j:25 + j], acc[:, NP:T],
                                                        ALU.mult, ALU.add))
                    else:
                        st.settle()
                        dve.scalar_tensor_tensor(acc[:, NP:T], old, cc[:, 24 + j:25 + j], acc[:, NP:T],
                                                 ALU.mult, ALU.add).then_inc(sem("conv_done"), 1)
            dve.wait_ge(sem("gates_ln"), 1)
            st.run(dve.tensor_scalar(gkz[:, :, :], gkz[:, :, :], 0.0, 1.0 / 16.0, ALU.min, ALU.mult))
            st.run(dve.scalar_tensor_tensor(gkg[:, :, :], gka[:, :, :], -1.0 / 16.0, gkz[:, :, :], ALU.mult, ALU.add))
            st.run(dve.scalar_tensor_tensor(dtT[:, 0, :], dtT[:, 0, :], 0.0, dtT[:, 1, :], ALU.max, ALU.add))
            st.run(dve.tensor_scalar(dtT[:, 2, :], dtT[:, 0, :], small[:, 2:3], None, ALU.mult))
            for c in range(NCS):
                s = slice(c * CS, (c + 1) * CS)
                st.add(dve.tensor_tensor_scan(dtT[:, 1, s], ones[0:16, 0:CS], dtT[:, 2, s], 0.0, ALU.mult, ALU.add))
            st.add(dve.tensor_copy(dtT[:, 1, NP:T], dtT[:, 2, NP:T]))
            st.settle()
            dve.sem_inc(sem("dt_scanned"), 1)
            stage_end(dve, 1)
            dve.sem_inc(sem("heads_area_free"), 1)

            def gated_heads(layer, nh, dv, qa, ka, va, ga, oa, scale, wcol):
                tag = "heads_"
                H0 = 4 * layer
                J = dv // P

                def prep(h):
                    hb = head_area(h)
                    g = ga(h)
                    v4 = lambda t: t.rearrange("p (c t) -> p c t", t=C)
                    st.run(dve.tensor_tensor_scan(hb["G"], restart[:, :], g[:, 0:NP], 0.0, ALU.mult, ALU.add))
                    G4 = v4(hb["G"])
                    st.add(dve.tensor_tensor(v4(hb["E1"]), G4, G4[:, :, C // 2 - 1:C // 2].to_broadcast([P, NC, C]),
                                             ALU.subtract))
                    st.add(dve.tensor_tensor(v4(hb["EL"]), G4[:, :, C - 1:C].to_broadcast([P, NC, C]), G4, ALU.subtract))
                    st.settle()
                    dve.sem_inc(sem(tag + "g_scanned"), 1)

                def prods(h):
                    hb = head_area(h)
                    dve.wait_ge(sem(tag + "exps"), (H0 + h) + 1)
                    q, k = qa(h), ka(h)
                    st.add(dve.scalar_tensor_tensor(hb["E1"], q[:, 0:NP], scale, hb["E1"], ALU.mult, ALU.mult))
                    st.add(dve.tensor_tensor(hb["E2"], k[:, 0:NP], hb["E2"], ALU.mult))
                    st.add(dve.scalar_tensor_tensor(hb["QD"], q[:, 0:NP], scale, hb["EG"], ALU.mult, ALU.mult))
                    st.add(dve.tensor_tensor(hb["EL"], k[:, 0:NP], hb["EL"], ALU.mult))
                    st.settle()
                    dve.sem_inc(sem(tag + "prepared"), 1)

                prep(0)
                prods(0)
                for h in range(nh):
                    hb = head_area(h)
                    if h + 1 < nh:
                        prep(h + 1)
                    st.add(dve.tensor_scalar(QS[:, :], qa(h)[:, NP:T], scale, None, ALU.mult))
                    dve.wait_ge(sem(tag + "v_turned"), (H0 + h) + 1)
                    st.add(dve.tensor_copy(KDEC[0:NB, :], bank[2][0:NB, 0:P]))
                    st.add(dve.tensor_copy(VDEC[0:NB, 0:dv], bank[2][0:NB, P:P + dv]))
                    st.settle()
                    km = lambda q: st.run(dve.tensor_tensor(
                        KMASK[0:NB, :, :], KDEC[0:NB, :].rearrange("p (o k) -> p o k", o=1).to_broadcast([NB, 4, P]),
                        ident[0:NB, 4 * q:4 * q + 4].rearrange("p (b o) -> p b o", o=1).to_broadcast([NB, 4, P]), ALU.mult))
                    km(0)
                    dve.sem_inc(sem(tag + "kmask_ready"), 1)
                    dve.wait_ge(sem(tag + "scores_ready"), (H0 + h) + 1)
                    if h >= 1:
                        dve.wait_ge(sem(tag + "out_ready"), (H0 + h))
                    st.run(dve.tensor_tensor(SC[0:C, :].rearrange("p (c t) -> p c t", t=C),
                                             bank[4][0:C, 0:NP].rearrange("p (c t) -> p c t", t=C),
                                             causal[0:C, 0:C].rearrange("p (o t) -> p o t", o=1).to_broadcast([C, NC, C]),
                                             ALU.mult))
                    dve.sem_inc(sem(tag + "scores_masked"), 1)
                    dve.wait_ge(sem(tag + "updates_ready"), (H0 + h) + 1)
                    if h >= 1:
                        dve.wait_ge(sem(tag + "prompt_state_stored"), 16 * (H0 + h))
                    per = 512 // dv
                    for c in range(NC):
                        u = bank[c // per][:, (c % per) * dv:(c % per + 1) * dv]
                        if c == 0:
                            st.run(dve.tensor_copy(ST[:, 0, 0:dv], u))
                        else:
                            st.run(dve.scalar_tensor_tensor(ST[:, c, 0:dv], ST[:, c - 1, 0:dv],
                                                            hb["EG"][:, (c + 1) * C - 1:(c + 1) * C], u, ALU.mult, ALU.add))
                    dve.sem_inc(sem(tag + "states_ready"), 1)
                    for b in range(NB):
                        if b % 4 == 0:
                            dve.wait_ge(sem(tag + "state_loaded"), 16 * (2 * (H0 + h) + b // 4 + 1))
                        if b == 4:
                            dve.wait_ge(sem(tag + "state_used"), 2 * (H0 + h) + 1)
                            km(1)
                            dve.sem_inc(sem(tag + "kmask_ready"), 1)
                        dve.wait_ge(sem(tag + "dec_update_ready"), NB * (H0 + h) + b + 1)
                        s = DST[:, b % 4, 0:dv]
                        dve.scalar_tensor_tensor(s, s, decg(h)[:, b:b + 1], bank[6 + b % 2][:, 0:dv],
                                                 ALU.mult, ALU.add).then_inc(sem(tag + "dec_updated"), 1)
                    if h + 1 < nh:
                        prods(h + 1)
                    dve.wait_ge(sem(tag + "out_ready"), (H0 + h) + 1)
                    dve.wait_ge(sem(tag + "state_used"), 2 * (H0 + h) + 2)
                    for j in range(J):
                        st.add(dve.tensor_copy(oa(h, j)[:, 0:NP], bank[5][:, j * NP:(j + 1) * NP]))
                        st.add(dve.tensor_copy(oa(h, j)[:, NP:T], bank[4][:, 256 + j * NB:256 + (j + 1) * NB]))
                    st.settle()
                    dve.sem_inc(sem(tag + "out_copied"), 1)
                    dve.wait_ge(sem(tag + "square_sums"), (H0 + h) + 1)
                    st.run(dve.tensor_scalar(ga(h), bank[3][:, 0:T], EPS, None, ALU.add))
                    dve.sem_inc(sem(tag + "normed"), 1)
                dve.wait_ge(sem(tag + "roots"), layer + 1)
                gall = gkg[:, :, :] if layer == 0 else A[:, 8:16, :]
                st.run(dve.reciprocal(gall, gall))
                for h in range(nh):
                    for j in range(J):
                        st.add(dve.tensor_tensor(oa(h, j), oa(h, j), ga(h), ALU.mult))
                st.settle()
                for h in range(nh):
                    for j in range(J):
                        st.add(dve.scalar_tensor_tensor(oa(h, j), oa(h, j), cols[:, wcol + j:wcol + j + 1],
                                                        gate_of(layer, h, j), ALU.mult, ALU.mult))
                st.settle()

            def decg(h):
                return decx[:, h, :]

            def gate_of(layer, h, j):
                return A[:, G0 + 2 * h + j, :] if layer == 0 else A[:, 24 + h, :]

            dve.wait_ge(sem("dec_exps"), 1)
            gated_heads(0, 4, 256, lambda h: A[:, Q0 + h, :], lambda h: A[:, K0 + h, :],
                        lambda h, j: A[:, VV0 + 2 * h + j, :], lambda h: gkg[:, h, :],
                        lambda h, j: A[:, VV0 + 2 * h + j, :], HEAD_SCALE, V_GLAN)
            stage_end(dve, 2)

            dve.wait_ge(sem("tm_copied"), 1)
            st.run(dve.tensor_tensor(s_w[:, :, :], s_el[:, :, :], s_tm[:, 0:2, :], ALU.subtract))
            dve.sem_inc(sem("w_diff"), 1)
            dve.wait_ge(sem("w_exp"), 1)
            st.run(dve.tensor_tensor(s_w[:, :, :], s_w[:, :, :], s_tm[:, 2:4, :], ALU.mult))
            for g in range(2):
                hs = slice(8 * g, 8 * g + 8)

                def per_head(a, n, w=64):
                    return a.rearrange("p (h o) -> p h o", o=1).to_broadcast([n, 8, w])
                h8 = lambda t: t.rearrange("p (h v) -> p h v", h=8)
                dve.wait_ge(sem("ssd_turned"), g + 1)
                for c in range(NCS):
                    xp = h8(bank[1 + c][:, :])
                    st.add(dve.tensor_tensor(h8(s_xdt[:, c, :]), xp, per_head(s_tm[:, 2 + c, hs], P), ALU.mult))
                    st.add(dve.tensor_tensor(h8(s_xw[:, c, :]), xp, per_head(s_w[:, c, hs], P), ALU.mult))
                st.add(dve.tensor_tensor(h8(s_xdec[0:NB, :]), h8(bank[3][0:NB, :]), per_head(s_dd[0:NB, hs], NB), ALU.mult))
                st.add(dve.tensor_tensor(s_g0[:, :, :], bank[4][:, 0:256].rearrange("p (c t) -> p c t", t=P),
                                         causal[:, :].rearrange("p (o t) -> p o t", o=1).to_broadcast([P, NCS, P]), ALU.mult))
                dve.wait_ge(sem("ssd_btm_copied"), g + 1)
                st.add(dve.tensor_tensor(
                    s_bmask[0:NB, :, :], s_bdec[0:NB, :].rearrange("p (o k) -> p o k", o=1).to_broadcast([NB, NB, P]),
                    ident[0:NB, 0:NB].rearrange("p (b o) -> p b o", o=1).to_broadcast([NB, NB, P]), ALU.mult))
                st.settle()
                dve.sem_inc(sem("ssd_tm_copied"), 1)
                dve.sem_inc(sem("bmask_ready"), 1)
                for pr in range(4):
                    dve.wait_ge(sem("gbc_ready"), 4 * g + pr + 1)
                    for i in range(2):
                        for c in range(NCS):
                            hh = 2 * pr + i
                            st.add(dve.tensor_scalar(s_E[:, c, hh, :], bank[5 + pr % 2][:, i * NP + c * CS:i * NP + (c + 1) * CS],
                                                     s_tm[:, c, 8 * g + hh:8 * g + hh + 1], 0.0, ALU.subtract, ALU.min))
                    st.settle()
                    dve.sem_inc(sem("ssd_diffs"), 1)
                dve.wait_ge(sem("ssd_exps"), g + 1)
                for c in range(NCS):
                    st.run(dve.tensor_tensor(s_E[:, c, :, :], s_E[:, c, :, :],
                                             s_g0[:, c, :].rearrange("p (o t) -> p o t", o=1).to_broadcast([P, 8, P]), ALU.mult))
                    dve.sem_inc(sem("ssd_scores"), 1)
                dve.wait_ge(sem("ssd_state0"), g + 1)
                if g == 1:
                    dve.wait_ge(sem("ssd_p_stored"), 16)
                st.run(dve.tensor_tensor(h8(s_S[:, 1, :]), h8(s_S[:, 0, :]), per_head(s_el[:, 1, hs], P), ALU.mult))
                dve.wait_ge(sem("ssd_update_ready"), 2 * g + 2)
                st.run(dve.tensor_tensor(s_S[:, 1, :], s_S[:, 1, :], bank[7][:, :], ALU.add))
                dve.sem_inc(sem("ssd_prompt_state"), 1)
                for b in range(NB):
                    n = NB * g + b
                    dve.wait_ge(sem(f"ssd_loaded{n % 2}"), 16 * (n // 2 + 1))
                    s = s_dst[:, n % 2, :]
                    st.run(dve.tensor_tensor(h8(s), h8(s), per_head(s_egd[:, b, hs], P), ALU.mult))
                    dve.wait_ge(sem("ssd_dec_ready"), n + 1)
                    dve.tensor_tensor(s, s, bank[5 + b % 2][:, :], ALU.add).then_inc(sem("ssd_dec_updated"), 1)
                dve.wait_ge(sem("eg_copied"), g + 1)
                dve.wait_ge(sem("ssd_inter"), g + 1)
                st.run(dve.tensor_tensor(s_yi[:, :], s_eg[:, :], bank[3][:, :], ALU.mult))
                dve.wait_ge(sem("ssd_state_used"), NB * g + NB)
                for j in range(4):
                    y = A[:, XS0 + 4 * g + j, :]
                    dk = dskip[:, 4 * g + j:4 * g + j + 1]
                    st.add(dve.scalar_tensor_tensor(y[:, 0:NP], y[:, 0:NP], dk, bank[1 + j // 2][:, (j % 2) * NP:(j % 2 + 1) * NP],
                                                    ALU.mult, ALU.add))
                    st.add(dve.scalar_tensor_tensor(y[:, NP:T], y[:, NP:T], dk, bank[4][:, 256 + j * NB:256 + (j + 1) * NB],
                                                    ALU.mult, ALU.add))
                st.settle()
                ys = A[:, XS0 + 4 * g:XS0 + 4 * g + 4, :]
                st.run(dve.tensor_tensor(ys[:, :, CS:NP], ys[:, :, CS:NP], s_yi[:, :].rearrange("p (j t) -> p j t", t=P), ALU.add))
                st.run(dve.tensor_tensor(ys, ys, A[:, Z0 + 4 * g:Z0 + 4 * g + 4, :], ALU.mult))
                dve.sem_inc(sem("ssd_gated"), 1)
                dve.wait_ge(sem("ssd_square_sums"), g + 1)
                st.run(dve.tensor_scalar(gkg[:, g, :], bank[7][:, 0:T], EPS, None, ALU.add))
                dve.sem_inc(sem("ssd_normed"), 1)
            dve.wait_ge(sem("ssd_roots"), 1)
            st.run(dve.reciprocal(gkg[:, 0:2, :], gkg[:, 0:2, :]))
            for j in range(8):
                w = cols[:, V_SSDN + j:V_SSDN + j + 1]
                st.add(dve.scalar_tensor_tensor(A[:, XS0 + j, :], A[:, XS0 + j, :], w, gkg[:, j // 4, :], ALU.mult, ALU.mult))
            st.settle()
            stage_end(dve, 3)

            def add_out(tag):
                for m in range(DC):
                    dve.wait_ge(sem(tag + "_ready"), m + 1)
                    st.add(dve.scalar_tensor_tensor(xT[:, m, :], xT[:, m, :], ALPHA, bank[m][:, 0:T], ALU.mult, ALU.add))
                st.settle()

            def layer_norm(k, src, wcol, bcol):
                dve.sem_inc(sem("norm_residual"), 1)
                dve.wait_ge(sem("norm_sum"), 2 * k + 1)
                st.run(dve.tensor_scalar(lnm[:, :], bank[0][:, 0:T], 1.0 / D, None, ALU.mult))
                bc = lambda t: t.rearrange("p (o t) -> p o t", o=1).to_broadcast([P, DC, T])
                st.run(dve.tensor_tensor(xT[:, :, :], src[:, :, :], bc(lnm[:, :]), ALU.subtract))
                dve.sem_inc(sem("norm_centered"), 1)
                dve.wait_ge(sem("norm_sum"), 2 * k + 2)
                st.run(dve.tensor_scalar(lnr[:, :], bank[1][:, 0:T], EPS, None, ALU.add))
                dve.sem_inc(sem("norm_variance"), 1)
                dve.wait_ge(sem("norm_roots"), k + 1)
                st.run(dve.reciprocal(lnr[:, :], lnr[:, :]))
                st.run(dve.tensor_tensor(xT[:, :, :], xT[:, :, :], bc(lnr[:, :]), ALU.mult))
                for c in range(DC):
                    st.add(dve.tensor_scalar(xT[:, c, :], xT[:, c, :], cols[:, wcol + c:wcol + c + 1],
                                             cols[:, bcol + c:bcol + c + 1], ALU.mult, ALU.add))
                st.settle()

            def pick_first(out, val, mx, sel, width):
                b3 = lambda t: t.to_broadcast([P, 3, width])
                ix = idx16[:, 0:width].rearrange("p (o e) -> p o e", o=1).to_broadcast([P, 3, width])
                st.run(dve.tensor_reduce(mx, val, AX, ALU.max))
                st.run(dve.tensor_tensor(sel, val, b3(mx), ALU.is_equal))
                st.run(dve.tensor_tensor(sel, sel, ix, ALU.mult))
                st.run(dve.tensor_reduce(mx, sel, AX, ALU.max))
                st.run(dve.tensor_tensor(out, sel, b3(mx), ALU.is_equal))

            def route(layer):
                tag = "moe"
                st.run(dve.memset(score[:, :, :], 0.5))
                dve.sem_inc(sem("moe_score_cleared"), 1)
                dve.wait_ge(sem("moe_scores"), layer + 1)
                sel, t1, t2, oh = (rt[:, i, :, :] for i in range(4))
                mx = rt[:, 4, :, 0:1]
                grp = rt[:, 5, :, 0:4]
                tt(sel, score[:, :, :], rbias[:, :].rearrange("p (o e) -> p o e", o=1).to_broadcast([P, 3, E_N]), ALU.add)
                s4 = sel.rearrange("p b (g i) -> p b g i", i=4)
                v = [s4[:, :, :, i] for i in range(4)]
                a1 = t1.rearrange("p b (g i) -> p b g i", i=4)
                w = [a1[:, :, :, i] for i in range(4)]
                tt(w[0], v[0], v[1], ALU.max)
                tt(w[1], v[0], v[1], ALU.min)
                tt(w[2], v[2], v[3], ALU.max)
                tt(w[3], v[2], v[3], ALU.min)
                a2 = t2.rearrange("p b (g i) -> p b g i", i=4)
                u = [a2[:, :, :, i] for i in range(4)]
                tt(u[0], w[0], w[2], ALU.max)
                tt(u[1], w[0], w[2], ALU.min)
                tt(u[2], w[1], w[3], ALU.max)
                tt(u[3], u[1], u[2], ALU.max)
                tt(grp, u[0], u[3], ALU.add)
                pick_first(rt[:, 6, :, 0:4], grp, mx, rt[:, 7, :, 0:4], 4)
                gsel = rt[:, 6, :, 0:4]
                for i in range(4):
                    tt(w[i], v[i], gsel, ALU.mult)
                st.run(dve.tensor_scalar(rt[:, 7, :, 0:4], gsel, -1.0, BIG, ALU.add, ALU.mult))
                for i in range(4):
                    tt(w[i], w[i], rt[:, 7, :, 0:4], ALU.add)
                pick_first(oh, t1, mx, t2, E_N)
                st.run(dve.scalar_tensor_tensor(t1, oh, -2.0 * BIG, t1, ALU.mult, ALU.add))
                pick_first(rt[:, 7, :, :], t1, mx, t2, E_N)
                tt(oh, oh, rt[:, 7, :, :], ALU.add)
                dve.sem_inc(sem("moe_chosen"), 1)
                tt(gate[:, :, :], score[:, :, :], oh, ALU.mult)
                st.run(dve.tensor_reduce(mx, gate[:, :, :], AX, ALU.add))
                st.run(dve.reciprocal(mx, mx))
                tt(gate[:, :, :], gate[:, :, :], mx.to_broadcast([P, 3, E_N]), ALU.mult)
                dve.wait_ge(sem("moe_places"), layer + 1)
                place = rt[:, 7, 0:2, :]
                psum = bank[3][:, 0:32].rearrange("p (b e) -> p b e", e=E_N)
                st.run(dve.scalar_tensor_tensor(place, psum, 1.0, oh[:, 0:2, :], ALU.add, ALU.mult))
                st.run(dve.tensor_reduce(mx[:, 0, :], bank[3][:, 32:48], AX, ALU.max))
                st.run(dve.tensor_scalar(over[:, :], mx[:, 0, :], PLIM + 0.5, None, ALU.is_gt))
                dve.sem_inc(sem("over_known"), 1)
                st.run(dve.tensor_scalar(place, place, -1.0, None, ALU.add))
                for b in range(2):
                    st.add(dve.tensor_tensor(
                        SLOT1[:, b, :, :], iota[:, :].rearrange("p (o s) -> p o s", o=1).to_broadcast([P, E_N, CAP]),
                        place[:, b, :].rearrange("p (e o) -> p e o", o=1).to_broadcast([P, E_N, CAP]), ALU.is_equal))
                st.settle()
                dve.sem_inc(sem("moe_slots"), 1)

                def over_gates():
                    st.run(dve.tensor_scalar(t1[:, 0:2, :], place, PLIM - 0.5, None, ALU.is_gt))
                    tt(rt[:, 6, 0:2, :], t1[:, 0:2, :], gate[:, 0:2, :], ALU.mult)

                def weigh(b):
                    st.run(dve.tensor_tensor(
                        WS[:, b, :, :], SLOT1[:, b, :, :],
                        gate[:, b, :].rearrange("p (e o) -> p e o", o=1).to_broadcast([P, E_N, CAP]), ALU.mult))
                    st.add(dve.memset(WS[:, b, :, PLIM:CAP], 0.0))

                def weigh_decode():
                    st.run(dve.memset(WS2[0:NB, :, :], 0.0))
                    st.run(dve.tensor_tensor(
                        WS2[0:NB, :, PCAP:CAP],
                        ident[0:NB, 0:NB].rearrange("p (o s) -> p o s", o=1).to_broadcast([NB, E_N, NB]),
                        gate[0:NB, 2, :].rearrange("p (e o) -> p e o", o=1).to_broadcast([NB, E_N, NB]), ALU.mult))
                    dve.sem_inc(sem("moe_weighted"), 1)

                def decode_inputs(e0):
                    for e in range(e0, e0 + 8):
                        st.add(dve.tensor_copy(XG[:, e, :, PCAP:CAP], xT[:, :, NP:T]))

                def residual():
                    st.add(dve.tensor_scalar(xacc[:, :, :], xT[:, :, :], ALPHA, None, ALU.mult))

                jobs = [over_gates, lambda: weigh(0), lambda: weigh(1), weigh_decode, lambda: decode_inputs(0),
                        lambda: decode_inputs(8), residual]
                for i in range(1, 2 * DC, 2):
                    dve.wait_ge(sem("gather_ready"), 2 * DC * layer + i + 1)
                    half, c = divmod(i, DC)
                    dve.tensor_copy(XG[:, 8 * half:8 * half + 8, c, 0:PCAP],
                                    bank[i % 4][:, 0:8 * PCAP].rearrange("p (e s) -> p e s", e=8)).then_inc(
                        sem("gathered1"), 1)
                    if jobs:
                        jobs.pop(0)()
                st.settle()

            def experts(layer):
                E0 = E_N * layer
                if layer == 0:
                    dve.sem_inc(sem("moe_hidden"), 2)
                    dve.sem_inc(sem("moe_added"), 2)
                    dve.sem_inc(sem("y_copied1"), 1)
                    dve.sem_inc(sem("over_hidden"), 2)
                    dve.sem_inc(sem("over_added"), 2)
                for i in range(2):
                    dve.wait_ge(sem(f"gathered{i}"), DC * (layer + 1))
                for j in range(2):
                    dve.tensor_copy(xg[:, j, :, :], XG[:, j, :, :]).then_inc(sem("xg_copied"), 1)
                with dve.Fori(0, E_N // 2) as pair:
                    e = 2 * pair + E0
                    for j in range(2):
                        dve.wait_ge(sem("moe_silu"), e + j + 1)
                        dve.tensor_tensor(hT[:, j, :], sg[:, j, :], bank[2 + j][:, 0:4 * CAP], ALU.mult).then_inc(
                            sem("moe_hidden"), 1)
                        nxt = XG[:, bass.ds(2 * pair + j + 2, 1), :, :].rearrange("p o c s -> p (o c) s")
                        dve.tensor_copy(xg[:, j, :, :], nxt).then_inc(sem("xg_copied"), 1)
                    dve.wait_ge(sem("moe_down"), e + 2)
                    dve.tensor_copy(Y[:, 512:1024], bank[5][:, :]).then_inc(sem("y_copied1"), 1)
                    dve.wait_ge(sem("moe_added"), DC * pair + 64 * layer + 2)
                    for c in range(DC):
                        dve.wait_ge(sem("moe_back"), DC * pair + (64 * layer + c + 1))
                        dve.tensor_tensor(xacc[:, c, :], xacc[:, c, :], bank[6 + c % 2][:, 0:T], ALU.add).then_inc(
                            sem("moe_added"), 1)
                dve.wait_ge(sem("moe_added"), 64 * (layer + 1) + 2)
                dve.wait_ge(sem("xg_copied"), 18 * (layer + 1))
                flag = dve.value_load(over[0:1, 0:1], min_val=0, max_val=1)
                with dve.If(flag > 0):
                    dve.sem_inc(sem("over_gates"), 1)
                    dve.wait_ge(sem("over_turned"), layer + 1)
                    dve.tensor_copy(ogT, bank[7][0:16, 0:NP]).then_inc(sem("over_gates_copied"), 1)
                    with dve.Fori(0, E_N) as e:
                        x = E0 + e
                        dve.tensor_copy(osel, ident[0:16, bass.ds(e, 1)].to_broadcast([16, P])).then_inc(sem("over_sel"), 1)
                        dve.wait_ge(sem("over_spread_copied"), x + 1)
                        for f in range(4):
                            dve.wait_ge(sem("over_silu"), 4 * x + f + 1)
                            dve.tensor_tensor(og[:, f % 2, :], og[:, f % 2, :], ogb, ALU.mult).then_inc(
                                sem("over_weighted"), 1)
                            dve.wait_ge(sem("over_weighted"), 4 * x + f + 1)
                            dve.tensor_tensor(oh_[:, f, :], og[:, f % 2, :], bank[2 + f % 2][:, 0:NP], ALU.mult).then_inc(
                                sem("over_hidden"), 1)
                        dve.wait_ge(sem("over_added"), DC * x + 2)
                        for d in range(DC):
                            dve.wait_ge(sem("over_down"), DC * x + d + 1)
                            dve.tensor_tensor(xacc[:, d, 0:NP], xacc[:, d, 0:NP], bank[4 + d % 2][:, 0:NP], ALU.add
                                              ).then_inc(sem("over_added"), 1)
                    dve.wait_ge(sem("over_added"), DC * E_N * (layer + 1) + 2)
                if layer == 0:
                    with dve.If(flag < 1):
                        for name, k in (("gates", 1), ("gates_copied", 1), ("sel", E_N), ("weighted", 4 * E_N),
                                        ("hidden", 4 * E_N), ("added", DC * E_N)):
                            dve.sem_inc(sem("over_" + name), k)

            add_out("out0")
            layer_norm(0, xT, V_LN1W, V_LN1B)
            stage_end(dve, 4)
            route(0)
            experts(0)
            layer_norm(1, xacc, V_LN2W, V_LN2B)
            stage_end(dve, 5)
            for m in range(1, 32, 2):
                dve.wait_ge(sem("in1_ready"), m + 1)
                dve.tensor_copy(A[:, m, :], bank[m % 4][:, 0:T]).then_inc(sem("in1_copied1"), 1)
            dve.wait_ge(sem("hg_tanh"), 1)
            for h in range(8):
                k = A[:, 32 + h, :]
                st.run(dve.tensor_scalar(k, A[:, 8 + h, :], -1.0, 1.0, ALU.mult, ALU.add))
                st.run(dve.tensor_scalar(k, k, lbc[:, 1, h:h + 1], None, ALU.mult))
            st.run(dve.tensor_scalar(A[:, 8:16, :], A[:, 32:40, :], -1.0, 1.0, ALU.mult, ALU.add))
            dve.sem_inc(sem("hg_forget"), 1)
            dve.wait_ge(sem("hg_log"), 1)
            dve.sem_inc(sem("hg_prepared"), 1)
            dve.sem_inc(sem("heads_area_free"), 1)
            dve.wait_ge(sem("dec_exps"), 2)
            gated_heads(1, 8, 128, lambda h: A[:, h, :], lambda h: A[:, 32 + h, :], None, lambda h: A[:, 8 + h, :],
                        lambda h, j: A[:, 16 + h, :], 1.0, V_HGN)
            stage_end(dve, 6)
            add_out("out1")
            layer_norm(2, xT, V_LN1W + 8, V_LN1B + 8)
            stage_end(dve, 7)
            route(1)
            experts(1)
            layer_norm(3, xacc, V_LN2W + 8, V_LN2B + 8)
            stage_end(dve, 8)


_INS = ['x_prompt', 'x_sample', 'state_gla', 'state_ssd', 'state_conv', 'state_hgrn', 'w_in_ab', 'w_gk2', 'b_gk2',
        'gla_norm_w', 'conv_w', 'conv_b', 'dt_bias', 'a_log', 'd_skip', 'ssd_norm_w', 'w_out_ab', 'w_in_c',
        'lower_bounds', 'hg_norm_w', 'w_out_c', 'router_w', 'router_bias', 'w_gate', 'w_up', 'w_down', 'ln1_w',
        'ln1_b', 'ln2_w', 'ln2_b']
_OUTS = [(1, 256, 1024), (8, 1, 1024), (1, 1, 4, 128, 256), (1, 1, 16, 128, 64), (1, 1, 3, 1536), (1, 1, 8, 128, 128),
         (1, 8, 4, 128, 256), (1, 8, 16, 128, 64), (1, 8, 3, 1536), (1, 8, 8, 128, 128)]


def kernel(**inputs):
    import numpy as np
    import concourse.bacc as bacc
    from concourse.bass_utils import run_bass_kernel_spmd

    nc = bacc.Bacc("TRN2", target_bir_lowering=False, num_devices=1)
    arrays, ins, outs = {}, [], []
    for name in _INS:
        a = np.ascontiguousarray(inputs[name])
        arrays[f"in_{name}"] = a
        ins.append(nc.dram_tensor(f"in_{name}", a.shape, mybir.dt.from_np(a.dtype), kind="ExternalInput").ap())
    for i, shape in enumerate(_OUTS):
        outs.append(nc.dram_tensor(f"out_{i}", shape, F32, kind="ExternalOutput").ap())
    trunk_program(nc, ins, outs)
    r = run_bass_kernel_spmd(nc, [arrays], core_ids=[0])
    return tuple(r.results[0][f"out_{i}"] for i in range(len(_OUTS)))
```

```python
from contextlib import ExitStack

import concourse.bass as bass
from concourse import mybir

F32 = mybir.dt.float32
ALU = mybir.AluOpType
ACT = mybir.ActivationFunctionType
AX = mybir.AxisListType.X

P = 128
D = 1024
DC = D // P
NP = 256
NB = 8
T = NP + NB
DEPTH = 2
ALPHA = (2 * DEPTH) ** 0.25
EPS = 1e-5
C = 64
NC = NP // C
CS = 128
NCS = NP // CS
E_N, E_G, E_K, FF = 16, 4, 2, 512
SLOTS = 6
SLOT_W = 4096
HEAD_SCALE = 128 ** -0.5
SSD_HEADS = 16
CAP = 64
PCAP = CAP - NB
PLIM = PCAP
DR = 64
NORM_GLA, NORM_SSD, NORM_HG = 256, 512, 128
BIG = 1.0e30

V_BGK, V_GLAN, V_SSDN, V_LN1W, V_LN1B, V_LN2W, V_LN2B, V_HGN, V_LB = 0, 4, 6, 14, 30, 46, 62, 78, 79
V_N = 95

Q0, K0, VV0, G0, Z0, XS0, B0, C0 = 0, 4, 8, 16, 24, 32, 40, 42
AB_CHUNKS = 44


def trunk_program(nc, ins, outs):
    (x_prompt, x_sample, state_gla, state_ssd, state_conv, state_hgrn, w_in_ab, w_gk2, b_gk2, gla_norm_w, conv_w,
     conv_b, dt_bias, a_log, d_skip, ssd_norm_w, w_out_ab, w_in_c, lower_bounds, hg_norm_w, w_out_c, router_w,
     router_bias, w_gate, w_up, w_down, ln1_w, ln1_b, ln2_w, ln2_b) = ins
    (y_prompt, y_sample, gla_p, ssd_p, conv_p, hg_p, gla_s, ssd_s, conv_s, hg_s) = outs

    with ExitStack() as ctx:
        def sb(name, shape, dt=F32):
            return ctx.enter_context(nc.sbuf_tensor(name, shape, dt))

        sems = {}

        def sem(name):
            if name not in sems:
                sems[name] = ctx.enter_context(nc.semaphore(name))
            return sems[name]

        bank = [ctx.enter_context(nc.psum_tensor(f"bank{i}", [P, 512], F32)) for i in range(8)]

        ring = sb("ring", [P, SLOTS, SLOT_W])
        xT = sb("xT", [P, DC, T])
        A = sb("A", [P, AB_CHUNKS, T])
        W = sb("W", [P, 10880])
        ident = sb("ident", [P, P])
        ones = sb("ones", [P, P])
        causal = sb("causal", [P, P])
        restart = sb("restart", [P, NP])
        cols = sb("cols", [P, V_N])
        router = sb("router", [P, DC, E_N])
        rbias = sb("rbias", [P, E_N])
        small = sb("small", [16, 4])
        dskip = sb("dskip", [P, 8])
        lbc = sb("lbc", [P, 3, 8])
        score = sb("score", [P, 3, E_N])
        gate = sb("gate", [P, 3, E_N])
        rt = sb("rt", [P, 8, 3, E_N])
        idx16 = sb("idx16", [P, E_N])
        strict = sb("strict", [P, P])
        iota = sb("iota", [P, 64])
        over = sb("over", [P, 1], mybir.dt.int32)

        def area(base, *shape):
            n = 1
            for s in shape:
                n *= s
            assert base + n <= W.shape[1]
            v = W[:, base:base + n]
            if len(shape) == 2:
                v = v.rearrange("p (a b) -> p a b", a=shape[0])
            if len(shape) == 3:
                v = v.rearrange("p (a b c) -> p a b c", a=shape[0], b=shape[1])
            return v

        Aflat = A[:, :, :].rearrange("p a t -> p (a t)")

        def chunks(n, k):
            return ring[:, n % SLOTS, :].rearrange("p (c n) -> p c n", c=k)

        HALF = NB // 2

        def states(n, heads):
            return ring[:, n % SLOTS, :].rearrange("p (b h v) -> p b h v", b=HALF, h=heads)

        def state_fills(n0, heads, src):
            return [(states(n0 + i, heads).rearrange("p b h v -> p (b h) v"),
                     src[0, HALF * i:HALF * (i + 1)].rearrange("b h k v -> k (b h) v")) for i in range(2)]

        AB_IN0, GLA_ST0, SSD_ST0, AB_OUT0, MOE0 = 0, 11, 13, 15, 19
        fills = []
        ab_cols = [4112, 4624, 5136, 3088, 3600, 0, 512, 1024, 1536, 2048, 2560]
        ab_order = [c for first, n in ((XS0, 12), (Z0, 8), (Q0, 4), (K0, 4), (VV0, 8), (G0, 8))
                    for c in range(first, first + n)]
        c_groups = [2, 3, 0, 1, 4, 5, 6, 7]
        c_order = [4 * g + i for g in c_groups for i in range(4)]
        conv_place = [G0 + i for i in range(8)] + [VV0 + 4 + i for i in range(4)]
        for c0 in ab_cols:
            fills.append((chunks(len(fills), 8), w_in_ab[0, :, c0:c0 + 512].rearrange("(c p) n -> p c n", p=P)))
        fills += state_fills(GLA_ST0, 4, state_gla)
        fills += state_fills(SSD_ST0, 16, state_ssd)
        for g in range(4):
            fills.append((chunks(len(fills), 16), w_out_ab[0, :, g * 256:g * 256 + 256].rearrange("(c p) n -> p c n", p=P)))
        MOE_SLOTS = 3 * E_N
        C_IN0 = MOE0 + MOE_SLOTS
        HG_ST0 = C_IN0 + 8
        C_OUT0 = HG_ST0 + 2
        MOE1 = C_OUT0 + 2
        slot = chunks

        PAIRS = E_N // 2
        GATHERS = PAIRS + 1

        def pair_views(layer, pair):
            views = [expert_views(layer, bass.ds(2 * pair + j, 1)) for j in range(2)]
            return [views[j][i] for i in range(3) for j in range(2)]

        def expert_views(layer, e):
            return [
                (w_gate[layer, e].rearrange("o (c p) n -> p (o c) n", p=P), 8),
                (w_up[layer, e].rearrange("o (c p) n -> p (o c) n", p=P), 8),
                (w_down[layer, e].rearrange("o (c p) n -> p (o c) n", p=P), 4),
            ]

        block = ctx.enter_context(nc.Block())

        class Steps:

            def __init__(self, eng, name):
                self.eng, self.sem, self.n = eng, sem(name), 0

            def add(self, ins):
                ins.then_inc(self.sem, 1)
                self.n += 1

            def settle(self):
                self.eng.wait_ge(self.sem, self.n)

            def run(self, ins):
                self.add(ins)
                self.settle()

        def stage_end(eng, k):
            eng.sem_inc(sem("stage_ended"), 1)
            eng.wait_ge(sem("stage_ended"), 4 * k)

        def gathered(eng, copy, i, g):
            eng.wait_ge(sem("gather_ready"), 2 * g + (i + 1))
            copy(xg.rearrange("p j c s -> p c j s")[:, 4 * i:4 * i + 4, :, 0:PCAP],
                 bank[2 + i][:, 0:8 * PCAP].rearrange("p (c j s) -> p c j s", c=4, j=2)).then_inc(
                sem(f"xg_copied{i}"), 1)

        xrows = area(0, 3, D)
        vrows = area(3072, P)
        crows = area(3200, 12 * P)
        wsmall = area(4736, 8, 32)
        convout = area(4992, 12 * P)

        MOE_READ = ("moe_gate", "moe_up", "moe_down")

        @block.sync
        def _(sp):
            def last_reader(n):
                if n < GLA_ST0:
                    return "in0_ready", 4 * (n + 1)
                if n < SSD_ST0:
                    return "gla_stored", 32
                if n < AB_OUT0:
                    return "ssd_stored", 32
                if n < MOE0:
                    return "out0_ready", 2 * (n - AB_OUT0 + 1)
                if n < C_IN0:
                    pair, i = divmod(n - MOE0, 6)
                    return MOE_READ[i // 2], pair + 1
                if n < HG_ST0:
                    return "in1_ready", 4 * (n - C_IN0 + 1)
                if n < C_OUT0:
                    return "hg_stored", 32
                return "out1_ready", 4 * (n - C_OUT0 + 1)

            def fill(n, dst, src):
                if n >= SLOTS:
                    name, value = last_reader(n - SLOTS)
                    sp.wait_ge(sem(name), value)
                sp.dma_start(dst, src).then_inc(sem(f"slot_filled{n % SLOTS}"), 16)

            def fill_experts(n0, layer):
                for i, (src, k) in enumerate(pair_views(layer, 0)):
                    fill(n0 + i, slot(n0 + i, k), src)
                with sp.Fori(1, PAIRS) as pair:
                    for i, (src, k) in enumerate(pair_views(layer, pair)):
                        sp.wait_ge(sem(MOE_READ[i // 2]), PAIRS * layer + pair)
                        sp.dma_start(slot(n0 + i, k), src).then_inc(sem(f"slot_filled{(n0 + i) % SLOTS}"), 16)

            def fill_over(layer):
                sp.wait_ge(sem("over_known"), layer + 1)
                flag = sp.value_load(over[0:1, 0:1], min_val=0, max_val=1)
                with sp.If(flag > 0):
                    for name in MOE_READ:
                        sp.wait_ge(sem(name), PAIRS * (layer + 1))
                    with sp.Fori(0, E_N) as e:
                        sp.wait_ge(sem("over_read"), E_N * layer + e + 1)
                        for i, (src, k) in enumerate(expert_views(layer, bass.ds(e, 1))):
                            sp.dma_start(slot(i, k), src).then_inc(sem(f"over_filled{i}"), 16)
                    sp.wait_ge(sem("over_read"), E_N * (layer + 1) + 1)
                if layer == 0:
                    with sp.If(flag < 1):
                        for i in range(3):
                            sp.sem_inc(sem(f"over_filled{i}"), 16 * E_N)

            sp.dma_start(xrows[:, 0:2, :], x_prompt[0].rearrange("(b p) d -> p b d", p=P)).then_inc(sem("x_loaded"), 16)
            sp.dma_start(xrows[0:NB, 2, :], x_sample.rearrange("b o d -> (b o) d")).then_inc(sem("x_loaded"), 16)
            for n, (dst, src) in enumerate(fills):
                fill(n, dst, src)
            fill_experts(MOE0, 0)
            fill_over(0)
            for i, g in enumerate(c_groups):
                fill(C_IN0 + i, slot(C_IN0 + i, 8), w_in_c[0, :, g * 512:g * 512 + 512].rearrange("(c p) n -> p c n", p=P))
            for i, (dst, src) in enumerate(state_fills(HG_ST0, 8, state_hgrn)):
                fill(HG_ST0 + i, dst, src)
            for g in range(2):
                fill(C_OUT0 + g, slot(C_OUT0 + g, 8), w_out_c[0, :, g * 512:g * 512 + 512].rearrange("(c p) n -> p c n", p=P))
            fill_experts(MOE1, 1)
            fill_over(1)

        convc = area(7056, 12, 29)
        gka = area(7564, 4, T)
        gkz = area(8620, 4, T)
        wgk = area(9676, 512)[0:16, :]
        lrT = area(10188, T)[0:16, :]
        gkg = sb("gkg", [P, 4, T])
        decx = sb("decx", [P, 8, NB])
        SLOT1 = Aflat[:, 2560:4864].rearrange("p (b e s) -> p b e s", b=2, e=E_N + 2)
        xg = Aflat[:, 4864:5888].rearrange("p (j c s) -> p j c s", j=2, c=DC)
        Y = Aflat[:, 5888:6912]
        xtm = area(0, 2, D)
        WS = area(2048, 2, E_N, CAP)
        WS2 = area(4096, E_N, CAP)
        PT = area(5120, 8, T)
        xacc = area(7232, DC, T)
        hT = area(9344, FF)
        hid = area(9856, FF)
        oh_ = Aflat[:, 0:4 * NP].rearrange("p (f t) -> p f t", f=4)
        og = Aflat[:, 1024:1024 + 2 * NP].rearrange("p (f t) -> p f t", f=2)
        ogb = Aflat[:, 1536:1536 + NP]
        osel = Aflat[0:16, 1792:1792 + P]
        ogT = Aflat[0:16, 2048:2048 + NP]
        lnsq = A[:, 0:8, :]
        lnm = area(0, T)
        lnr = area(512, T)

        def head_area(h):
            b = 3072 * (h % 2)
            names = {}
            for i, n in enumerate(["G", "E1", "E2", "EL", "EG", "QD"]):
                names[n] = area(b + 256 * i, NP)
            names["ktm"] = area(b + 1536, NC, P)
            names["vtm"] = area(b + 2048, NC, 256)
            names["vdec"] = area(b + 1536, 256)[DR:DR + NB, :]
            names["kmask"] = area(b + 2048, NB, P)[DR:DR + NB, :, :]
            return names
        SC = area(6144, 2, NP)
        ST = W[:, 6656:8704].rearrange("p (i c v) -> p i c v", i=2, c=NC)
        SQ = area(8704, 2, T)
        QS = area(9232, 2, NB)

        def decode_state(layer, h, b):
            n0, heads = (HG_ST0, 8) if layer else (GLA_ST0, 4)
            return states(n0 + b // HALF, heads)[:, b % HALF, h, :]

        def ssd_state(g, b):
            return states(SSD_ST0 + b // HALF, 16)[:, b % HALF, 8 * g:8 * g + 8, :]

        def slot_ready(eng, n):
            eng.wait_ge(sem(f"slot_filled{n % SLOTS}"), 16 * (n // SLOTS + 1))

        s_E = W[:, 0:2048].rearrange("p (c h t) -> p c h t", c=NCS, h=8)
        s_xdt = area(2048, NCS, 512)
        s_xw = area(3072, NCS, 512)
        s_btm = area(4096, NCS, P)
        s_g0 = area(4352, NCS, P)
        s_S = area(4608, NCS, 512)
        s_eg = area(5632, 512)
        s_yi = area(6144, 512)
        s_xdec = area(6656, 512)
        s_bdec = area(7168, P)
        s_bmask = area(7296, NB, P)
        s_sq = area(9344, 4, T)
        s_tm = area(10400, 4, 16)
        s_w = area(10464, 2, 16)
        s_el = area(10496, 2, 16)
        s_dd = area(10528, 16)
        s_egd = area(10544, NB, 16)
        dtT = sb("dtT", [16, 3, T])

        @block.gpsimd
        def _(pool):
            st = Steps(pool, "pool_steps")
            st.add(pool.memset(ident[:, :], 0.0))
            st.add(pool.memset(ones[:, :], 1.0))
            st.add(pool.memset(causal[:, :], 1.0))
            st.add(pool.memset(strict[:, :], 1.0))
            st.add(pool.memset(restart[:, :], 1.0))
            st.add(pool.iota(rt[:, 0, 0, :].bitcast(mybir.dt.int32), pattern=[[-1, E_N]], base=E_N, channel_multiplier=0))
            st.add(pool.iota(convout[:, 0:64].bitcast(mybir.dt.int32), pattern=[[1, 64]], base=0, channel_multiplier=0))
            st.settle()
            st.add(pool.tensor_copy(iota[:, :], convout[:, 0:64].bitcast(mybir.dt.int32)))
            st.add(pool.affine_select(out=ident[:, :], in_=ident[:, :], compare_op=ALU.not_equal, fill=1.0, base=0,
                                      pattern=[[-1, P]], channel_multiplier=1))
            st.add(pool.affine_select(out=causal[:, :], in_=causal[:, :], compare_op=ALU.is_ge, fill=0.0, base=0,
                                      pattern=[[1, P]], channel_multiplier=-1))
            st.add(pool.affine_select(out=strict[:, :], in_=strict[:, :], compare_op=ALU.is_ge, fill=0.0, base=-1,
                                      pattern=[[1, P]], channel_multiplier=-1))
            st.add(pool.memset(restart[:, :].rearrange("p (c t) -> p c t", t=C)[:, :, 0:1], 0.0))
            st.add(pool.tensor_copy(idx16[:, :], rt[:, 0, 0, :].bitcast(mybir.dt.int32)))
            st.settle()
            pool.sem_inc(sem("consts_made"), 1)

            def gated_states(layer, nh, dv, dst_p, gates, wcol, between):
                H0, J = 4 * layer, dv // P
                for h in range(nh):
                    for j in range(J):
                        st.add(pool.tensor_scalar(gates(h, j), gates(h, j), cols[:, wcol + j:wcol + j + 1], None, ALU.mult))
                st.settle()
                for h in range(nh):
                    n = H0 + h
                    between(h)
                    pool.wait_ge(sem("heads_states_ready"), n + 1)
                    pool.dma_start(dst_p[0, 0, h], ST[:, h % 2, NC - 1, 0:dv]).then_inc(
                        sem(f"heads_prompt_state_stored{h % 2}"), 16)
                    pool.wait_ge(sem("heads_squared"), n + 1)
                    for j in range(J):
                        o = A[:, (VV0 + 2 * h + j) if layer == 0 else 16 + h, :]
                        st.add(pool.tensor_tensor(o, o, gates(h, j), ALU.mult))
                    st.settle()
                pool.sem_inc(sem("heads_gated"), 1)
                for i in range(2):
                    pool.wait_ge(sem(f"heads_prompt_state_stored{i}"), 16 * (H0 + nh) // 2)

            def decay_ssd(h):
                g, half = h // 2, h % 2
                if h == 0:
                    pool.wait_ge(sem("tm_copied"), 1)
                slot_ready(pool, SSD_ST0 + half)
                for b in range(HALF * half, HALF * (half + 1)):
                    s = ssd_state(g, b)
                    st.add(pool.tensor_tensor(s, s, s_egd[:, b, 8 * g:8 * g + 8].rearrange("p (h o) -> p h o", o=1)
                                              .to_broadcast([P, 8, 64]), ALU.mult))
                st.settle()

            def store_states(n0, heads, dst, name):
                for i in range(2):
                    pool.dma_start(dst[0, HALF * i:HALF * (i + 1)].rearrange("b h k v -> k (b h) v"),
                                   states(n0 + i, heads).rearrange("p b h v -> p (b h) v")).then_inc(sem(name), 16)

            pool.wait_ge(sem("convout_ready"), 3)
            pool.dma_start(conv_p[0, 0], convout[5:8, :]).then_inc(sem("conv_stored"), 16)
            pool.dma_start(conv_s[0, :, 2], convout[8:16, :]).then_inc(sem("conv_stored"), 16)
            pool.dma_start(conv_s[0, :, 0:2], state_conv[0, :, 1:3]).then_inc(sem("conv_stored"), 16)
            pool.wait_ge(sem("conv_stored"), 48)
            stage_end(pool, 1)
            gated_states(0, 4, 256, gla_p, lambda h, j: A[:, G0 + 2 * h + j, :], V_GLAN, decay_ssd)
            pool.wait_ge(sem("heads_out_ready"), 4)
            store_states(GLA_ST0, 4, gla_s, "gla_stored")
            stage_end(pool, 2)
            for g in range(2):
                pool.wait_ge(sem("ssd_prompt_state"), g + 1)
                pool.dma_start(ssd_p[0, 0, 8 * g:8 * g + 8].rearrange("h n v -> n h v"),
                               s_S[:, 1, :].rearrange("p (h v) -> p h v", h=8)).then_inc(sem("ssd_p_stored"), 16)
            pool.wait_ge(sem("ssd_state_used"), 2)
            store_states(SSD_ST0, 16, ssd_s, "ssd_stored")
            pool.wait_ge(sem("ssd_p_stored"), 32)

            def expert_start(layer):
                for j in range(2):
                    st.add(pool.tensor_copy(xg[:, j, :, PCAP:CAP], xT[:, :, NP:T]))
                st.settle()
                pool.sem_inc(sem("decode_inputs"), 1)
                st.run(pool.tensor_scalar(xacc[:, :, :], xT[:, :, :], ALPHA, None, ALU.mult))
                pool.sem_inc(sem("moe_residual"), 1)

            stage_end(pool, 3)
            stage_end(pool, 4)
            expert_start(0)
            stage_end(pool, 5)
            pool.wait_ge(sem("in1_copied"), 32)
            gated_states(1, 8, 128, hg_p, lambda h, j: A[:, 24 + h, :], V_HGN, lambda h: None)
            pool.wait_ge(sem("heads_out_ready"), 12)
            store_states(HG_ST0, 8, hg_s, "hg_stored")
            stage_end(pool, 6)
            stage_end(pool, 7)
            expert_start(1)
            stage_end(pool, 8)
            for name in ("gla_stored", "ssd_stored", "hg_stored"):
                pool.wait_ge(sem(name), 32)

        @block.tensor
        def _(pe):
            pe.sem_inc(sem("over_read"), 1)
            pe.wait_ge(sem("consts_made"), 1)
            pe.wait_ge(sem("x_loaded"), 32)
            for c in range(DC):
                for b, n in enumerate((P, P, NB)):
                    tr = pe.transpose(bank[c][:, b * P:b * P + n], xrows[0:n, b, c * P:(c + 1) * P], ident[0:n, 0:n])
                tr.then_inc(sem("xT_turned"), 1)
            pe.wait_ge(sem("xT_copied"), 8)

            def turn_vectors():
                pe.wait_ge(sem("vectors_loaded"), 16 * 21)
                pe.transpose(bank[4][:, 0:V_N], vrows[0:V_N, :], ident[0:V_N, 0:V_N])
                for m in range(12):
                    tr = pe.transpose(bank[4][:, V_N + m * 29:V_N + (m + 1) * 29], crows[0:29, m * P:(m + 1) * P],
                                      ident[0:29, 0:29])
                tr.then_inc(sem("vectors_turned"), 1)

            def turn_conv_rows(i):
                pe.transpose(bank[5 + i // 4][0:16, (i % 4) * P:(i % 4 + 1) * P], A[:, XS0 + i, NP - 8:T],
                             ident[:, :]).then_inc(sem("conv_turned"), 1)

            def project_small():
                pe.wait_ge(sem("vectors_copied"), 1)
                pe.wait_ge(sem("convout_ready"), 3)
                for i in range(2):
                    for c in range(DC):
                        mm = pe.matmul(bank[4 + i][0:16, 0:T], wsmall[:, c, 16 * i:16 * i + 16], xT[:, c, :],
                                       start=(c == 0), stop=(c == DC - 1))
                    mm.then_inc(sem("small_ready"), 1)

            def project_gates():
                pe.wait_ge(sem("small_copied"), 2)
                for h in range(4):
                    pe.matmul(bank[4 + h][:, 0:T], wgk[:, h * P:(h + 1) * P], lrT[:, :], start=True, stop=True
                              ).then_inc(sem("gk_ready"), 1)

            def project(n0, groups, name, extra):
                m = 0
                for g in range(groups):
                    slot_ready(pe, n0 + g)
                    w = slot(n0 + g, 8)
                    for i in range(4):
                        if m >= 4:
                            pe.wait_ge(sem(name + "_copied"), m - 3)
                        for job in extra.get(m, []):
                            job()
                        for c in range(DC):
                            mm = pe.matmul(bank[m % 4][:, 0:T], w[:, c, i * P:(i + 1) * P], xT[:, c, :],
                                           start=(c == 0), stop=(c == DC - 1))
                        mm.then_inc(sem(name + "_ready"), 1)
                        m += 1

            extra = {m: [lambda i=m - 4: turn_conv_rows(i)] for m in range(4, 16)}
            extra[8].append(turn_vectors)
            extra[26] = [project_small]
            extra[29] = [project_gates]
            project(AB_IN0, 11, "in0", extra)
            stage_end(pe, 1)

            def gated_heads(layer, nh, dv, qa, ka, va, between):
                H0, J = 4 * layer, dv // P
                per = 512 // dv
                F = NB // per
                F0 = 16 * layer

                def turn(h):
                    hb, n = head_area(h), H0 + h
                    if h >= 1:
                        pe.wait_ge(sem("heads_states_ready"), n)
                    if h >= 2:
                        pe.wait_ge(sem("heads_normed"), n - 1)
                    for c in range(NC):
                        for j in range(J):
                            pe.transpose(bank[c // per][0:C, (c % per) * dv + j * P:(c % per) * dv + (j + 1) * P],
                                         va(h, j)[:, c * C:(c + 1) * C], ident[:, :])
                    for j, rows in enumerate([ka(h)] + [va(h, j) for j in range(J)]):
                        tr = pe.matmul(bank[2][DR:DR + NB, j * P:(j + 1) * P], rows[:, NP:T], ident[:, :], start=True,
                                       stop=True)
                    tr.then_inc(sem("heads_v_turned"), 1)
                    pe.wait_ge(sem("heads_prepared"), n + 1)
                    if h >= 1:
                        pe.wait_ge(sem("heads_scores_masked"), n)
                    for c in range(NC):
                        s = slice(c * C, (c + 1) * C)
                        mm = pe.matmul(bank[4][0:C, s], hb["E2"][:, s], hb["E1"][:, s], start=True, stop=True)
                    mm.then_inc(sem("heads_scores_ready"), 1)
                    for c in range(NC):
                        s = slice(c * C, (c + 1) * C)
                        tr = pe.transpose(bank[3][0:C, c * P:(c + 1) * P], hb["EL"][:, s], ident[:, :])
                    tr.then_inc(sem("heads_k_turned"), 1)

                def update(h):
                    hb = head_area(h)
                    pe.wait_ge(sem("heads_kv_copied"), 3 * (H0 + h) + 3)
                    for c in range(NC):
                        mm = pe.matmul(bank[c // per][:, (c % per) * dv:(c % per + 1) * dv], hb["ktm"][0:C, c, :],
                                       hb["vtm"][0:C, c, 0:dv], start=True, stop=True)
                    mm.then_inc(sem("heads_updates_ready"), 1)

                def decode(h, half):
                    hb, n = head_area(h), H0 + h
                    if half == 0:
                        pe.wait_ge(sem("heads_kmask_ready"), n + 1)
                    for i in range(F // 2 * half, F // 2 * (half + 1)):
                        if i >= 2:
                            pe.wait_ge(sem("heads_dec_updated"), F0 + F * h + i - 1)
                        for b in range(per * i, per * (i + 1)):
                            mm = pe.matmul(bank[6 + i % 2][:, (b % per) * dv:(b % per + 1) * dv], hb["kmask"][:, b, :],
                                           hb["vdec"][:, 0:dv], start=True, stop=True)
                        mm.then_inc(sem("heads_dec_update_ready"), 1)

                def outputs(h):
                    hb, n = head_area(h), H0 + h
                    pe.wait_ge(sem("heads_scores_masked"), n + 1)
                    pe.wait_ge(sem("heads_states_ready"), n + 1)
                    if h >= 1:
                        pe.wait_ge(sem("heads_out_copied"), n)
                        pe.wait_ge(sem("heads_squared"), n)
                    for j in range(J):
                        for c in range(NC):
                            s = slice(c * C, (c + 1) * C)
                            o = bank[5][:, j * NP + c * C:j * NP + (c + 1) * C]
                            pe.matmul(o, hb["vtm"][0:C, c, j * P:(j + 1) * P], SC[0:C, h % 2, s], start=True, stop=(c == 0))
                            if c > 0:
                                pe.matmul(o, ST[:, h % 2, c - 1, j * P:(j + 1) * P], hb["QD"][:, s], start=False, stop=True)
                    pe.wait_ge(sem("heads_dec_updated"), F0 + F * (h + 1))
                    for b in range(NB):
                        for j in range(J):
                            mm = pe.matmul(bank[4][:, 256 + j * NB + b:257 + j * NB + b],
                                           decode_state(layer, h, b)[:, j * P:(j + 1) * P], QS[:, h % 2, b:b + 1],
                                           start=True, stop=True)
                    mm.then_inc(sem("heads_out_ready"), 1)

                def sums(h):
                    n = H0 + h
                    if h + 1 < nh:
                        pe.wait_ge(sem("heads_kmask_ready"), n + 2)
                    pe.wait_ge(sem("heads_squared"), n + 1)
                    for j in range(J):
                        mm = pe.matmul(bank[2][:, 0:T], ones[:, :], SQ[:, j, :], start=(j == 0), stop=(j == J - 1))
                    mm.then_inc(sem("heads_square_sums"), 1)

                turn(0)
                between()
                update(0)
                for h in range(nh):
                    decode(h, 0)
                    if h + 1 < nh:
                        turn(h + 1)
                    decode(h, 1)
                    outputs(h)
                    if h + 1 < nh:
                        update(h + 1)
                    sums(h)

            def decays_token_major():
                pe.wait_ge(sem("dt_ready"), 1)
                t = bank[7]
                for c in range(NCS):
                    s = slice(c * CS, (c + 1) * CS)
                    pe.transpose(t[:, 16 * c:16 * c + 16], dtT[:, 1, s], ident[0:16, 0:16])
                    pe.transpose(t[:, 32 + 16 * c:48 + 16 * c], dtT[:, 0, s], ident[0:16, 0:16])
                pe.transpose(t[0:NB, 64:80], dtT[:, 0, NP:T], ident[0:16, 0:16])
                for c in range(NCS):
                    pe.matmul(t[:, 80 + 16 * c:96 + 16 * c],
                              dtT[:, 1, (c + 1) * CS - 1:(c + 1) * CS].to_broadcast([16, P]), ident[0:16, 0:16],
                              start=True, stop=True)
                for b in range(NB):
                    mm = pe.matmul(t[:, 112 + 16 * b:128 + 16 * b],
                                   dtT[:, 2, NP + b:NP + b + 1].to_broadcast([16, P]), ident[0:16, 0:16],
                                   start=True, stop=True)
                mm.then_inc(sem("tm_ready"), 1)
                pe.wait_ge(sem("tm_copied"), 1)

            gated_heads(0, 4, 256, lambda h: A[:, Q0 + h, :], lambda h: A[:, K0 + h, :],
                        lambda h, j: A[:, VV0 + 2 * h + j, :], decays_token_major)
            stage_end(pe, 2)

            for g in range(2):
                BT, CT = A[:, B0 + g, :], A[:, C0 + g, :]
                if g == 1:
                    pe.wait_ge(sem("ssd_normed"), 1)
                for c in range(NCS):
                    s = slice(c * CS, (c + 1) * CS)
                    pe.transpose(bank[0][:, c * P:(c + 1) * P], BT[:, s], ident[:, :])
                pe.transpose(bank[0][0:NB, 256:384], BT[:, NP:T], ident[:, :])
                for c in range(NCS):
                    s = slice(c * CS, (c + 1) * CS)
                    for j in range(4):
                        pe.transpose(bank[1 + c][:, j * P:(j + 1) * P], A[:, XS0 + 4 * g + j, s], ident[:, :])
                for j in range(4):
                    pe.transpose(bank[3][0:NB, j * P:(j + 1) * P], A[:, XS0 + 4 * g + j, NP:T], ident[:, :])
                for c in range(NCS):
                    s = slice(c * CS, (c + 1) * CS)
                    mm = pe.matmul(bank[4][:, c * P:(c + 1) * P], BT[:, s], CT[:, s], start=True, stop=True)
                mm.then_inc(sem("ssd_turned"), 1)
                for pr in range(4):
                    if pr >= 2:
                        pe.wait_ge(sem("ssd_diffs"), 4 * g + pr - 1)
                    for i in range(2):
                        h = 8 * g + 2 * pr + i
                        mm = pe.matmul(bank[5 + pr % 2][:, i * NP:(i + 1) * NP],
                                       ident[0:16, h:h + 1].to_broadcast([16, P]), dtT[:, 1, 0:NP],
                                       start=True, stop=True)
                    mm.then_inc(sem("gbc_ready"), 1)
                pe.wait_ge(sem("ssd_tm_copied"), g + 1)
                for c in range(NCS):
                    if c == 1:
                        pe.wait_ge(sem("ssd_state0"), g + 1)
                    pe.matmul(bank[7][:, :], s_btm[:, c, :], s_xw[:, c, :], start=True, stop=True).then_inc(
                        sem("ssd_update_ready"), 1)
                pe.wait_ge(sem("ssd_btm_copied"), g + 1)
                for j in range(4):
                    h = 8 * g + 2 * j
                    for i in range(2):
                        mm = pe.matmul(bank[0][64 * i:64 * i + 64, j * P:(j + 1) * P],
                                       ident[0:16, h + i:h + i + 1].to_broadcast([16, 64]), dtT[:, 2, CS:NP],
                                       start=True, stop=True)
                mm.then_inc(sem("eg_ready"), 1)
                pe.wait_ge(sem("ssd_scores"), 2 * g + 2)
                for j in range(4):
                    for c in range(NCS):
                        for i in range(2):
                            hh = 2 * j + i
                            mm = pe.matmul(bank[1 + j // 2][64 * i:64 * i + 64,
                                                            (j % 2) * NP + c * CS:(j % 2) * NP + (c + 1) * CS],
                                           s_xdt[:, c, hh * 64:(hh + 1) * 64], s_E[:, c, hh, :], start=True, stop=True)
                mm.then_inc(sem("ssd_intra"), 1)
                for j in range(4):
                    mm = pe.matmul(bank[3][:, j * P:(j + 1) * P], s_S[:, 0, j * P:(j + 1) * P], CT[:, CS:NP],
                                   start=True, stop=True)
                mm.then_inc(sem("ssd_inter"), 1)
                def read_state(b):
                    pe.wait_ge(sem("ssd_dec_updated"), NB * g + b + 1)
                    for j in range(4):
                        mm = pe.matmul(bank[4][:, 256 + j * NB + b:257 + j * NB + b],
                                       ssd_state(g, b)[:, 2 * j:2 * j + 2, :].rearrange("p h v -> p (h v)"),
                                       CT[:, NP + b:NP + b + 1], start=True, stop=True)
                    return mm

                pe.wait_ge(sem("ssd_diffs"), 4 * g + 4)
                pe.wait_ge(sem("bmask_ready"), g + 1)
                for b in range(NB):
                    if b >= 2:
                        pe.wait_ge(sem("ssd_dec_updated"), NB * g + b - 1)
                    pe.matmul(bank[5 + b % 2][:, :], s_bmask[0:NB, b, :], s_xdec[0:NB, :], start=True, stop=True
                              ).then_inc(sem("ssd_dec_ready"), 1)
                    if b >= 1:
                        read_state(b - 1)
                read_state(NB - 1).then_inc(sem("ssd_state_used"), 1)
                pe.wait_ge(sem("ssd_squared"), g + 1)
                for j in range(4):
                    mm = pe.matmul(bank[7][:, 0:T], ones[:, :], s_sq[:, j, :], start=(j == 0), stop=(j == 3))
                mm.then_inc(sem("ssd_square_sums"), 1)
            stage_end(pe, 3)

            def out_project(n0, groups, kc, srcs, tag):
                m = 0
                per = DC // groups
                for g in range(groups):
                    slot_ready(pe, n0 + g)
                    w = slot(n0 + g, kc)
                    for i in range(per):
                        for c in range(kc):
                            mm = pe.matmul(bank[m][:, 0:T], w[:, c, i * P:(i + 1) * P], srcs(c),
                                           start=(c == 0), stop=(c == kc - 1))
                        mm.then_inc(sem(tag + "_ready"), 1)
                        m += 1

            def norm_sums(k, src):
                pe.wait_ge(sem("norm_residual"), k + 1)
                for c in range(DC):
                    mm = pe.matmul(bank[0][:, 0:T], ones[:, :], src[:, c, :], start=(c == 0), stop=(c == DC - 1))
                mm.then_inc(sem("norm_sum"), 1)
                pe.wait_ge(sem("norm_squares"), k + 1)
                for c in range(DC):
                    mm = pe.matmul(bank[1][:, 0:T], ones[:, :], lnsq[:, c, :], start=(c == 0), stop=(c == DC - 1))
                mm.then_inc(sem("norm_sum"), 1)

            def experts(n0, layer):
                E0 = E_N * layer
                for b, n in enumerate((P, P, NB)):
                    for c in range(DC):
                        mm = pe.matmul(bank[2][0:n, 16 * b:16 * b + 16], xT[:, c, b * P:b * P + n], router[:, c, :],
                                       start=(c == 0), stop=(c == DC - 1))
                mm.then_inc(sem("moe_logits"), 1)
                for b in range(2):
                    for c in range(DC):
                        tr = pe.transpose(bank[4 + 2 * b + c // 4][:, (c % 4) * P:(c % 4 + 1) * P],
                                          xT[:, c, b * P:(b + 1) * P], ident[:, :])
                        if c % 4 == 3:
                            tr.then_inc(sem("xtm_turned"), 1)
                pe.wait_ge(sem("moe_chosen"), layer + 1)
                chosen = rt[:, 3, :, :]
                pe.matmul(bank[3][:, 0:16], strict[:, :], chosen[:, 0, :], start=True, stop=True)
                for i, last in enumerate((strict[:, :], ones[:, :])):
                    pe.matmul(bank[3][:, 16 + 16 * i:32 + 16 * i], ones[:, :], chosen[:, 0, :], start=True, stop=False)
                    mm = pe.matmul(bank[3][:, 16 + 16 * i:32 + 16 * i], last, chosen[:, 1, :], start=False, stop=True)
                mm.then_inc(sem("moe_places"), 1)
                def gather(pair):
                    for i in range(2):
                        for c in range(4):
                            for b in range(2):
                                mm = pe.matmul(bank[2 + i][:, c * 2 * PCAP:(c + 1) * 2 * PCAP],
                                               xtm[:, b, (4 * i + c) * P:(4 * i + c + 1) * P],
                                               SLOT1[:, b, bass.ds(2 * pair, 2), 0:PCAP], start=(b == 0), stop=(b == 1))
                        mm.then_inc(sem("gather_ready"), 1)

                pe.wait_ge(sem("moe_slots"), layer + 1)
                pe.wait_ge(sem("xtm_copied"), 4 * (layer + 1))
                gather(0)
                pe.wait_ge(sem("moe_weighted"), layer + 1)
                for q in range(8):
                    if q >= 4:
                        pe.wait_ge(sem("pt_copied"), 8 * layer + q - 3)
                    for b in range(2):
                        pe.transpose(bank[4 + q % 4][:, b * P:(b + 1) * P],
                                     WS[:, b, 2 * q:2 * q + 2, :].rearrange("p e s -> p (e s)"), ident[:, :])
                    pe.transpose(bank[4 + q % 4][:, NP:T], WS2[0:NB, 2 * q:2 * q + 2, :].rearrange("p e s -> p (e s)"),
                                 ident[0:NB, 0:NB]).then_inc(sem("pt_turned"), 1)
                pe.wait_ge(sem("pt_copied"), 8 * (layer + 1))
                pe.wait_ge(sem("decode_inputs"), layer + 1)
                with pe.Fori(0, PAIRS) as pair:
                    p = pair + PAIRS * layer
                    for i in range(2):
                        pe.wait_ge(sem(f"xg_copied{i}"), pair + (GATHERS * layer + 1))
                    pe.wait_ge(sem("moe_hidden"), p + 1)
                    for i in range(2):
                        for j in range(2):
                            n = n0 + 2 * i + j
                            pe.wait_ge(sem(f"slot_filled{n % SLOTS}"), 16 * pair + 16 * (n // SLOTS + 1))
                        for c in range(DC):
                            for j in range(2):
                                mm = pe.matmul(bank[i][64 * j:64 * j + 64, :], xg[:, j, c, :],
                                               slot(n0 + 2 * i + j, 8)[:, c, :], start=(c == 0), stop=(c == DC - 1))
                        mm.then_inc(sem(MOE_READ[i]), 1)
                    gather(pair + 1)
                    pe.wait_ge(sem("moe_hidden"), p + 2)
                    for f in range(4):
                        tr = pe.transpose(bank[0][:, f * P:(f + 1) * P], hid[:, f * P:(f + 1) * P], ident[:, :])
                    tr.then_inc(sem("moe_turned"), 1)
                    for i in range(2):
                        pe.wait_ge(sem(f"y_copied{i}"), p + 1)
                    for j in range(2):
                        n = n0 + 4 + j
                        pe.wait_ge(sem(f"slot_filled{n % SLOTS}"), 16 * pair + 16 * (n // SLOTS + 1))
                    pe.wait_ge(sem("hT_copied"), p + 1)
                    for i in range(2):
                        for f in range(4):
                            for j in range(2):
                                mm = pe.matmul(bank[4 + i][64 * j:64 * j + 64, :], hT[:, f * P + CAP * j:f * P + CAP * (j + 1)],
                                               slot(n0 + 4 + j, 4)[:, f, 512 * i:512 * (i + 1)],
                                               start=(f == 0), stop=(f == 3))
                    mm.then_inc(sem("moe_down"), 1)
                    for i in range(2):
                        pe.wait_ge(sem(f"y_copied{i}"), p + 2)
                    for c in range(DC):
                        pe.wait_ge(sem("moe_added"), DC * pair + (64 * layer + c + 1))
                        pe.matmul(bank[6 + c % 2][:, 0:T], Y[:, c * P:(c + 1) * P],
                                  PT[:, bass.ds(pair, 1), :].rearrange("p o t -> p (o t)"),
                                  start=True, stop=True).then_inc(sem("moe_back"), 1)
                for i in range(2):
                    pe.wait_ge(sem(f"xg_copied{i}"), GATHERS * (layer + 1))
                pe.wait_ge(sem("over_known"), layer + 1)
                flag = pe.value_load(over[0:1, 0:1], min_val=0, max_val=1)
                with pe.If(flag > 0):
                    pe.wait_ge(sem("over_gates"), layer + 1)
                    for b in range(2):
                        tr = pe.transpose(bank[7][0:16, b * P:(b + 1) * P], rt[:, 6, b, :], ident[:, :])
                    tr.then_inc(sem("over_turned"), 1)
                    with pe.Fori(0, E_N) as e:
                        x = E0 + e
                        pe.wait_ge(sem("over_sel"), x + 1)
                        pe.wait_ge(sem("over_gates_copied"), layer + 1)
                        pe.matmul(bank[6][:, 0:NP], osel, ogT, start=True, stop=True).then_inc(sem("over_spread"), 1)
                        for i in range(2):
                            pe.wait_ge(sem(f"over_filled{i}"), 16 * x + 16)
                        for f in range(4):
                            pe.wait_ge(sem("over_hidden"), 4 * x + f + 1)
                            for i in range(2):
                                for c in range(DC):
                                    mm = pe.matmul(bank[2 * i + f % 2][:, 0:NP], slot(i, 8)[:, c, f * P:(f + 1) * P],
                                                   xT[:, c, 0:NP], start=(c == 0), stop=(c == DC - 1))
                            mm.then_inc(sem("over_gu"), 1)
                        pe.wait_ge(sem("over_filled2"), 16 * x + 16)
                        pe.wait_ge(sem("over_hidden"), 4 * x + 6)
                        for d in range(DC):
                            pe.wait_ge(sem("over_added"), DC * x + d + 1)
                            for f in range(4):
                                mm = pe.matmul(bank[4 + d % 2][:, 0:NP], slot(2, 4)[:, f, d * P:(d + 1) * P],
                                               oh_[:, f, :], start=(f == 0), stop=(f == 3))
                            mm.then_inc(sem("over_down"), 1)
                        pe.wait_ge(sem("over_down"), DC * x + DC)
                        pe.sem_inc(sem("over_read"), 1)
                if layer == 0:
                    with pe.If(flag < 1):
                        for name, k in (("turned", 1), ("spread", E_N), ("gu", 4 * E_N), ("down", DC * E_N), ("read", E_N)):
                            pe.sem_inc(sem("over_" + name), k)

            def out_chunks(c):
                return A[:, (VV0 + c) if c < 8 else (XS0 + c - 8), :]

            out_project(AB_OUT0, 4, 16, out_chunks, "out0")
            norm_sums(0, xT)
            stage_end(pe, 4)
            experts(MOE0, 0)
            norm_sums(1, xacc)
            stage_end(pe, 5)
            project(C_IN0, 8, "in1", {})
            pe.wait_ge(sem("in1_copied"), 32)
            gated_heads(1, 8, 128, lambda h: A[:, h, :], lambda h: A[:, 32 + h, :], lambda h, j: A[:, 16 + h, :],
                        lambda: None)
            stage_end(pe, 6)
            out_project(C_OUT0, 2, 8, lambda c: A[:, 16 + c, :], "out1")
            norm_sums(2, xT)
            stage_end(pe, 7)
            experts(MOE1, 1)
            norm_sums(3, xacc)
            stage_end(pe, 8)
            for b, n in enumerate((P, P, NB)):
                for c in range(DC):
                    tr = pe.transpose(bank[2 * b + c // 4][0:n, (c % 4) * P:(c % 4 + 1) * P], xT[:, c, b * P:b * P + n],
                                      ident[:, :])
                    if c % 4 == 3:
                        tr.then_inc(sem("y_turned"), 1)

        @block.scalar
        def _(act):
            def load(dst, src, name):
                act.dma_start(dst, src, allow_slow_non_contiguous=True).then_inc(sem(name), 16)

            def rows(r, n, v):
                load(vrows[r:r + n, :], v, "vectors_loaded")

            rows(V_BGK, 4, b_gk2.rearrange("o (r p) -> (o r) p", p=P))
            rows(V_GLAN, 2, gla_norm_w.rearrange("o (r p) -> (o r) p", p=P))
            rows(V_SSDN, 8, ssd_norm_w.rearrange("o (r p) -> (o r) p", p=P))
            for r, v in ((V_LN1W, ln1_w), (V_LN1B, ln1_b), (V_LN2W, ln2_w), (V_LN2B, ln2_b)):
                rows(r, 16, v.rearrange("o (r p) -> (o r) p", p=P))
            rows(V_HGN, 1, hg_norm_w)
            rows(V_LB, 16, lower_bounds.rearrange("o (r p) -> (o r) p", p=P))
            load(crows[0:24, :], state_conv[0].rearrange("b j n -> (b j) n"), "vectors_loaded")
            load(crows[24:28, :], conv_w[0], "vectors_loaded")
            load(crows[28:29, :], conv_b, "vectors_loaded")
            load(wgk[:, :], w_gk2[0], "vectors_loaded")
            load(router[:, :, :], router_w.rearrange("(c p) e -> p c e", p=P), "vectors_loaded")
            load(wsmall[:, :, 0:16], w_in_ab[0, :, 3072:3088].rearrange("(c p) n -> p c n", p=P), "vectors_loaded")
            load(wsmall[:, :, 16:32], w_in_ab[0, :, 5648:5664].rearrange("(c p) n -> p c n", p=P), "vectors_loaded")
            load(small[:, 0:1], dt_bias.rearrange("o h -> h o"), "vectors_loaded")
            load(small[:, 1:2], a_log.rearrange("o h -> h o"), "vectors_loaded")
            load(rbias[:, :], router_bias.rearrange("(o e) -> o e", o=1).to_broadcast([P, E_N]), "vectors_loaded")
            for i in range(2):
                load(dskip[64 * i:64 * i + 64, :],
                     d_skip.rearrange("o (j i) -> o i j", i=2)[:, i, :].to_broadcast([64, 8]), "vectors_loaded")

            st = Steps(act, "act_steps")
            for c in range(0, DC, 2):
                act.wait_ge(sem("xT_turned"), c + 1)
                st.run(act.copy(xT[:, c, :], bank[c][:, 0:T]))
                act.sem_inc(sem("xT_copied"), 1)

            def exps(layer, h):
                hb, n = head_area(h), 4 * layer + h
                act.wait_ge(sem("heads_g_scanned"), n + 1)
                st.add(act.activation(hb["E2"], hb["E1"], ACT.Exp, scale=-1.0))
                st.add(act.activation(hb["EG"], hb["G"], ACT.Exp))
                st.add(act.activation(hb["EL"], hb["EL"], ACT.Exp))
                st.settle()
                act.activation(hb["E1"], hb["E1"], ACT.Exp).then_inc(sem("heads_exps"), 1)
                act.wait_ge(sem("heads_exps"), n + 1)

            def small_exp():
                act.wait_ge(sem("vectors_copied"), 1)
                act.activation(small[:, 2:3], small[:, 1:2], ACT.Exp).then_inc(sem("a_exp"), 1)

            def bound_tanh():
                act.wait_ge(sem("lb_diff"), 1)
                act.activation(lbc[:, 0, :], lbc[:, 2, :], ACT.Tanh, scale=0.5).then_inc(sem("lb_tanh"), 1)

            def conv_silu(i):
                act.wait_ge(sem("conv_done"), i + 1)
                act.wait_ge(sem("conv_turned"), i + 1)
                act.activation(A[:, XS0 + i, :], A[:, conv_place[i], :], ACT.Silu).then_inc(sem("conv_silu"), 1)

            def gate_logs():
                act.wait_ge(sem("gkz_ready"), 1)
                for out, z in ((gka[:, :, :], gkz[:, :, :]), (dtT[:, 1, :], dtT[:, 0, :])):
                    st.run(act.activation(out, z, ACT.Abs))
                    st.run(act.activation(out, out, ACT.Exp, scale=-1.0))
                    st.run(act.activation(out, out, ACT.Ln, bias=1.0))
                act.sem_inc(sem("gates_ln"), 1)

            def dt_exp():
                act.wait_ge(sem("dt_scanned"), 1)
                act.activation(dtT[:, 2, :], dtT[:, 1, :], ACT.Exp).then_inc(sem("dt_ready"), 1)

            def take(order, name, kinds, extra):
                for m, c in enumerate(order):
                    act.wait_ge(sem(name + "_ready"), m + 1)
                    func, scale = kinds(c)
                    act.activation(A[:, c, :], bank[m % 4][:, 0:T], func, scale=scale).then_inc(sem(name + "_copied"), 1)
                    for job in extra.get(m, []):
                        job()

            extra = {m: [lambda i=m - 12: conv_silu(i)] for m in range(12, 24)}
            extra[10] = [small_exp]
            extra[13].append(bound_tanh)
            extra[33] = [gate_logs]
            extra[37] = [dt_exp, lambda: exps(0, 0)]
            take(ab_order, "in0", lambda c: (ACT.Silu if G0 <= c < XS0 else ACT.Copy, 1.0), extra)

            def gated_heads(layer, nh, dv, between):
                H0, J = 4 * layer, dv // P
                per = 512 // dv

                def copy_rows(h):
                    hb = head_area(h)
                    act.wait_ge(sem("heads_v_turned"), (H0 + h) + 1)
                    for i in range(NC // per):
                        act.copy(hb["vtm"][0:C, per * i:per * (i + 1), 0:dv],
                                 bank[i][0:C, :].rearrange("p (c v) -> p c v", v=dv)).then_inc(sem("heads_kv_copied"), 1)
                    if per == NC:
                        act.sem_inc(sem("heads_kv_copied"), 1)
                    act.wait_ge(sem("heads_k_turned"), (H0 + h) + 1)
                    act.copy(hb["ktm"][0:C, :, :], bank[3][0:C, :].rearrange("p (c k) -> p c k", k=P)).then_inc(
                        sem("heads_kv_copied"), 1)

                def squares(h):
                    act.wait_ge(sem("heads_out_copied"), (H0 + h) + 1)
                    o = A[:, (VV0 + 2 * h if layer == 0 else 16 + h):(VV0 + 2 * h if layer == 0 else 16 + h) + J, :]
                    st.add(act.activation(SQ[:, 0:J, :], o, ACT.Square, scale=dv ** -0.5))
                    st.settle()
                    act.sem_inc(sem("heads_squared"), 1)

                exps(layer, 1)
                st.run(act.activation(decx[:, 0:nh, :], (gkg[:, 0:4, NP:T] if layer == 0 else A[:, 8:16, NP:T]), ACT.Exp))
                act.sem_inc(sem("dec_exps"), 1)
                copy_rows(0)
                between()
                for h in range(nh):
                    if h + 1 < nh:
                        copy_rows(h + 1)
                    squares(h)
                    if h + 2 < nh:
                        exps(layer, h + 2)
                gall = gkg[:, :, :] if layer == 0 else A[:, 8:16, :]
                act.wait_ge(sem("heads_normed"), H0 + nh)
                st.run(act.activation(gall, gall, ACT.Sqrt))
                act.sem_inc(sem("heads_roots"), 1)

            def copy_decays():
                act.wait_ge(sem("tm_ready"), 1)
                t = bank[7]
                st.add(act.copy(s_tm[:, :, :], t[:, 0:64].rearrange("p (a h) -> p a h", h=16)))
                st.add(act.copy(s_dd[0:NB, :], t[0:NB, 64:80]))
                st.add(act.copy(s_el[:, :, :], t[:, 80:112].rearrange("p (a h) -> p a h", h=16)))
                st.add(act.copy(s_egd[:, :, :], t[:, 112:240].rearrange("p (a h) -> p a h", h=16)))
                st.settle()
                act.sem_inc(sem("tm_copied"), 1)

            act.wait_ge(sem("in0_copied"), AB_CHUNKS)
            act.wait_ge(sem("conv_silu"), 12)
            stage_end(act, 1)
            gated_heads(0, 4, 256, copy_decays)
            stage_end(act, 2)
            act.wait_ge(sem("w_diff"), 1)
            st.add(act.activation(s_w[:, :, :], s_w[:, :, :], ACT.Exp))
            st.add(act.activation(s_el[:, :, :], s_el[:, :, :], ACT.Exp))
            st.settle()
            act.sem_inc(sem("w_exp"), 1)
            for g in range(2):
                act.wait_ge(sem("ssd_turned"), g + 1)
                if g == 1:
                    act.wait_ge(sem("ssd_normed"), 1)
                st.add(act.copy(s_btm[:, :, :], bank[0][:, 0:256].rearrange("p (c k) -> p c k", k=P)))
                st.add(act.copy(s_bdec[0:NB, :], bank[0][0:NB, 256:384]))
                st.settle()
                act.sem_inc(sem("ssd_btm_copied"), 1)
                for pr in range(4):
                    act.wait_ge(sem("ssd_diffs"), 4 * g + pr + 1)
                    for c in range(NCS):
                        e = s_E[:, c, 2 * pr:2 * pr + 2, :]
                        st.add(act.activation(e, e, ACT.Exp))
                st.settle()
                act.sem_inc(sem("ssd_exps"), 1)
                act.wait_ge(sem("ssd_update_ready"), 2 * g + 1)
                st.run(act.copy(s_S[:, 0, :], bank[7][:, :]))
                act.sem_inc(sem("ssd_state0"), 1)
                act.wait_ge(sem("eg_ready"), g + 1)
                st.run(act.copy(s_eg[:, :], bank[0][:, :]))
                act.sem_inc(sem("eg_copied"), 1)
                act.wait_ge(sem("ssd_gated"), g + 1)
                st.run(act.activation(s_sq[:, :, :], A[:, XS0 + 4 * g:XS0 + 4 * g + 4, :], ACT.Square,
                                      scale=NORM_SSD ** -0.5))
                act.sem_inc(sem("ssd_squared"), 1)
            act.wait_ge(sem("ssd_normed"), 2)
            st.run(act.activation(gkg[:, 0:2, :], gkg[:, 0:2, :], ACT.Sqrt))
            act.sem_inc(sem("ssd_roots"), 1)
            stage_end(act, 3)

            def squares(k):
                act.wait_ge(sem("norm_centered"), k + 1)
                st.run(act.activation(lnsq[:, :, :], xT[:, :, :], ACT.Square, scale=D ** -0.5))
                act.sem_inc(sem("norm_squares"), 1)
                act.wait_ge(sem("norm_variance"), k + 1)
                st.run(act.activation(lnr[:, :], lnr[:, :], ACT.Sqrt))
                act.sem_inc(sem("norm_roots"), 1)

            def experts(layer):
                E0 = E_N * layer
                act.wait_ge(sem("moe_logits"), layer + 1)
                act.wait_ge(sem("moe_score_cleared"), layer + 1)
                for b, n in enumerate((P, P, NB)):
                    st.add(act.activation(score[0:n, b, :], bank[2][0:n, 16 * b:16 * b + 16], ACT.Sigmoid))
                st.settle()
                act.sem_inc(sem("moe_scores"), 1)
                for i in range(4):
                    act.wait_ge(sem("xtm_turned"), 4 * layer + i + 1)
                    act.copy(xtm[:, i // 2, (i % 2) * 512:(i % 2 + 1) * 512], bank[4 + i][:, :]).then_inc(
                        sem("xtm_copied"), 1)
                gathered(act, act.copy, 0, GATHERS * layer)
                for q in range(8):
                    act.wait_ge(sem("pt_turned"), 8 * layer + q + 1)
                    act.copy(PT[:, q, :], bank[4 + q % 4][:, 0:T]).then_inc(sem("pt_copied"), 1)
                if layer == 0:
                    act.sem_inc(sem("y_copied0"), 1)
                with act.Fori(0, PAIRS) as pair:
                    p = pair + PAIRS * layer
                    act.wait_ge(sem("moe_gate"), p + 1)
                    act.activation(hid, bank[0][:, :], ACT.Silu).then_inc(sem("moe_silu"), 1)
                    gathered(act, act.copy, 0, pair + (GATHERS * layer + 1))
                    act.wait_ge(sem("moe_turned"), p + 1)
                    act.copy(hT, bank[0][:, :]).then_inc(sem("hT_copied"), 1)
                    act.wait_ge(sem("moe_down"), p + 1)
                    act.copy(Y[:, 0:512], bank[4][:, :]).then_inc(sem("y_copied0"), 1)
                act.wait_ge(sem("over_known"), layer + 1)
                flag = act.value_load(over[0:1, 0:1], min_val=0, max_val=1)
                with act.If(flag > 0):
                    with act.Fori(0, E_N) as e:
                        x = E0 + e
                        act.wait_ge(sem("over_spread"), x + 1)
                        act.wait_ge(sem("over_hidden"), 4 * x + 2)
                        act.copy(ogb, bank[6][:, 0:NP]).then_inc(sem("over_spread_copied"), 1)
                        for f in range(4):
                            act.wait_ge(sem("over_gu"), 4 * x + f + 1)
                            act.wait_ge(sem("over_hidden"), 4 * x + f + 1)
                            act.activation(og[:, f % 2, :], bank[f % 2][:, 0:NP], ACT.Silu).then_inc(sem("over_silu"), 1)
                if layer == 0:
                    with act.If(flag < 1):
                        act.sem_inc(sem("over_spread_copied"), E_N)
                        act.sem_inc(sem("over_silu"), 4 * E_N)

            squares(0)
            stage_end(act, 4)
            experts(0)
            squares(1)
            stage_end(act, 5)

            def forget_logs():
                act.wait_ge(sem("hg_forget"), 1)
                act.activation(A[:, 8:16, :], A[:, 8:16, :], ACT.Ln).then_inc(sem("hg_log"), 1)

            def c_kind(c):
                group = c // 8
                return (ACT.Silu, 1.0) if group in (0, 3) else (ACT.Tanh, 0.5) if group == 1 else (ACT.Copy, 1.0)

            take(c_order, "in1", c_kind, {11: [forget_logs], 19: [lambda: exps(1, 0)]})
            gated_heads(1, 8, 128, lambda: None)
            stage_end(act, 6)
            squares(2)
            stage_end(act, 7)
            experts(1)
            squares(3)
            stage_end(act, 8)
            yrows = area(0, 3, D)
            for b, n in enumerate((P, P, NB)):
                for i in range(2):
                    act.wait_ge(sem("y_turned"), 2 * b + i + 1)
                    st.run(act.copy(yrows[0:n, b, i * 512:(i + 1) * 512], bank[2 * b + i][0:n, :]))
                if b < 2:
                    act.dma_start(y_prompt[0, b * P:(b + 1) * P, :], yrows[:, b, :]).then_inc(sem("y_stored"), 16)
                else:
                    act.dma_start(y_sample.rearrange("b o d -> (b o) d"), yrows[0:NB, 2, :]).then_inc(sem("y_stored"), 16)
            act.wait_ge(sem("y_stored"), 48)

        @block.vector
        def _(dve):
            st = Steps(dve, "dve_steps")

            def tt(out, a, b, op):
                st.run(dve.tensor_tensor(out, a, b, op))

            for c in range(1, DC, 2):
                dve.wait_ge(sem("xT_turned"), c + 1)
                st.run(dve.tensor_copy(xT[:, c, :], bank[c][:, 0:T]))
                dve.sem_inc(sem("xT_copied"), 1)
            dve.wait_ge(sem("vectors_turned"), 1)
            st.add(dve.tensor_copy(cols[:, :], bank[4][:, 0:V_N]))
            st.add(dve.tensor_copy(convc[:, :, :], bank[4][:, V_N:V_N + 348].rearrange("p (m r) -> p m r", r=29)))
            st.settle()
            dve.sem_inc(sem("vectors_copied"), 1)
            dve.tensor_tensor(lbc[:, 2, :], cols[:, V_LB + 8:V_LB + 16], cols[:, V_LB:V_LB + 8], ALU.subtract
                              ).then_inc(sem("lb_diff"), 1)

            for m in range(12):
                x, acc, cc = A[:, XS0 + m, :], A[:, conv_place[m], :], convc[:, m, :]
                dve.wait_ge(sem("in0_copied"), m + 1)
                st.run(dve.tensor_scalar(acc, x, cc[:, 27:28], cc[:, 28:29], ALU.mult, ALU.add))
                for j in range(3):
                    sh = 3 - j
                    old = cc[:, 0:24].rearrange("p (b j) -> p b j", j=3)[:, :, j]
                    st.add(dve.scalar_tensor_tensor(acc[:, sh:NP], x[:, 0:NP - sh], cc[:, 24 + j:25 + j],
                                                    acc[:, sh:NP], ALU.mult, ALU.add))
                    st.add(dve.scalar_tensor_tensor(acc[:, NP:T], old, cc[:, 24 + j:25 + j], acc[:, NP:T],
                                                    ALU.mult, ALU.add))
                    st.settle()
                dve.sem_inc(sem("conv_done"), 1)
            dve.wait_ge(sem("conv_turned"), 12)
            for i in range(3):
                dve.tensor_copy(convout[0:16, i * 512:(i + 1) * 512], bank[5 + i][0:16, :]).then_inc(sem("convout_ready"), 1)
            dve.wait_ge(sem("lb_tanh"), 1)
            st.run(dve.tensor_scalar(lbc[:, 1, :], lbc[:, 0, :], -0.25, 0.25, ALU.mult, ALU.add))
            dve.wait_ge(sem("a_exp"), 1)
            st.run(dve.tensor_scalar(small[:, 2:3], small[:, 2:3], -1.0, None, ALU.mult))
            dve.wait_ge(sem("small_ready"), 2)
            dve.tensor_copy(lrT[:, :], bank[4][0:16, 0:T]).then_inc(sem("small_copied"), 1)
            dve.tensor_scalar(dtT[:, 0, :], bank[5][0:16, 0:T], small[:, 0:1], None, ALU.add).then_inc(sem("small_copied"), 1)
            for h in range(4):
                dve.wait_ge(sem("gk_ready"), h + 1)
                st.add(dve.tensor_scalar(gkz[:, h, :], bank[4 + h][:, 0:T], cols[:, V_BGK + h:V_BGK + h + 1], None, ALU.add))
            st.settle()
            dve.wait_ge(sem("small_copied"), 2)
            dve.sem_inc(sem("gkz_ready"), 1)
            dve.wait_ge(sem("gates_ln"), 1)
            st.run(dve.tensor_scalar(gkz[:, :, :], gkz[:, :, :], 0.0, 1.0 / 16.0, ALU.min, ALU.mult))
            st.run(dve.scalar_tensor_tensor(gkg[:, :, :], gka[:, :, :], -1.0 / 16.0, gkz[:, :, :], ALU.mult, ALU.add))
            st.run(dve.scalar_tensor_tensor(dtT[:, 0, :], dtT[:, 0, :], 0.0, dtT[:, 1, :], ALU.max, ALU.add))
            st.run(dve.tensor_scalar(dtT[:, 2, :], dtT[:, 0, :], small[:, 2:3], None, ALU.mult))
            for c in range(NCS):
                s = slice(c * CS, (c + 1) * CS)
                st.add(dve.tensor_tensor_scan(dtT[:, 1, s], ones[0:16, 0:CS], dtT[:, 2, s], 0.0, ALU.mult, ALU.add))
            st.add(dve.tensor_copy(dtT[:, 1, NP:T], dtT[:, 2, NP:T]))
            st.settle()
            dve.sem_inc(sem("dt_scanned"), 1)

            def gated_heads(layer, nh, dv, qa, ka, ga, oa, scale, start):
                H0, J = 4 * layer, dv // P
                per = 512 // dv
                F = NB // per
                F0 = 16 * layer
                v4 = lambda t: t.rearrange("p (c t) -> p c t", t=C)

                def prep(h):
                    hb = head_area(h)
                    st.run(dve.tensor_tensor_scan(hb["G"], restart[:, :], ga(h)[:, 0:NP], 0.0, ALU.mult, ALU.add))
                    G4 = v4(hb["G"])
                    st.add(dve.tensor_tensor(v4(hb["E1"]), G4, G4[:, :, C // 2 - 1:C // 2].to_broadcast([P, NC, C]),
                                             ALU.subtract))
                    st.add(dve.tensor_tensor(v4(hb["EL"]), G4[:, :, C - 1:C].to_broadcast([P, NC, C]), G4, ALU.subtract))
                    st.settle()
                    dve.sem_inc(sem("heads_g_scanned"), 1)

                def prods(h):
                    hb = head_area(h)
                    dve.wait_ge(sem("heads_exps"), (H0 + h) + 1)
                    q, k = qa(h), ka(h)
                    st.add(dve.scalar_tensor_tensor(hb["E1"], q[:, 0:NP], scale, hb["E1"], ALU.mult, ALU.mult))
                    st.add(dve.tensor_tensor(hb["E2"], k[:, 0:NP], hb["E2"], ALU.mult))
                    st.add(dve.tensor_tensor(hb["EL"], k[:, 0:NP], hb["EL"], ALU.mult))
                    st.add(dve.scalar_tensor_tensor(hb["QD"], q[:, 0:NP], scale, hb["EG"], ALU.mult, ALU.mult))
                    st.settle()
                    dve.sem_inc(sem("heads_prepared"), 1)

                def decode_rows(h):
                    hb, n = head_area(h), H0 + h
                    st.add(dve.tensor_scalar(QS[:, h % 2, :], qa(h)[:, NP:T], scale, None, ALU.mult))
                    dve.wait_ge(sem("heads_v_turned"), n + 1)
                    st.add(dve.tensor_copy(hb["vdec"][:, 0:dv], bank[2][DR:DR + NB, P:P + dv]))
                    st.add(dve.tensor_tensor(
                        hb["kmask"], bank[2][DR:DR + NB, 0:P].rearrange("p (o k) -> p o k", o=1).to_broadcast([NB, NB, P]),
                        ident[DR:DR + NB, DR:DR + NB].rearrange("p (b o) -> p b o", o=1).to_broadcast([NB, NB, P]), ALU.mult))
                    st.settle()
                    dve.sem_inc(sem("heads_kmask_ready"), 1)

                def mask(h):
                    dve.wait_ge(sem("heads_scores_ready"), (H0 + h) + 1)
                    st.run(dve.tensor_tensor(v4(SC[0:C, h % 2, :]), v4(bank[4][0:C, 0:NP]),
                                             causal[0:C, 0:C].rearrange("p (o t) -> p o t", o=1).to_broadcast([C, NC, C]),
                                             ALU.mult))
                    dve.sem_inc(sem("heads_scores_masked"), 1)

                def states(h):
                    hb, n = head_area(h), H0 + h
                    dve.wait_ge(sem("heads_updates_ready"), n + 1)
                    if h >= 2:
                        dve.wait_ge(sem(f"heads_prompt_state_stored{h % 2}"), 16 * (n // 2))
                    for c in range(NC):
                        u = bank[c // per][:, (c % per) * dv:(c % per + 1) * dv]
                        if c == 0:
                            st.run(dve.tensor_copy(ST[:, h % 2, 0, 0:dv], u))
                        else:
                            st.run(dve.scalar_tensor_tensor(ST[:, h % 2, c, 0:dv], ST[:, h % 2, c - 1, 0:dv],
                                                            hb["EG"][:, (c + 1) * C - 1:(c + 1) * C], u, ALU.mult, ALU.add))
                    dve.sem_inc(sem("heads_states_ready"), 1)

                def decode(h, half):
                    if h == 0:
                        slot_ready(dve, (HG_ST0 if layer else GLA_ST0) + half)
                    for i in range(F // 2 * half, F // 2 * (half + 1)):
                        dve.wait_ge(sem("heads_dec_update_ready"), F0 + F * h + i + 1)
                        for b in range(per * i, per * (i + 1)):
                            s = decode_state(layer, h, b)
                            up = dve.scalar_tensor_tensor(s, s, decx[:, h, b:b + 1],
                                                          bank[6 + i % 2][:, (b % per) * dv:(b % per + 1) * dv],
                                                          ALU.mult, ALU.add)
                        up.then_inc(sem("heads_dec_updated"), 1)

                def finish(h):
                    dve.wait_ge(sem("heads_out_ready"), (H0 + h) + 1)
                    o = oa(h)
                    st.add(dve.tensor_copy(o[:, :, 0:NP], bank[5][:, 0:J * NP].rearrange("p (j t) -> p j t", j=J)))
                    st.add(dve.tensor_copy(o[:, :, NP:T], bank[4][:, 256:256 + J * NB].rearrange("p (j b) -> p j b", j=J)))
                    st.settle()
                    dve.sem_inc(sem("heads_out_copied"), 1)

                def norm(h):
                    dve.wait_ge(sem("heads_square_sums"), (H0 + h) + 1)
                    st.run(dve.tensor_scalar(ga(h), bank[2][:, 0:T], EPS, None, ALU.add))
                    dve.sem_inc(sem("heads_normed"), 1)

                prep(0)
                start()
                prods(0)
                prep(1)
                decode_rows(0)
                mask(0)
                dve.wait_ge(sem("dec_exps"), layer + 1)
                for h in range(nh):
                    states(h)
                    decode(h, 0)
                    if h + 1 < nh:
                        prods(h + 1)
                        decode_rows(h + 1)
                        mask(h + 1)
                    decode(h, 1)
                    finish(h)
                    if h + 2 < nh:
                        prep(h + 2)
                    norm(h)
                dve.wait_ge(sem("heads_roots"), layer + 1)
                dve.wait_ge(sem("heads_gated"), layer + 1)
                gall = gkg[:, :, :] if layer == 0 else A[:, 8:16, :]
                st.run(dve.reciprocal(gall, gall))
                for h in range(nh):
                    st.add(dve.tensor_tensor(oa(h), oa(h), ga(h).rearrange("p (o t) -> p o t", o=1).to_broadcast([P, J, T]),
                                             ALU.mult))
                st.settle()

            gated_heads(0, 4, 256, lambda h: A[:, Q0 + h, :], lambda h: A[:, K0 + h, :], lambda h: gkg[:, h, :],
                        lambda h: A[:, VV0 + 2 * h:VV0 + 2 * h + 2, :], HEAD_SCALE, lambda: stage_end(dve, 1))
            stage_end(dve, 2)

            st.run(dve.tensor_tensor(s_w[:, :, :], s_el[:, :, :], s_tm[:, 0:2, :], ALU.subtract))
            dve.sem_inc(sem("w_diff"), 1)
            dve.wait_ge(sem("w_exp"), 1)
            st.run(dve.tensor_tensor(s_w[:, :, :], s_w[:, :, :], s_tm[:, 2:4, :], ALU.mult))
            for g in range(2):
                hs = slice(8 * g, 8 * g + 8)

                def per_head(a, n, w=64):
                    return a.rearrange("p (h o) -> p h o", o=1).to_broadcast([n, 8, w])
                h8 = lambda t: t.rearrange("p (h v) -> p h v", h=8)
                dve.wait_ge(sem("ssd_turned"), g + 1)
                for c in range(NCS):
                    xp = h8(bank[1 + c][:, :])
                    st.add(dve.tensor_tensor(h8(s_xdt[:, c, :]), xp, per_head(s_tm[:, 2 + c, hs], P), ALU.mult))
                    st.add(dve.tensor_tensor(h8(s_xw[:, c, :]), xp, per_head(s_w[:, c, hs], P), ALU.mult))
                st.add(dve.tensor_tensor(h8(s_xdec[0:NB, :]), h8(bank[3][0:NB, :]), per_head(s_dd[0:NB, hs], NB), ALU.mult))
                st.add(dve.tensor_tensor(s_g0[:, :, :], bank[4][:, 0:256].rearrange("p (c t) -> p c t", t=P),
                                         causal[:, :].rearrange("p (o t) -> p o t", o=1).to_broadcast([P, NCS, P]), ALU.mult))
                dve.wait_ge(sem("ssd_btm_copied"), g + 1)
                st.add(dve.tensor_tensor(
                    s_bmask[0:NB, :, :], s_bdec[0:NB, :].rearrange("p (o k) -> p o k", o=1).to_broadcast([NB, NB, P]),
                    ident[0:NB, 0:NB].rearrange("p (b o) -> p b o", o=1).to_broadcast([NB, NB, P]), ALU.mult))
                st.settle()
                dve.sem_inc(sem("ssd_tm_copied"), 1)
                dve.sem_inc(sem("bmask_ready"), 1)
                for pr in range(4):
                    dve.wait_ge(sem("gbc_ready"), 4 * g + pr + 1)
                    for i in range(2):
                        for c in range(NCS):
                            hh = 2 * pr + i
                            st.add(dve.tensor_scalar(s_E[:, c, hh, :], bank[5 + pr % 2][:, i * NP + c * CS:i * NP + (c + 1) * CS],
                                                     s_tm[:, c, 8 * g + hh:8 * g + hh + 1], 0.0, ALU.subtract, ALU.min))
                    st.settle()
                    dve.sem_inc(sem("ssd_diffs"), 1)
                dve.wait_ge(sem("ssd_exps"), g + 1)
                for c in range(NCS):
                    st.run(dve.tensor_tensor(s_E[:, c, :, :], s_E[:, c, :, :],
                                             s_g0[:, c, :].rearrange("p (o t) -> p o t", o=1).to_broadcast([P, 8, P]), ALU.mult))
                    dve.sem_inc(sem("ssd_scores"), 1)
                dve.wait_ge(sem("ssd_state0"), g + 1)
                if g == 1:
                    dve.wait_ge(sem("ssd_p_stored"), 16)
                st.run(dve.tensor_tensor(h8(s_S[:, 1, :]), h8(s_S[:, 0, :]), per_head(s_el[:, 1, hs], P), ALU.mult))
                dve.wait_ge(sem("ssd_update_ready"), 2 * g + 2)
                st.run(dve.tensor_tensor(s_S[:, 1, :], s_S[:, 1, :], bank[7][:, :], ALU.add))
                dve.sem_inc(sem("ssd_prompt_state"), 1)
                for b in range(NB):
                    dve.wait_ge(sem("ssd_dec_ready"), NB * g + b + 1)
                    s = ssd_state(g, b)
                    dve.tensor_tensor(s, s, h8(bank[5 + b % 2][:, :]), ALU.add).then_inc(sem("ssd_dec_updated"), 1)
                dve.wait_ge(sem("eg_copied"), g + 1)
                dve.wait_ge(sem("ssd_inter"), g + 1)
                st.run(dve.tensor_tensor(s_yi[:, :], s_eg[:, :], bank[3][:, :], ALU.mult))
                dve.wait_ge(sem("ssd_state_used"), g + 1)
                for j in range(4):
                    y = A[:, XS0 + 4 * g + j, :]
                    dk = dskip[:, 4 * g + j:4 * g + j + 1]
                    st.add(dve.scalar_tensor_tensor(y[:, 0:NP], y[:, 0:NP], dk, bank[1 + j // 2][:, (j % 2) * NP:(j % 2 + 1) * NP],
                                                    ALU.mult, ALU.add))
                    st.add(dve.scalar_tensor_tensor(y[:, NP:T], y[:, NP:T], dk, bank[4][:, 256 + j * NB:256 + (j + 1) * NB],
                                                    ALU.mult, ALU.add))
                st.settle()
                ys = A[:, XS0 + 4 * g:XS0 + 4 * g + 4, :]
                st.run(dve.tensor_tensor(ys[:, :, CS:NP], ys[:, :, CS:NP], s_yi[:, :].rearrange("p (j t) -> p j t", t=P), ALU.add))
                st.run(dve.tensor_tensor(ys, ys, A[:, Z0 + 4 * g:Z0 + 4 * g + 4, :], ALU.mult))
                dve.sem_inc(sem("ssd_gated"), 1)
                dve.wait_ge(sem("ssd_square_sums"), g + 1)
                st.run(dve.tensor_scalar(gkg[:, g, :], bank[7][:, 0:T], EPS, None, ALU.add))
                dve.sem_inc(sem("ssd_normed"), 1)
            dve.wait_ge(sem("ssd_roots"), 1)
            st.run(dve.reciprocal(gkg[:, 0:2, :], gkg[:, 0:2, :]))
            for j in range(8):
                w = cols[:, V_SSDN + j:V_SSDN + j + 1]
                st.add(dve.scalar_tensor_tensor(A[:, XS0 + j, :], A[:, XS0 + j, :], w, gkg[:, j // 4, :], ALU.mult, ALU.mult))
            st.settle()
            stage_end(dve, 3)

            def add_out(tag):
                for m in range(DC):
                    dve.wait_ge(sem(tag + "_ready"), m + 1)
                    st.add(dve.scalar_tensor_tensor(xT[:, m, :], xT[:, m, :], ALPHA, bank[m][:, 0:T], ALU.mult, ALU.add))
                st.settle()

            def layer_norm(k, src, wcol, bcol):
                dve.sem_inc(sem("norm_residual"), 1)
                dve.wait_ge(sem("norm_sum"), 2 * k + 1)
                st.run(dve.tensor_scalar(lnm[:, :], bank[0][:, 0:T], 1.0 / D, None, ALU.mult))
                bc = lambda t: t.rearrange("p (o t) -> p o t", o=1).to_broadcast([P, DC, T])
                st.run(dve.tensor_tensor(xT[:, :, :], src[:, :, :], bc(lnm[:, :]), ALU.subtract))
                dve.sem_inc(sem("norm_centered"), 1)
                dve.wait_ge(sem("norm_sum"), 2 * k + 2)
                st.run(dve.tensor_scalar(lnr[:, :], bank[1][:, 0:T], EPS, None, ALU.add))
                dve.sem_inc(sem("norm_variance"), 1)
                dve.wait_ge(sem("norm_roots"), k + 1)
                st.run(dve.reciprocal(lnr[:, :], lnr[:, :]))
                st.run(dve.tensor_tensor(xT[:, :, :], xT[:, :, :], bc(lnr[:, :]), ALU.mult))
                for c in range(DC):
                    st.add(dve.tensor_scalar(xT[:, c, :], xT[:, c, :], cols[:, wcol + c:wcol + c + 1],
                                             cols[:, bcol + c:bcol + c + 1], ALU.mult, ALU.add))
                st.settle()

            def pick_first(out, val, mx, sel, width):
                b3 = lambda t: t.to_broadcast([P, 3, width])
                ix = idx16[:, 0:width].rearrange("p (o e) -> p o e", o=1).to_broadcast([P, 3, width])
                st.run(dve.tensor_reduce(mx, val, AX, ALU.max))
                st.run(dve.tensor_tensor(sel, val, b3(mx), ALU.is_equal))
                st.run(dve.tensor_tensor(sel, sel, ix, ALU.mult))
                st.run(dve.tensor_reduce(mx, sel, AX, ALU.max))
                st.run(dve.tensor_tensor(out, sel, b3(mx), ALU.is_equal))

            def route(layer):
                tag = "moe"
                st.add(dve.memset(SLOT1[:, :, E_N:E_N + 2, :], 0.0))
                st.run(dve.memset(score[:, :, :], 0.5))
                dve.sem_inc(sem("moe_score_cleared"), 1)
                dve.wait_ge(sem("moe_scores"), layer + 1)
                sel, t1, t2, oh = (rt[:, i, :, :] for i in range(4))
                mx = rt[:, 4, :, 0:1]
                grp = rt[:, 5, :, 0:4]
                tt(sel, score[:, :, :], rbias[:, :].rearrange("p (o e) -> p o e", o=1).to_broadcast([P, 3, E_N]), ALU.add)
                s4 = sel.rearrange("p b (g i) -> p b g i", i=4)
                v = [s4[:, :, :, i] for i in range(4)]
                a1 = t1.rearrange("p b (g i) -> p b g i", i=4)
                w = [a1[:, :, :, i] for i in range(4)]
                tt(w[0], v[0], v[1], ALU.max)
                tt(w[1], v[0], v[1], ALU.min)
                tt(w[2], v[2], v[3], ALU.max)
                tt(w[3], v[2], v[3], ALU.min)
                a2 = t2.rearrange("p b (g i) -> p b g i", i=4)
                u = [a2[:, :, :, i] for i in range(4)]
                tt(u[0], w[0], w[2], ALU.max)
                tt(u[1], w[0], w[2], ALU.min)
                tt(u[2], w[1], w[3], ALU.max)
                tt(u[3], u[1], u[2], ALU.max)
                tt(grp, u[0], u[3], ALU.add)
                pick_first(rt[:, 6, :, 0:4], grp, mx, rt[:, 7, :, 0:4], 4)
                gsel = rt[:, 6, :, 0:4]
                for i in range(4):
                    tt(w[i], v[i], gsel, ALU.mult)
                st.run(dve.tensor_scalar(rt[:, 7, :, 0:4], gsel, -1.0, BIG, ALU.add, ALU.mult))
                for i in range(4):
                    tt(w[i], w[i], rt[:, 7, :, 0:4], ALU.add)
                pick_first(oh, t1, mx, t2, E_N)
                st.run(dve.scalar_tensor_tensor(t1, oh, -2.0 * BIG, t1, ALU.mult, ALU.add))
                pick_first(rt[:, 7, :, :], t1, mx, t2, E_N)
                tt(oh, oh, rt[:, 7, :, :], ALU.add)
                dve.sem_inc(sem("moe_chosen"), 1)
                tt(gate[:, :, :], score[:, :, :], oh, ALU.mult)
                st.run(dve.tensor_reduce(mx, gate[:, :, :], AX, ALU.add))
                st.run(dve.reciprocal(mx, mx))
                tt(gate[:, :, :], gate[:, :, :], mx.to_broadcast([P, 3, E_N]), ALU.mult)
                dve.wait_ge(sem("moe_places"), layer + 1)
                place = rt[:, 7, 0:2, :]
                psum = bank[3][:, 0:32].rearrange("p (b e) -> p b e", e=E_N)
                st.run(dve.scalar_tensor_tensor(place, psum, 1.0, oh[:, 0:2, :], ALU.add, ALU.mult))
                st.run(dve.tensor_reduce(mx[:, 0, :], bank[3][:, 32:48], AX, ALU.max))
                st.run(dve.tensor_scalar(over[:, :], mx[:, 0, :], PLIM + 0.5, None, ALU.is_gt))
                dve.sem_inc(sem("over_known"), 1)
                st.run(dve.tensor_scalar(place, place, -1.0, None, ALU.add))
                for b in range(2):
                    st.add(dve.tensor_tensor(
                        SLOT1[:, b, 0:E_N, :], iota[:, :].rearrange("p (o s) -> p o s", o=1).to_broadcast([P, E_N, CAP]),
                        place[:, b, :].rearrange("p (e o) -> p e o", o=1).to_broadcast([P, E_N, CAP]), ALU.is_equal))
                st.settle()
                dve.sem_inc(sem("moe_slots"), 1)

                def over_gates():
                    st.run(dve.tensor_scalar(t1[:, 0:2, :], place, PLIM - 0.5, None, ALU.is_gt))
                    tt(rt[:, 6, 0:2, :], t1[:, 0:2, :], gate[:, 0:2, :], ALU.mult)

                def weigh(b):
                    st.run(dve.tensor_tensor(
                        WS[:, b, :, :], SLOT1[:, b, 0:E_N, :],
                        gate[:, b, :].rearrange("p (e o) -> p e o", o=1).to_broadcast([P, E_N, CAP]), ALU.mult))
                    st.add(dve.memset(WS[:, b, :, PLIM:CAP], 0.0))

                def weigh_decode():
                    st.run(dve.memset(WS2[0:NB, :, :], 0.0))
                    st.run(dve.tensor_tensor(
                        WS2[0:NB, :, PCAP:CAP],
                        ident[0:NB, 0:NB].rearrange("p (o s) -> p o s", o=1).to_broadcast([NB, E_N, NB]),
                        gate[0:NB, 2, :].rearrange("p (e o) -> p e o", o=1).to_broadcast([NB, E_N, NB]), ALU.mult))
                    dve.sem_inc(sem("moe_weighted"), 1)

                weigh(0)
                weigh(1)
                st.settle()
                weigh_decode()
                gathered(dve, dve.tensor_copy, 1, GATHERS * layer)
                over_gates()
                st.settle()

            def experts(layer):
                E0 = E_N * layer
                if layer == 0:
                    dve.sem_inc(sem("moe_hidden"), 1)
                    dve.sem_inc(sem("moe_added"), 2)
                    dve.sem_inc(sem("y_copied1"), 1)
                    dve.sem_inc(sem("over_hidden"), 2)
                    dve.sem_inc(sem("over_added"), 2)
                dve.wait_ge(sem("moe_residual"), layer + 1)
                with dve.Fori(0, PAIRS) as pair:
                    p = pair + PAIRS * layer
                    dve.wait_ge(sem("moe_silu"), p + 1)
                    dve.wait_ge(sem("moe_up"), p + 1)
                    dve.tensor_tensor(hid, hid, bank[1][:, :], ALU.mult).then_inc(sem("moe_hidden"), 1)
                    gathered(dve, dve.tensor_copy, 1, pair + (GATHERS * layer + 1))
                    dve.wait_ge(sem("moe_down"), p + 1)
                    dve.tensor_copy(Y[:, 512:1024], bank[5][:, :]).then_inc(sem("y_copied1"), 1)
                    dve.wait_ge(sem("moe_added"), DC * pair + 64 * layer + 2)
                    for c in range(DC):
                        dve.wait_ge(sem("moe_back"), DC * pair + (64 * layer + c + 1))
                        dve.tensor_tensor(xacc[:, c, :], xacc[:, c, :], bank[6 + c % 2][:, 0:T], ALU.add).then_inc(
                            sem("moe_added"), 1)
                dve.wait_ge(sem("moe_added"), 64 * (layer + 1) + 2)
                flag = dve.value_load(over[0:1, 0:1], min_val=0, max_val=1)
                with dve.If(flag > 0):
                    dve.sem_inc(sem("over_gates"), 1)
                    dve.wait_ge(sem("over_turned"), layer + 1)
                    dve.tensor_copy(ogT, bank[7][0:16, 0:NP]).then_inc(sem("over_gates_copied"), 1)
                    with dve.Fori(0, E_N) as e:
                        x = E0 + e
                        dve.tensor_copy(osel, ident[0:16, bass.ds(e, 1)].to_broadcast([16, P])).then_inc(sem("over_sel"), 1)
                        dve.wait_ge(sem("over_spread_copied"), x + 1)
                        for f in range(4):
                            dve.wait_ge(sem("over_silu"), 4 * x + f + 1)
                            dve.tensor_tensor(og[:, f % 2, :], og[:, f % 2, :], ogb, ALU.mult).then_inc(
                                sem("over_weighted"), 1)
                            dve.wait_ge(sem("over_weighted"), 4 * x + f + 1)
                            dve.tensor_tensor(oh_[:, f, :], og[:, f % 2, :], bank[2 + f % 2][:, 0:NP], ALU.mult).then_inc(
                                sem("over_hidden"), 1)
                        dve.wait_ge(sem("over_added"), DC * x + 2)
                        for d in range(DC):
                            dve.wait_ge(sem("over_down"), DC * x + d + 1)
                            dve.tensor_tensor(xacc[:, d, 0:NP], xacc[:, d, 0:NP], bank[4 + d % 2][:, 0:NP], ALU.add
                                              ).then_inc(sem("over_added"), 1)
                    dve.wait_ge(sem("over_added"), DC * E_N * (layer + 1) + 2)
                if layer == 0:
                    with dve.If(flag < 1):
                        for name, k in (("gates", 1), ("gates_copied", 1), ("sel", E_N), ("weighted", 4 * E_N),
                                        ("hidden", 4 * E_N), ("added", DC * E_N)):
                            dve.sem_inc(sem("over_" + name), k)

            add_out("out0")
            layer_norm(0, xT, V_LN1W, V_LN1B)
            stage_end(dve, 4)
            route(0)
            experts(0)
            layer_norm(1, xacc, V_LN2W, V_LN2B)
            stage_end(dve, 5)
            for h in range(8):
                dve.wait_ge(sem("in1_copied"), h + 1)
                k = A[:, 32 + h, :]
                st.run(dve.tensor_scalar(k, A[:, 8 + h, :], -1.0, 1.0, ALU.mult, ALU.add))
                st.run(dve.tensor_scalar(k, k, lbc[:, 1, h:h + 1], None, ALU.mult))
                st.run(dve.tensor_scalar(A[:, 8 + h, :], k, -1.0, 1.0, ALU.mult, ALU.add))
            dve.sem_inc(sem("hg_forget"), 1)
            dve.wait_ge(sem("hg_log"), 1)
            gated_heads(1, 8, 128, lambda h: A[:, h, :], lambda h: A[:, 32 + h, :], lambda h: A[:, 8 + h, :],
                        lambda h: A[:, 16 + h:17 + h, :], 1.0, lambda: dve.wait_ge(sem("in1_copied"), 16))
            stage_end(dve, 6)
            add_out("out1")
            layer_norm(2, xT, V_LN1W + 8, V_LN1B + 8)
            stage_end(dve, 7)
            route(1)
            experts(1)
            layer_norm(3, xacc, V_LN2W + 8, V_LN2B + 8)
            stage_end(dve, 8)


_INS = ['x_prompt', 'x_sample', 'state_gla', 'state_ssd', 'state_conv', 'state_hgrn', 'w_in_ab', 'w_gk2', 'b_gk2',
        'gla_norm_w', 'conv_w', 'conv_b', 'dt_bias', 'a_log', 'd_skip', 'ssd_norm_w', 'w_out_ab', 'w_in_c',
        'lower_bounds', 'hg_norm_w', 'w_out_c', 'router_w', 'router_bias', 'w_gate', 'w_up', 'w_down', 'ln1_w',
        'ln1_b', 'ln2_w', 'ln2_b']
_OUTS = [(1, 256, 1024), (8, 1, 1024), (1, 1, 4, 128, 256), (1, 1, 16, 128, 64), (1, 1, 3, 1536), (1, 1, 8, 128, 128),
         (1, 8, 4, 128, 256), (1, 8, 16, 128, 64), (1, 8, 3, 1536), (1, 8, 8, 128, 128)]


def kernel(**inputs):
    import numpy as np
    import concourse.bacc as bacc
    from concourse.bass_utils import run_bass_kernel_spmd

    nc = bacc.Bacc("TRN2", target_bir_lowering=False, num_devices=1)
    arrays, ins, outs = {}, [], []
    for name in _INS:
        a = np.ascontiguousarray(inputs[name])
        arrays[f"in_{name}"] = a
        ins.append(nc.dram_tensor(f"in_{name}", a.shape, mybir.dt.from_np(a.dtype), kind="ExternalInput").ap())
    for i, shape in enumerate(_OUTS):
        outs.append(nc.dram_tensor(f"out_{i}", shape, F32, kind="ExternalOutput").ap())
    trunk_program(nc, ins, outs)
    r = run_bass_kernel_spmd(nc, [arrays], core_ids=[0])
    return tuple(r.results[0][f"out_{i}"] for i in range(len(_OUTS)))
```
